# Optimizing a Trainium2 kernel written in Bass

```python
import math
import jax, jax.numpy as jnp
from jax import lax
import numpy as np

D_MODEL = 1024
BATCH = 1
SEQ = 256
DEPTH = 2
DEC_BATCH = 1
DEC_SEQ = 32
PAST_LEN = 128

CHUNK = 64
CONV_W = 4
EPS = 1e-6
N_AB_LAYERS = (DEPTH + 1) // 2
N_C_LAYERS = DEPTH // 2
SSD_HEADS = 16
SSD_HEAD_DIM = 64
SSD_INNER = SSD_HEADS * SSD_HEAD_DIM
SSD_GROUPS = 2
SSD_STATE = 128
SSD_CONV_DIM = SSD_INNER + 2 * SSD_GROUPS * SSD_STATE
GDN_K_HEADS = 4
GDN_V_HEADS = 8
GDN_K_DIM = 128
GDN_V_DIM = 128
GDN_CONV_DIM = 2 * GDN_K_HEADS * GDN_K_DIM + GDN_V_HEADS * GDN_V_DIM
AB_IN_DIM = SSD_INNER + SSD_CONV_DIM + SSD_HEADS + GDN_CONV_DIM + GDN_V_HEADS * GDN_V_DIM + 2 * GDN_V_HEADS
AB_MIX_DIM = SSD_INNER + GDN_V_HEADS * GDN_V_DIM
HGRN_HEADS = 8
HGRN_K_DIM = 128
HGRN_V_DIM = 128
HGRN_IN_DIM = HGRN_HEADS * (2 * HGRN_K_DIM + 2 * HGRN_V_DIM)
HGRN_BLOCK = 16
MOE_GROUPS = 4
MOE_EXPERTS_PER_GROUP = 8
MOE_EXPERTS = MOE_GROUPS * MOE_EXPERTS_PER_GROUP
MOE_TOP_K = 2
MOE_D_EXPERT = 512
MOE_ROWS = 128

kernel_name = 'hybrid_ssd_gdn_hgrn2_hmoe_stream_step'

def rms_norm(x, w):
    xf = x.astype(jnp.float32)
    y = xf * lax.rsqrt(jnp.mean(xf * xf, axis=-1, keepdims=True) + EPS)
    return (y * w.astype(jnp.float32)).astype(x.dtype)

def l2_normalize(x):
    xf = x.astype(jnp.float32)
    return (xf * lax.rsqrt(jnp.sum(xf * xf, axis=-1, keepdims=True) + EPS)).astype(x.dtype)

def split_cols(a, sizes):
    return jnp.split(a, np.cumsum(sizes)[:-1].tolist(), axis=-1)

def causal_mask(l, strict):
    i = jnp.arange(l)
    return (i[:, None] > i[None, :]) if strict else (i[:, None] >= i[None, :])

def causal_dwconv(x, prev, w, b=None):
    xp = jnp.concatenate([prev.astype(x.dtype), x], axis=1)
    y = lax.conv_general_dilated(xp, w.astype(x.dtype)[:, None, :], (1,), 'VALID',
                                 dimension_numbers=('NWC', 'WIO', 'NWC'),
                                 feature_group_count=x.shape[-1])
    if b is not None:
        y = y + b.astype(x.dtype)
    return y, xp[:, xp.shape[1] - (CONV_W - 1):]

def scan_blocks(step, state0, xs, block):
    bsz, l = xs[0].shape[:2]
    nb = l // block
    to_blocks = lambda a: jnp.swapaxes(a.reshape(bsz, nb, block, *a.shape[2:]), 0, 1)
    state, ys = lax.scan(step, state0, tuple(to_blocks(a) for a in xs))
    return jnp.swapaxes(ys, 0, 1).reshape(bsz, l, *ys.shape[3:]), state

def ssd_block(h, inp):
    x, dt, a, bm, cm = inp
    l, n_h = x.shape[1], x.shape[2]
    rep = n_h // bm.shape[2]
    bh = jnp.repeat(bm, rep, axis=2)
    ch = jnp.repeat(cm, rep, axis=2)
    cum = jnp.cumsum(a.astype(jnp.float32), axis=1)
    decay = jnp.exp(jnp.where(causal_mask(l, False)[None, :, :, None],
                              cum[:, :, None, :] - cum[:, None, :, :], -jnp.inf))
    w_ts = jnp.einsum('bthn,bshn->btsh', ch, bh) * decay * dt[:, None, :, :]
    y = jnp.einsum('btsh,bshp->bthp', w_ts, x)
    y = y + jnp.einsum('bthn,bhpn->bthp', ch, h) * jnp.exp(cum)[..., None]
    tail = jnp.exp(cum[:, -1:, :] - cum) * dt
    h_new = h * jnp.exp(cum[:, -1])[:, :, None, None] + jnp.einsum('bshn,bsh,bshp->bhpn', bh, tail, x)
    return h_new.astype(h.dtype), y

def gdn_block(s_mat, inp):
    q, k, v, beta, g = inp
    l = q.shape[1]
    gam = jnp.cumsum(g.astype(jnp.float32), axis=1)
    diff = gam[:, :, None, :] - gam[:, None, :, :]
    dec_incl = jnp.exp(jnp.where(causal_mask(l, False)[None, :, :, None], diff, -jnp.inf))
    dec_strict = jnp.where(causal_mask(l, True)[None, :, :, None], dec_incl, 0.0)
    a_mat = (beta[:, :, None, :] * dec_strict * jnp.einsum('bthk,bshk->btsh', k, k)).transpose(0, 3, 1, 2)
    eg = jnp.exp(gam)
    rhs = beta[..., None] * (v - eg[..., None] * jnp.einsum('bthk,bhkv->bthv', k, s_mat))
    u = lax.linalg.triangular_solve(a_mat.astype(jnp.float32) + jnp.eye(l, dtype=jnp.float32),
                                    rhs.transpose(0, 2, 1, 3).astype(jnp.float32),
                                    left_side=True, lower=True, unit_diagonal=True)
    qk = jnp.einsum('bthk,bshk->bhts', q, k) * dec_incl.transpose(0, 3, 1, 2)
    o = jnp.einsum('bhts,bhsv->bthv', qk, u) + eg[..., None] * jnp.einsum('bthk,bhkv->bthv', q, s_mat)
    tail = jnp.exp(gam[:, -1:, :] - gam)
    s_new = s_mat * jnp.exp(gam[:, -1])[:, :, None, None] + jnp.einsum('bshk,bsh,bhsv->bhkv', k, tail, u)
    return s_new.astype(s_mat.dtype), o

def hgrn_block(s_mat, inp):
    q, k, v, logf = inp
    l = q.shape[1]
    gam = jnp.cumsum(logf.astype(jnp.float32), axis=1)
    dec = jnp.exp(jnp.where(causal_mask(l, False)[None, :, :, None, None],
                            gam[:, :, None] - gam[:, None], -jnp.inf))
    att = jnp.einsum('bthk,btshk,bshk->bhts', q, dec, k)
    o = jnp.einsum('bhts,bshv->bthv', att, v) + jnp.einsum('bthk,bhkv->bthv', q * jnp.exp(gam), s_mat)
    s_new = s_mat * jnp.exp(gam[:, -1])[..., None] + jnp.einsum('bshk,bshv->bhkv', k * jnp.exp(gam[:, -1:] - gam), v)
    return s_new.astype(s_mat.dtype), o

def ab_mixer(u, s_ssd0, conv_ssd0, s_gdn0, conv_gdn0, w, j, block):
    bsz, l, _ = u.shape
    z_s, xbc, dt_raw, qkv, z_g, b_raw, a_raw = split_cols(
        u @ w['w_in_ab'][j],
        [SSD_INNER, SSD_CONV_DIM, SSD_HEADS, GDN_CONV_DIM, GDN_V_HEADS * GDN_V_DIM, GDN_V_HEADS, GDN_V_HEADS])
    xbc, conv_ssd = causal_dwconv(xbc, conv_ssd0, w['ssd_conv_w'][j], w['ssd_conv_b'][j])
    xs, bm, cm = split_cols(jax.nn.silu(xbc), [SSD_INNER, SSD_GROUPS * SSD_STATE, SSD_GROUPS * SSD_STATE])
    xs = xs.reshape(bsz, l, SSD_HEADS, SSD_HEAD_DIM)
    bm = bm.reshape(bsz, l, SSD_GROUPS, SSD_STATE)
    cm = cm.reshape(bsz, l, SSD_GROUPS, SSD_STATE)
    dt = jax.nn.softplus(dt_raw.astype(jnp.float32) + w['ssd_dt_bias'][j].astype(jnp.float32))
    a = -jnp.exp(w['ssd_a_log'][j].astype(jnp.float32)) * dt
    y, s_ssd = scan_blocks(ssd_block, s_ssd0, (xs, dt, a, bm, cm), block)
    y = (y + w['ssd_d'][j][:, None] * xs).reshape(bsz, l, SSD_INNER) * jax.nn.silu(z_s)
    y = rms_norm(y.reshape(bsz, l, SSD_GROUPS, SSD_INNER // SSD_GROUPS),
                 w['ssd_norm'][j].reshape(SSD_GROUPS, -1)).reshape(bsz, l, SSD_INNER)
    qkv, conv_gdn = causal_dwconv(qkv, conv_gdn0, w['gdn_conv_w'][j])
    q, k, v = split_cols(jax.nn.silu(qkv), [GDN_K_HEADS * GDN_K_DIM, GDN_K_HEADS * GDN_K_DIM, GDN_V_HEADS * GDN_V_DIM])
    rep = GDN_V_HEADS // GDN_K_HEADS
    q = jnp.repeat(l2_normalize(q.reshape(bsz, l, GDN_K_HEADS, GDN_K_DIM)), rep, axis=2) * (GDN_K_DIM ** -0.5)
    k = jnp.repeat(l2_normalize(k.reshape(bsz, l, GDN_K_HEADS, GDN_K_DIM)), rep, axis=2)
    v = v.reshape(bsz, l, GDN_V_HEADS, GDN_V_DIM)
    beta = jax.nn.sigmoid(b_raw.astype(jnp.float32))
    g = -jnp.exp(w['gdn_a_log'][j].astype(jnp.float32)) * jax.nn.softplus(
        a_raw.astype(jnp.float32) + w['gdn_dt_bias'][j].astype(jnp.float32))
    o, s_gdn = scan_blocks(gdn_block, s_gdn0, (q, k, v, beta, g), block)
    o = rms_norm(o, w['gdn_norm'][j]) * jax.nn.silu(z_g.reshape(bsz, l, GDN_V_HEADS, GDN_V_DIM))
    mix = jnp.concatenate([y, o.reshape(bsz, l, -1)], axis=-1) @ w['w_out_ab'][j]
    return mix.astype(u.dtype), s_ssd, conv_ssd, s_gdn, conv_gdn

def hgrn_mixer(u, s0, lb, w, j, block):
    bsz, l, _ = u.shape
    shp_k = (bsz, l, HGRN_HEADS, HGRN_K_DIM)
    shp_v = (bsz, l, HGRN_HEADS, HGRN_V_DIM)
    q, fz, i, gz = split_cols(u @ w['w_in_c'][j], [HGRN_HEADS * HGRN_K_DIM] * 2 + [HGRN_HEADS * HGRN_V_DIM] * 2)
    q = jax.nn.silu(q).reshape(shp_k)
    lb = lb.reshape(HGRN_HEADS, HGRN_K_DIM)
    f = lb + (1.0 - lb) * jax.nn.sigmoid(fz.astype(jnp.float32).reshape(shp_k))
    o, s_new = scan_blocks(hgrn_block, s0, (q, 1.0 - f, i.reshape(shp_v), jnp.log(f)), block)
    o = rms_norm(o, w['hgrn_norm'][j]) * jax.nn.silu(gz.reshape(shp_v))
    mix = o.reshape(bsz, l, -1) @ w['w_out_c'][j]
    return mix.astype(u.dtype), s_new

def hier_moe(x, w_group, w_router, w_gate, w_up, w_down):
    bsz, l, d = x.shape
    xt = x.reshape(bsz * l, d)
    n_tok = xt.shape[0]
    xf = xt.astype(jnp.float32)
    group_p = jax.nn.softmax(xf @ w_group.astype(jnp.float32), axis=-1)
    g_sel = jnp.argmax(group_p, axis=-1)
    g_prob = jnp.take_along_axis(group_p, g_sel[:, None], axis=-1)
    e_logits = (xf @ w_router.astype(jnp.float32)).reshape(n_tok, MOE_GROUPS, MOE_EXPERTS_PER_GROUP)
    e_logits = jnp.take_along_axis(e_logits, g_sel[:, None, None], axis=1)[:, 0]
    top_v, top_i = lax.top_k(e_logits, MOE_TOP_K)
    gates = jax.nn.softmax(top_v, axis=-1) * g_prob
    expert = g_sel[:, None] * MOE_EXPERTS_PER_GROUP + top_i
    n_as = n_tok * MOE_TOP_K
    flat_e = expert.reshape(-1)
    order = jnp.argsort(flat_e)
    e_sorted = flat_e[order]
    tok = order // MOE_TOP_K
    counts = jnp.bincount(flat_e, length=MOE_EXPERTS)
    padded = (counts + MOE_ROWS - 1) // MOE_ROWS * MOE_ROWS
    pad_end = jnp.cumsum(padded)
    dest = (pad_end - padded)[e_sorted] + jnp.arange(n_as) - (jnp.cumsum(counts) - counts)[e_sorted]
    n_blocks = (n_as + MOE_EXPERTS * (MOE_ROWS - 1) + MOE_ROWS - 1) // MOE_ROWS
    buf = jnp.zeros((n_blocks * MOE_ROWS, d), x.dtype).at[dest].set(xt[tok])
    block_e = jnp.minimum(jnp.searchsorted(pad_end, jnp.arange(n_blocks) * MOE_ROWS, side='right'), MOE_EXPERTS - 1)

    def expert_rows(args):
        xb, e = args
        hid = jax.nn.silu(xb @ w_gate[e]) * (xb @ w_up[e])
        return hid @ w_down[e]

    yb = lax.map(expert_rows, (buf.reshape(n_blocks, MOE_ROWS, d), block_e))
    y_as = yb.reshape(n_blocks * MOE_ROWS, d)[dest] * gates.reshape(-1)[order][:, None].astype(x.dtype)
    y = jnp.zeros_like(xt).at[tok].add(y_as)
    return y.reshape(bsz, l, d)

def run_trunk(x, st_ssd, st_ssd_conv, st_gdn, st_gdn_conv, st_hgrn, w, block_ab, block_c):
    sm = jax.nn.softmax(w['hgrn_lb_logits'].astype(jnp.float32), axis=0)
    lower_bounds = jnp.cumsum(sm, axis=0) - sm[0]
    h = x
    n_ssd, n_ssd_conv, n_gdn, n_gdn_conv, n_hgrn = [], [], [], [], []
    for li in range(DEPTH):
        j = li // 2
        u = rms_norm(h, w['norm_mix'][li])
        if li % 2 == 0:
            mix, s1, c1, s2, c2 = ab_mixer(u, st_ssd[:, j], st_ssd_conv[:, j], st_gdn[:, j], st_gdn_conv[:, j], w, j, block_ab)
            n_ssd.append(s1)
            n_ssd_conv.append(c1)
            n_gdn.append(s2)
            n_gdn_conv.append(c2)
        else:
            mix, s3 = hgrn_mixer(u, st_hgrn[:, j], lower_bounds[li], w, j, block_c)
            n_hgrn.append(s3)
        h = h + mix
        ffn = hier_moe(rms_norm(h, w['norm_ffn'][li]), w['moe_w_group'][li], w['moe_w_router'][li],
                       w['moe_w_gate'][li], w['moe_w_up'][li], w['moe_w_down'][li])
        h = h + ffn.astype(h.dtype)
    y = rms_norm(h, w['norm_final'])
    return (y, jnp.stack(n_ssd, 1), jnp.stack(n_ssd_conv, 1), jnp.stack(n_gdn, 1),
            jnp.stack(n_gdn_conv, 1), jnp.stack(n_hgrn, 1))

def setup_inputs(seed: int = 0) -> dict:
    key = jax.random.key(seed)
    ks = iter(jax.random.split(key, 40))

    def nrm(shape, scale):
        return jax.random.normal(next(ks), shape, jnp.float32) * scale

    def gain(shape):
        return 1.0 + nrm(shape, 0.02)

    def dt_bias(shape):
        dt = jnp.exp(jax.random.uniform(next(ks), shape, jnp.float32, math.log(1e-3), math.log(1e-1)))
        return dt + jnp.log(-jnp.expm1(-dt))

    def a_log(shape):
        return jnp.log(jax.random.uniform(next(ks), shape, jnp.float32, 1.0, 16.0))

    return {
        'x_prompt': nrm((BATCH, SEQ, D_MODEL), 1.0),
        'x_sample': nrm((DEC_BATCH, DEC_SEQ, D_MODEL), 1.0),
        'state_ssd': nrm((DEC_BATCH, N_AB_LAYERS, SSD_HEADS, SSD_HEAD_DIM, SSD_STATE), 0.3),
        'state_ssd_conv': nrm((DEC_BATCH, N_AB_LAYERS, CONV_W - 1, SSD_CONV_DIM), 1.0),
        'state_gdn': nrm((DEC_BATCH, N_AB_LAYERS, GDN_V_HEADS, GDN_K_DIM, GDN_V_DIM), 0.1),
        'state_gdn_conv': nrm((DEC_BATCH, N_AB_LAYERS, CONV_W - 1, GDN_CONV_DIM), 1.0),
        'state_hgrn': nrm((DEC_BATCH, N_C_LAYERS, HGRN_HEADS, HGRN_K_DIM, HGRN_V_DIM), 0.3),
        'norm_mix': gain((DEPTH, D_MODEL)),
        'norm_ffn': gain((DEPTH, D_MODEL)),
        'norm_final': gain((D_MODEL,)),
        'w_in_ab': nrm((N_AB_LAYERS, D_MODEL, AB_IN_DIM), D_MODEL ** -0.5),
        'ssd_conv_w': nrm((N_AB_LAYERS, CONV_W, SSD_CONV_DIM), CONV_W ** -0.5),
        'ssd_conv_b': nrm((N_AB_LAYERS, SSD_CONV_DIM), 0.02),
        'ssd_dt_bias': dt_bias((N_AB_LAYERS, SSD_HEADS)),
        'ssd_a_log': a_log((N_AB_LAYERS, SSD_HEADS)),
        'ssd_d': 1.0 + nrm((N_AB_LAYERS, SSD_HEADS), 0.1),
        'ssd_norm': gain((N_AB_LAYERS, SSD_INNER)),
        'gdn_conv_w': nrm((N_AB_LAYERS, CONV_W, GDN_CONV_DIM), CONV_W ** -0.5),
        'gdn_dt_bias': dt_bias((N_AB_LAYERS, GDN_V_HEADS)),
        'gdn_a_log': a_log((N_AB_LAYERS, GDN_V_HEADS)),
        'gdn_norm': gain((N_AB_LAYERS, GDN_V_DIM)),
        'w_out_ab': nrm((N_AB_LAYERS, AB_MIX_DIM, D_MODEL), AB_MIX_DIM ** -0.5),
        'w_in_c': nrm((N_C_LAYERS, D_MODEL, HGRN_IN_DIM), D_MODEL ** -0.5),
        'hgrn_lb_logits': nrm((DEPTH, HGRN_HEADS * HGRN_K_DIM), 0.5),
        'hgrn_norm': gain((N_C_LAYERS, HGRN_V_DIM)),
        'w_out_c': nrm((N_C_LAYERS, HGRN_HEADS * HGRN_V_DIM, D_MODEL), (HGRN_HEADS * HGRN_V_DIM) ** -0.5),
        'moe_w_group': nrm((DEPTH, D_MODEL, MOE_GROUPS), D_MODEL ** -0.5),
        'moe_w_router': nrm((DEPTH, D_MODEL, MOE_EXPERTS), D_MODEL ** -0.5),
        'moe_w_gate': nrm((DEPTH, MOE_EXPERTS, D_MODEL, MOE_D_EXPERT), D_MODEL ** -0.5),
        'moe_w_up': nrm((DEPTH, MOE_EXPERTS, D_MODEL, MOE_D_EXPERT), D_MODEL ** -0.5),
        'moe_w_down': nrm((DEPTH, MOE_EXPERTS, MOE_D_EXPERT, D_MODEL), MOE_D_EXPERT ** -0.5),
    }

def reference(x_prompt, x_sample, state_ssd, state_ssd_conv, state_gdn, state_gdn_conv, state_hgrn,
              norm_mix, norm_ffn, norm_final,
              w_in_ab, ssd_conv_w, ssd_conv_b, ssd_dt_bias, ssd_a_log, ssd_d, ssd_norm,
              gdn_conv_w, gdn_dt_bias, gdn_a_log, gdn_norm, w_out_ab,
              w_in_c, hgrn_lb_logits, hgrn_norm, w_out_c,
              moe_w_group, moe_w_router, moe_w_gate, moe_w_up, moe_w_down):
    w = dict(norm_mix=norm_mix, norm_ffn=norm_ffn, norm_final=norm_final,
             w_in_ab=w_in_ab, ssd_conv_w=ssd_conv_w, ssd_conv_b=ssd_conv_b, ssd_dt_bias=ssd_dt_bias,
             ssd_a_log=ssd_a_log, ssd_d=ssd_d, ssd_norm=ssd_norm,
             gdn_conv_w=gdn_conv_w, gdn_dt_bias=gdn_dt_bias, gdn_a_log=gdn_a_log, gdn_norm=gdn_norm,
             w_out_ab=w_out_ab, w_in_c=w_in_c, hgrn_lb_logits=hgrn_lb_logits, hgrn_norm=hgrn_norm,
             w_out_c=w_out_c, moe_w_group=moe_w_group, moe_w_router=moe_w_router,
             moe_w_gate=moe_w_gate, moe_w_up=moe_w_up, moe_w_down=moe_w_down)
    bp, dtp = x_prompt.shape[0], x_prompt.dtype
    z_ssd = jnp.zeros((bp, N_AB_LAYERS, SSD_HEADS, SSD_HEAD_DIM, SSD_STATE), dtp)
    z_ssd_conv = jnp.zeros((bp, N_AB_LAYERS, CONV_W - 1, SSD_CONV_DIM), dtp)
    z_gdn = jnp.zeros((bp, N_AB_LAYERS, GDN_V_HEADS, GDN_K_DIM, GDN_V_DIM), dtp)
    z_gdn_conv = jnp.zeros((bp, N_AB_LAYERS, CONV_W - 1, GDN_CONV_DIM), dtp)
    z_hgrn = jnp.zeros((bp, N_C_LAYERS, HGRN_HEADS, HGRN_K_DIM, HGRN_V_DIM), dtp)
    y_prompt, p_ssd, p_ssd_conv, p_gdn, p_gdn_conv, p_hgrn = run_trunk(
        x_prompt, z_ssd, z_ssd_conv, z_gdn, z_gdn_conv, z_hgrn, w, CHUNK, HGRN_BLOCK)
    ls = x_sample.shape[1]
    y_sample, s_ssd, s_ssd_conv, s_gdn, s_gdn_conv, s_hgrn = run_trunk(
        x_sample, state_ssd, state_ssd_conv, state_gdn, state_gdn_conv, state_hgrn, w, ls, ls)
    return (y_prompt, y_sample, p_ssd, p_ssd_conv, p_gdn, p_gdn_conv, p_hgrn,
            s_ssd, s_ssd_conv, s_gdn, s_gdn_conv, s_hgrn)


_drawn_inputs = setup_inputs


def setup_inputs(seed=0):
    import zlib

    import numpy as np

    out = dict(_drawn_inputs(seed))
    spreads = {}
    factors = {'norm_final': 2.839, 'gdn_norm': 3.229, 'hgrn_norm': 2.73}
    for name, (base, spread) in spreads.items():
        noise = np.random.default_rng([zlib.crc32(name.encode()), seed]).standard_normal(out[name].shape)
        drawn = base * np.exp(spread * noise) if base else spread * noise
        out[name] = __import__('jax').numpy.asarray(drawn.astype(out[name].dtype))
    for name, factor in factors.items():
        out[name] = (out[name] * factor).astype(out[name].dtype)
    return out
```

```python
import concourse.bass as bass
from concourse import mybir
from contextlib import ExitStack

D_MODEL = 1024
SEQ, DEC_SEQ = 256, 32
TOK = SEQ + DEC_SEQ
P = 128
KD = D_MODEL // P
TILES = 3
LEN = [P, P, DEC_SEQ]
AT = [0, P, 2 * P]
CONV_W = 4
TAPS = CONV_W - 1
XW = TOK + TAPS
AX = [0, P, SEQ + TAPS]
XP = XW + TAPS
EPS = 1e-6
SSD_HEADS, SSD_GROUPS, SSD_TILES = 16, 2, 8
XBC_TILES, QKV_TILES = 12, 16
CONV_TILES = XBC_TILES + QKV_TILES
GDN_HEADS, GDN_K_HEADS = 8, 4
Z_TILES = 16
HEADS = 8
SCAL = SSD_HEADS + GDN_HEADS
GROUP = 512
AB_GROUPS = (CONV_TILES + Z_TILES) * P // GROUP
C_GROUPS = 4 * D_MODEL // GROUP
EXPERTS, E_GROUPS, E_PER, D_EXP = 32, 4, 8, 512
KE = D_EXP // P
EXTRA = 2 * TOK // P
BLOCKS = EXPERTS + EXTRA
PAIRS = BLOCKS // 2
COLS = BLOCKS + 1
NOWHERE = 1.0e6
LEVELS = [1, 2, 4, 8, 16, 32, 64]

C_ID, C_ONES, C_TRIU, C_STRIU, C_MASK = 0, P, 2 * P, 3 * P, 4 * P
C_IOTA = C_MASK + len(LEVELS) * P
C_VAL = C_IOTA + P
C_SCAN = C_VAL + TILES * 2
C_EPS = C_SCAN + TOK
C_END = C_EPS + 1
V_NORM, V_CONV, V_BIAS = 0, 4 * KD, 4 * KD + CONV_TILES * CONV_W
V_D = V_BIAS + CONV_TILES
V_SNORM = V_D + SSD_TILES
V_GNORM = V_SNORM + SSD_TILES
V_HNORM = V_GNORM + 1
V_LB = V_HNORM + 1
V_END = V_LB + 2 * HEADS
R_BIAS, R_ALOG, R_END = 0, SCAL, 2 * SCAL


def build(nc, ins, outs, stop=99):
    F, I32, U32 = mybir.dt.float32, mybir.dt.int32, mybir.dt.uint32
    ACT, ALU, AX_X = mybir.ActivationFunctionType, mybir.AluOpType, mybir.AxisListType.X

    xn_dram = nc.dram_tensor("xn_rows", [TOK, D_MODEL], F, kind="Internal").ap()
    y2_dram = nc.dram_tensor("expert_rows", [2 * TOK, D_MODEL], F, kind="Internal").ap()
    wg_dram = ins["wg"].rearrange("l e (p k) f -> (l e) p (k f)", p=P)
    wu_dram = ins["wu"].rearrange("l e (p k) f -> (l e) p (k f)", p=P)
    wd_dram = ins["wd"].rearrange("l e (p k) f -> (l e) p (k f)", p=P)

    ctx = ExitStack()
    with ctx:
        def sb(name, shape, dt=F):
            return ctx.enter_context(nc.sbuf_tensor(name, shape, dt))

        def sem(name):
            return ctx.enter_context(nc.semaphore(name))

        h = sb("h", [P, TILES, D_MODEL])
        xn = sb("xn", [P, TILES, D_MODEL])
        uT = sb("uT", [P, KD, TOK])
        con = sb("con", [P, C_END])
        vec = sb("vec", [P, V_END])
        row = sb("row", [P, R_END])
        wsm = sb("wsm", [P, KD, 32])
        wrt = sb("wrt", [P, 2, KD, 36])
        ss = sb("ss", [P, 5, TILES])
        rstd = sb("rstd", [P, 5, TILES])
        ps = ctx.enter_context(nc.psum_tensor("ps", [P, 8, 512], F))
        ARENA = 37900
        arena = sb("arena", [P, ARENA])

        def at(off, *dims):
            n = 1
            for d in dims:
                n *= d
            assert off + n <= ARENA, (off, dims)
            flat = arena[:, off:off + n]
            if len(dims) == 1:
                return flat
            names = ["a", "b", "c", "d"][:len(dims)]
            return flat.rearrange("p (" + " ".join(names) + ") -> p " + " ".join(names),
                                  **dict(zip(names[1:], dims[1:])))

        def bank(b, *dims, n=1):
            flat = ps[:, b:b + n, :].rearrange("p a b -> p (a b)")
            size = 1
            for d in dims:
                size *= d
            names = ["a", "b", "c"][:len(dims)]
            if len(dims) == 1:
                return flat[:, 0:size]
            return flat[:, 0:size].rearrange("p (" + " ".join(names) + ") -> p " + " ".join(names),
                                             **dict(zip(names[1:], dims[1:])))

        ident = con[:, C_ID:C_ID + P]
        ones = con[:, C_ONES:C_ONES + P]
        triu = con[:, C_TRIU:C_TRIU + P]
        striu = con[:, C_STRIU:C_STRIU + P]
        eps = con[:, C_EPS:C_EPS + 1]
        iota = con[:, C_IOTA:C_IOTA + P]

        def mask(n):
            return con[:, C_MASK + n * P:C_MASK + (n + 1) * P]

        def take(cursor, end, *dims):
            n = 1
            for d in dims:
                n *= d
            off = cursor[0]
            cursor[0] += n
            assert cursor[0] <= end, (cursor, end)
            return at(off, *dims)

        RING = 3 * KD * GROUP
        ring = [at(s * KD * GROUP, KD, GROUP) for s in range(3)]
        cur = [RING]
        XC = take(cur, ARENA, CONV_TILES, XW)
        Z = take(cur, ARENA, Z_TILES, TOK)
        cat = take(cur, ARENA, 16, TOK)
        in_pad = cur[0]
        xpad = take(cur, ARENA, CONV_TILES, XP)
        STAGE = RING - 1024
        s_stage = at(STAGE, 8, P)
        cur = [0]
        Xdt, Xtl = take(cur, STAGE, 8, 64), take(cur, STAGE, 8, 64)
        Btok, BCm = take(cur, STAGE, P), take(cur, STAGE, P)
        HT = [take(cur, STAGE, 2, 512) for _ in range(2)]
        s_load = take(cur, STAGE, 8, P)
        cur = [in_pad]
        Dm, EG, W8, Cs = [take(cur, ARENA, 8, P) for _ in range(4)]
        DQK, DKK = take(cur, ARENA, 8, P), take(cur, ARENA, 8, P)
        tail, dec, ecum, nbe = [take(cur, ARENA, 8) for _ in range(4)]
        qs = W8
        cur = [0]
        GS = [take(cur, STAGE, 8, P) for _ in range(2)]
        T8, TT8, P8, VB, U8, Bm, Kt, RHS = [take(cur, STAGE, 8, P) for _ in range(8)]
        Ktok = take(cur, STAGE, 4, P)
        conv_st = sb("conv_st", [P, CONV_TILES, TAPS])
        conv_new = sb("conv_new", [P, 2, CONV_TILES, TAPS])
        cvt = sb("cvt", [P, 2, XW])
        sc = sb("sc", [P, TILES, 32])
        spx = sb("spx", [P, 4, TILES, SCAL])
        dtg = sb("dtg", [P, TILES, SCAL])
        G24 = sb("G24", [P, TILES, SCAL])
        cum = sb("cum", [P, TILES, SCAL])
        eA = sb("eA", [P, SCAL])
        beta = sb("beta", [P, TILES, 8])
        cur = [RING]
        hq, hk, hg, hv, hz, hcat = [take(cur, ARENA, HEADS, TOK) for _ in range(6)]
        in_hE = cur[0]
        hE, hQ, hK, hA, hVt, hKt, hEq = [take(cur, ARENA, 8, P) for _ in range(7)]
        hDec = take(cur, ARENA, 8)
        hS = [at(0, 8, P), at(1024, 8, P)]
        lbv = sb("lbv", [P, 6, HEADS])
        cur = [0]
        wgb = [take(cur, ARENA, KD, D_EXP) for _ in range(2)]
        wub = [take(cur, ARENA, KD, D_EXP) for _ in range(2)]
        wdb = [take(cur, ARENA, KE, D_MODEL) for _ in range(2)]
        in_xg = cur[0]
        xg = [take(cur, ARENA, D_MODEL) for _ in range(2)]
        xT = [take(cur, ARENA, KD, P) for _ in range(2)]
        hid, sg, hidT = take(cur, ARENA, D_EXP), take(cur, ARENA, D_EXP), take(cur, ARENA, KE, P)
        yb = [take(cur, ARENA, D_MODEL) for _ in range(2)]
        in_yl = cur[0]
        YL = [take(cur, ARENA, 2, D_MODEL) for _ in range(2)] + [at(in_xg, 2, D_MODEL)]
        OPm, OBm = at(in_yl, 6, P), at(in_yl + 6 * P, 6, COLS)
        LG = sb("LG", [P, TILES, 36])
        RT = sb("rt", [P, 1560])
        rcur = [0]

        def small(*dims):
            n = 1
            for d in dims:
                n *= d
            off = rcur[0]
            rcur[0] += n
            assert rcur[0] <= 1560
            flat = RT[:, off:off + n]
            if len(dims) == 1:
                return flat
            names = ["a", "b", "c"][:len(dims)]
            return flat.rearrange("p (" + " ".join(names) + ") -> p " + " ".join(names),
                                  **dict(zip(names[1:], dims[1:])))

        gl8, gm8 = small(3, 8), small(3, 8)
        gif, sgm, den = small(3, 1), small(3, 1), small(3, 1)
        rt_ge, ohg = small(3, 4), small(3, 4)
        selm, esel, ev8 = small(3, 32), small(3, 8), small(3, 8)
        eif, eid, rt_e2 = small(3, 2), small(3, 2), small(3, 1)
        O2, OD = small(3, 2, 32), small(3, 2, 32)
        A2, R2, over, extb = small(3, 32), small(3, 32), small(3, 32), small(3, 32)
        cnt, nx, incl, exb = small(32), small(32), small(32), small(32)
        pos, p1f, b1f = small(6), small(6), small(6)
        tb, inv, jj, c2 = small(COLS), small(COLS), small(COLS), small(COLS)
        xe = small(EXTRA)
        cmp = small(EXTRA, 32)
        gi8 = sb("gi8", [P, 3, 8], U32)
        ei8 = sb("ei8", [P, 3, 8], U32)
        posi = sb("posi", [P, 3, 6], I32)
        gates = sb("gates", [P, TILES, 2])
        gidx = sb("gidx", [P, COLS], U32)
        sidx = sb("sidx", [P, COLS], U32)
        extra_e = sb("extra_e", [1, EXTRA], I32)

        uT_flat = uT[:, :, :].rearrange("p a b -> p (a b)")
        sq4 = uT_flat[:, 0:4 * XW].rearrange("p (a b) -> p a b", a=4)
        final_w = uT_flat[:, 0:D_MODEL]
        rs0 = at(in_pad, 4, XW)
        rs1 = at(in_hE, 4, XW)
        S = {}

        def s_(name):
            if name not in S:
                S[name] = sem(name)
            return S[name]

        for name in ("x_loaded consts_loaded h_ready sq_done xn_ready xnT_ps uT_ready dve_step act_step proj_ps proj_evac "
                     "conv_out conv_act z_act small_ps small_evac sp_exp1 sp_pos sp_ln g_ready ea_ready cum_ps "
                     "cum_ready ssd_in ssd_diff ssd_exp ssd_w ssd_y ssd_upd st_T st_Tevac state_in ssd_final "
                     "yg_ready sq2_done nrm_ps nrm_done qk_sq qk_ps qk_done gdn_in gdn_diff gdn_exp gdn_mats "
                     "gdn_bm gdn_p gdn_pe gdn_t gdn_tu gdn_ks gdn_rhs gdn_u gdn_ue gdn_o gdn_upd gdn_init gdn_final "
                     "cat_ready out_ps out_loaded0 out_loaded1 out_loaded2 states_out conv_new_ready beta_ready "
                     "ring0 ring1 ring2 lf_in lf_ready lb_e lb_in hg_d hg_e hg_qk hg_att hg_acc hg_in hg_x hg_y hg_ex hg_upd hg_tr "
                     "lg_ps rt_diff rt_exp rt_A rt_R rt_OH rt_tab route_done xn_stored "
                     "xgathered0 xgathered1 xg_T xT_ready wg0 wg1 wu0 wu1 wd0 wd1 gate_ps up_ps sg_ready "
                     "hid_ready hT_ps hidT_ready y_ps yA_ready yB_ready scattered0 scattered1 "
                     "xg_zero y2_loaded0 y2_loaded1 y2_loaded2 y_out act_tmp hist_loaded final_loaded rs_done rs_done").split():
            s_(name)
        def need(eng, semaphore, value):
            if not isinstance(value, int) or value > 0:
                eng.wait_ge(semaphore, value)

        block = ctx.enter_context(nc.Block())

        @block.sync
        def _(sp):
            sp.dma_start(con[:, :], ins["con"]).then_inc(S["consts_loaded"], 16)
            sp.dma_start(vec[:, :], ins["vec"]).then_inc(S["consts_loaded"], 16)
            sp.dma_start(row[:, :], ins["row"].to_broadcast([P, R_END])).then_inc(S["consts_loaded"], 16)
            sp.dma_start(wsm[:, :, :], ins["wsm"]).then_inc(S["consts_loaded"], 16)
            sp.dma_start(wrt[:, :, :, :], ins["wrt"]).then_inc(S["consts_loaded"], 16)
            sp.dma_start(h[:, 0:2, :], ins["xp"].rearrange("(t p) d -> p t d", p=P)).then_inc(S["x_loaded"], 16)
            sp.dma_start(h[0:DEC_SEQ, 2, :], ins["xs"]).then_inc(S["x_loaded"], 16)
            sp.dma_start(conv_st[:, :, :], ins["conv_st"]).then_inc(S["hist_loaded"], 16)

            def load_ring(src, groups, first, evac_base):
                for g in range(groups):
                    if g >= 3:
                        sp.wait_ge(S["proj_ps"], evac_base + 4 * (g - 2))
                    n = first + g
                    sp.dma_start(ring[g % 3].rearrange("p a b -> p (a b)"), src[g]).then_inc(S[f"ring{g % 3}"], 16)

            load_ring(ins["wA"], AB_GROUPS, 0, 0)
            sp.wait_ge(S["proj_ps"], AB_GROUPS * 4)
            sp.dma_start(s_load, ins["st_ssd"].rearrange("(c q) n -> q c n", q=P)).then_inc(S["state_in"], 16)
            sp.wait_ge(S["conv_new_ready"], 2)
            for j in range(2):
                sp.dma_start(outs["conv"][j], conv_new[:, j]).then_inc(S["states_out"], 16)
            for n, name in enumerate(("ssd_p", "ssd_s")):
                sp.wait_ge(S["ssd_final"], n + 1)
                sp.dma_start(outs[name].rearrange("(c q) n -> q c n", q=P), s_stage).then_inc(S["states_out"], 16)
            sp.wait_ge(S["nrm_done"], 3)
            sp.dma_start(GS[1], ins["st_gdn"].rearrange("h k v -> k h v")).then_inc(S["gdn_init"], 16)
            for n, name in enumerate(("gdn_p", "gdn_s")):
                sp.wait_ge(S["gdn_upd"], 2 + n)
                sp.dma_start(outs[name].rearrange("h k v -> k h v"), GS[n]).then_inc(S["states_out"], 16)
            sp.wait_ge(S["states_out"], 16 * 6)

            def load_out(src, groups, first):
                for g in range(groups):
                    if g >= 3:
                        sp.wait_ge(S["out_ps"], first + g - 2)
                    sp.dma_start(ring[g % 3].rearrange("p a b -> p (a b)").rearrange("p (c d) -> p c d", c=4),
                                 src[g * 4 * P:(g + 1) * 4 * P, :].rearrange("(c p) d -> p c d", p=P)
                                 ).then_inc(S[f"out_loaded{g % 3}"], 16)

            sp.wait_ge(S["cat_ready"], 1)
            load_out(ins["w_out_ab"], 4, 0)

            def moe_loads(l):
                base = BLOCKS * l

                def one(q, e, waits):
                    for ring_, w, free, loaded in ((wgb, wg_dram, "gate_ps", "wg"), (wub, wu_dram, "up_ps", "wu"),
                                                   (wdb, wd_dram, "y_ps", "wd")):
                        if waits is not None:
                            sp.wait_ge(S[free], waits * 2 if free == "y_ps" else waits)
                        sp.dma_start(ring_[q].rearrange("p a b -> p (a b)"),
                                     w[bass.ds(e, 1), :, :].rearrange("a p f -> p (a f)")
                                     ).then_inc(S[f"{loaded}{q}"], 16)

                one(0, l * EXPERTS, None)
                one(1, l * EXPERTS + 1, None)
                with sp.Fori(1, EXPERTS // 2) as i:
                    for q in range(2):
                        one(q, i * 2 + (l * EXPERTS + q), i * 2 + (base + q - 1))
                sp.wait_ge(S["route_done"], l + 1)
                for x in range(EXTRA):
                    q = x % 2
                    e = sp.value_load(extra_e[0:1, x:x + 1], min_val=0, max_val=2 * EXPERTS - 1)
                    one(q, e, base + EXPERTS + x - 1)
                sp.wait_ge(S["scattered0"], 16 * PAIRS * (l + 1))
                sp.wait_ge(S["scattered1"], 16 * PAIRS * (l + 1))
                for i in range(TILES):
                    for c in range(2):
                        sp.dma_start(YL[i][0:LEN[i], c, :],
                                     y2_dram[c * TOK + AT[i]:c * TOK + AT[i] + LEN[i], :]
                                     ).then_inc(S[f"y2_loaded{i}"], 16)

            def store_rows(l):
                for i in range(TILES):
                    sp.wait_ge(S["xn_ready"], (2 * l + 1) * TILES + i + 1)
                    sp.dma_start(xn_dram[AT[i]:AT[i] + LEN[i], :], xn[0:LEN[i], i, :]).then_inc(S["xn_stored"], 16)

            sp.wait_ge(S["h_ready"], TILES)
            store_rows(0)
            if stop > 1:
                moe_loads(0)
            if stop > 2:
                sp.wait_ge(S["h_ready"], 2 * TILES)
                load_ring(ins["wC"], C_GROUPS, AB_GROUPS, AB_GROUPS * 4)
                sp.wait_ge(S["proj_ps"], (AB_GROUPS + C_GROUPS) * 4)
                sp.dma_start(hS[1], ins["st_hgrn"].rearrange("h k v -> k h v")).then_inc(S["gdn_init"], 16)
                for n, name in enumerate(("hgrn_p", "hgrn_s")):
                    sp.wait_ge(S["hg_upd"], 2 + n)
                    sp.dma_start(outs[name].rearrange("h k v -> k h v"), hS[n]).then_inc(S["states_out"], 16)
                sp.wait_ge(S["states_out"], 16 * 8)
                sp.wait_ge(S["cat_ready"], 2)
                load_out(ins["w_out_c"], 2, 4)
                sp.wait_ge(S["h_ready"], 3 * TILES)
                store_rows(1)
                moe_loads(1)
                sp.dma_start(final_w, ins["final"].to_broadcast([P, D_MODEL])).then_inc(S["final_loaded"], 16)
                for i in range(TILES):
                    sp.wait_ge(S["xn_ready"], 4 * TILES + i + 1)
                    dst = outs["y_p"][AT[i]:AT[i] + P, :] if i < 2 else outs["y_s"]
                    sp.dma_start(dst, xn[0:LEN[i], i, :]).then_inc(S["y_out"], 16)
                sp.wait_ge(S["y_out"], 16 * TILES)

        @block.gpsimd
        def _(pool):
            if stop > 1:
                for l in range(2 if stop > 2 else 1):
                    pool.wait_ge(S["h_ready"], (2 * l + 1) * TILES)
                    nc.gpsimd.memset(xg[0], 0.0).then_inc(S["xg_zero"], 1)
                    nc.gpsimd.memset(xg[1], 0.0).then_inc(S["xg_zero"], 1)
                    pool.wait_ge(S["xg_zero"], 2 * l + 2)
                    pool.wait_ge(S["xn_stored"], 16 * TILES * (l + 1))
                    pool.wait_ge(S["route_done"], l + 1)
                    done = l * (BLOCKS + 1)

                    def gather(b):
                        if b >= 2:
                            pool.wait_ge(S["xg_T"], 2 * (done + b - 1))
                        nc.gpsimd.indirect_dma_start(
                            out=xg[b % 2], out_offset=None, in_=xn_dram,
                            in_offset=bass.IndirectOffsetOnAxis(ap=gidx[:, b:b + 1], axis=0),
                            bounds_check=TOK - 1, oob_is_err=False).then_inc(S[f"xgathered{b % 2}"], 16)

                    gather(0)
                    gather(1)
                    for b in range(BLOCKS):
                        if b + 2 <= BLOCKS:
                            gather(b + 2)
                        pool.wait_ge(S["yA_ready"], l * BLOCKS + b + 1)
                        pool.wait_ge(S["yB_ready"], l * BLOCKS + b + 1)
                        nc.gpsimd.indirect_dma_start(
                            out=y2_dram, out_offset=bass.IndirectOffsetOnAxis(ap=sidx[:, b:b + 1], axis=0),
                            in_=yb[b % 2], in_offset=None,
                            bounds_check=2 * TOK - 1, oob_is_err=False).then_inc(S[f"scattered{b % 2}"], 16)

        @block.scalar
        def _(act):
            na = [0]

            def a(ins_):
                na[0] += 1
                ins_.then_inc(S["act_step"], 1)
                act.wait_ge(S["act_step"], na[0])

            def squares(n):
                for i in range(TILES):
                    if n == 0:
                        act.wait_ge(S["x_loaded"], 32)
                    else:
                        act.wait_ge(S["h_ready"], (n - 1) * TILES + i + 1)
                    L = LEN[i]
                    a(nc.scalar.activation(xn[0:L, i, :], h[0:L, i, :], ACT.Square,
                                           accum_out=ss[0:L, n, i:i + 1]))
                    nc.scalar.activation(rstd[0:L, n, i:i + 1], ss[0:L, n, i:i + 1], ACT.Sqrt, scale=1.0 / D_MODEL,
                                         bias=eps[0:L]).then_inc(S["sq_done"], 1)

            act.wait_ge(S["consts_loaded"], 80)
            squares(0)
            for t in range(CONV_TILES + Z_TILES):
                b = t % 4
                act.wait_ge(S["proj_ps"], t + 1)
                if t < CONV_TILES:
                    nc.scalar.activation(xpad[:, t, TAPS:TAPS + SEQ], ps[:, b, 0:SEQ], ACT.Copy)
                    nc.scalar.activation(xpad[:, t, SEQ + 2 * TAPS:XP], ps[:, b, SEQ:TOK], ACT.Copy
                                         ).then_inc(S["proj_evac"], 1)
                else:
                    nc.scalar.activation(Z[:, t - CONV_TILES, :], ps[:, b, 0:TOK], ACT.Silu
                                         ).then_inc(S["proj_evac"], 1)
                u = t - 2
                if 0 <= u < CONV_TILES:
                    act.wait_ge(S["conv_out"], u + 1)
                    nc.scalar.activation(XC[:, u, :], cvt[:, u % 2, :], ACT.Silu,
                                         bias=vec[:, V_BIAS + u:V_BIAS + u + 1]).then_inc(S["conv_act"], 1)
            act.wait_ge(S["small_evac"], 1)
            nc.scalar.activation(beta[:, :, :], sc[:, :, SCAL:SCAL + 8], ACT.Sigmoid).then_inc(S["beta_ready"], 1)
            nc.scalar.activation(spx[:, 1], spx[:, 0], ACT.Exp, scale=-1.0).then_inc(S["sp_exp1"], 1)
            nc.scalar.activation(eA[:, :], row[:, R_ALOG:R_ALOG + SCAL], ACT.Exp).then_inc(S["ea_ready"], 1)
            act.wait_ge(S["sp_pos"], 1)
            nc.scalar.activation(spx[:, 3], spx[:, 2], ACT.Ln).then_inc(S["sp_ln"], 1)
            for u in range(2 * TILES):
                i = u // 2
                L = LEN[i]
                GB = bank(0, 8, P, n=2)
                act.wait_ge(S["ssd_in"], u + 1)
                if u:
                    act.wait_ge(S["ssd_upd"], u)
                nc.scalar.activation(EG[:, :, 0:L], GB[:, :, 0:L], ACT.Exp)
                nc.scalar.activation(dec, GB[:, :, L - 1], ACT.Exp).then_inc(S["ssd_exp"], 1)
                act.wait_ge(S["ssd_diff"], 2 * u + 1)
                nc.scalar.activation(Dm[0:L, :, 0:L], Dm[0:L, :, 0:L], ACT.Exp).then_inc(S["ssd_exp"], 1)
                act.wait_ge(S["ssd_diff"], 2 * u + 2)
                nc.scalar.activation(tail[0:L], tail[0:L], ACT.Exp).then_inc(S["ssd_exp"], 1)
            act.wait_ge(S["yg_ready"], 1)
            nc.scalar.activation(uT[:, :, :], cat[:, 0:8, :], ACT.Square).then_inc(S["sq2_done"], 1)
            act.wait_ge(S["nrm_ps"], 1)
            nc.scalar.activation(rs0[:, 0:2, 0:TOK], ps[:, 0:2, 0:TOK], ACT.Sqrt, scale=1.0 / 512,
                                 bias=eps).then_inc(S["rs_done"], 1)
            for r in range(2):
                act.wait_ge(S["nrm_done"], r + 1)
                nc.scalar.activation(sq4, XC[:, 12 + 4 * r:16 + 4 * r, :], ACT.Square
                                     ).then_inc(S["sq2_done"], 1)
                act.wait_ge(S["nrm_ps"], 2 + r)
                nc.scalar.activation(rs0, ps[:, 0:4, 0:XW], ACT.Sqrt, bias=eps).then_inc(S["rs_done"], 1)
            for i in range(TILES):
                L = LEN[i]
                GB = bank(0, 8, P, n=2)
                act.wait_ge(S["gdn_in"], i + 1)
                if i:
                    act.wait_ge(S["gdn_upd"], i)
                nc.scalar.activation(EG[:, :, 0:L], GB[:, :, 0:L], ACT.Exp)
                nc.scalar.activation(dec, GB[:, :, L - 1], ACT.Exp)
                nc.scalar.activation(ecum[0:L], cum[0:L, i, SSD_HEADS:SCAL], ACT.Exp).then_inc(S["gdn_exp"], 1)
                act.wait_ge(S["gdn_diff"], 2 * i + 1)
                nc.scalar.activation(Dm[0:L, :, 0:L], Dm[0:L, :, 0:L], ACT.Exp).then_inc(S["gdn_exp"], 1)
                act.wait_ge(S["gdn_diff"], 2 * i + 2)
                nc.scalar.activation(tail[0:L], tail[0:L], ACT.Exp).then_inc(S["gdn_exp"], 1)

            def head_roots(src, rs, ready, sq, nrm):
                act.wait_ge(S["yg_ready"], ready)
                nc.scalar.activation(uT[:, :, :], src, ACT.Square).then_inc(S["sq2_done"], 1)
                for r in range(2):
                    act.wait_ge(S["nrm_ps"], nrm + r)
                    if r:
                        act.wait_ge(S["nrm_done"], nrm)
                    nc.scalar.activation(rs[:, :, 0:TOK], ps[:, 4 * r:4 * r + 4, 0:TOK], ACT.Sqrt, scale=1.0 / P,
                                         bias=eps).then_inc(S["rs_done"], 1)

            head_roots(cat[:, 8:16, :], rs0, 2, 4, 4)

            def moe_act(l):
                squares(2 * l + 1)
                act.wait_ge(S["rt_diff"], 2 * l + 1)
                nc.scalar.activation(rt_ge, rt_ge, ACT.Exp).then_inc(S["rt_exp"], 1)
                act.wait_ge(S["rt_diff"], 2 * l + 2)
                nc.scalar.activation(rt_e2, rt_e2, ACT.Exp).then_inc(S["rt_exp"], 1)
                if stop <= 1:
                    return
                def blocks(i):
                    for q in range(2):
                        b = i * 2 + (l * BLOCKS + q)
                        act.wait_ge(S["gate_ps"], b + 1)
                        need(act, S["hid_ready"], b)
                        nc.scalar.activation(sg, bank(2, 512), ACT.Silu).then_inc(S["sg_ready"], 1)
                        act.wait_ge(S["hT_ps"], b + 1)
                        need(act, S["y_ps"], b * 2)
                        nc.scalar.activation(hidT, bank(4, KE, P), ACT.Copy).then_inc(S["hidT_ready"], 1)
                        act.wait_ge(S["y_ps"], b * 2 + 1)
                        need(act, S[f"scattered{q}"], i * 16 + 16 * l * PAIRS)
                        nc.scalar.activation(yb[q][:, 0:512], bank(5, 512), ACT.Copy).then_inc(S["yA_ready"], 1)

                blocks(0)
                with act.Fori(1, PAIRS) as i:
                    blocks(i)

            moe_act(0)
            if stop <= 2:
                return
            squares(2)
            base = CONV_TILES + Z_TILES
            for t in range(4 * HEADS):
                act.wait_ge(S["proj_ps"], base + t + 1)
                part, hd = t // HEADS, t % HEADS
                dst = (hq, hg, hv, hz)[part]
                fn = (ACT.Silu, ACT.Sigmoid, ACT.Copy, ACT.Silu)[part]
                nc.scalar.activation(dst[:, hd, :], ps[:, t % 4, 0:TOK], fn).then_inc(S["proj_evac"], 1)
            act.wait_ge(S["lb_in"], 1)
            nc.scalar.activation(lbv[:, 1:3, :], lbv[:, 1:3, :], ACT.Exp).then_inc(S["lb_e"], 1)
            act.wait_ge(S["lf_in"], 1)
            nc.scalar.activation(hg, hg, ACT.Ln).then_inc(S["lf_ready"], 1)
            n = 0
            for i in range(TILES):
                L = LEN[i]
                c0 = AT[i]
                for lv, b in enumerate(LEVELS):
                    if b >= L:
                        continue
                    n += 1
                    act.wait_ge(S["hg_d"], n)
                    nc.scalar.activation(hE[:, :, 0:L], hE[:, :, 0:L], ACT.Exp, scale=-1.0).then_inc(S["hg_e"], 1)
                act.wait_ge(S["hg_x"], i + 1)
                nc.scalar.activation(hE[:, :, 0:L], hg[:, :, c0:c0 + L], ACT.Exp)
                nc.scalar.activation(hEq[:, :, 0:L], hEq[:, :, 0:L], ACT.Exp)
                nc.scalar.activation(hDec, hg[:, :, c0 + L - 1], ACT.Exp).then_inc(S["hg_ex"], 1)
            head_roots(hcat, rs1, 3, 5, 6)
            moe_act(1)
            squares(4)

        @block.vector
        def _(dve):
            nv = [0]

            def v(ins_):
                nv[0] += 1
                ins_.then_inc(S["dve_step"], 1)
                dve.wait_ge(S["dve_step"], nv[0])

            V = nc.vector

            def tt(out, a, b, op):
                return V.tensor_tensor(out, a, b, op)

            def bc(ap, *dims):
                return ap.to_broadcast([ap.shape[0], *dims])

            def norm(n):
                for i in range(TILES):
                    L = LEN[i]
                    r = rstd[0:L, n, i:i + 1]
                    dve.wait_ge(S["sq_done"], n * TILES + i + 1)
                    v(V.reciprocal(r, r))
                    if n < 4:
                        V.tensor_scalar(xn[0:L, i, :], h[0:L, i, :], r, None, ALU.mult).then_inc(S["xn_ready"], 1)
                    else:
                        v(V.tensor_scalar(xn[0:L, i, :], h[0:L, i, :], r, None, ALU.mult))
                        dve.wait_ge(S["final_loaded"], 16)
                        tt(xn[0:L, i, :], xn[0:L, i, :], final_w[0:L], ALU.mult).then_inc(S["xn_ready"], 1)
                if n == 4:
                    return
                for i in range(TILES):
                    for c in range(2):
                        k = 2 * i + c
                        w = vec[:, V_NORM + KD * n + 4 * c:V_NORM + KD * n + 4 * c + 4]
                        dve.wait_ge(S["xnT_ps"], 6 * n + k + 1)
                        tt(uT[:, 4 * c:4 * c + 4, AT[i]:AT[i] + LEN[i]], bank(4 + k % 4, 4, P)[:, :, 0:LEN[i]],
                           bc(w.unsqueeze(2), 4, LEN[i]), ALU.mult).then_inc(S["uT_ready"], 1)

            v(V.memset(xpad[:, :, 0:TAPS], 0.0))
            v(V.memset(sc[:, :, :], 0.0))
            v(V.memset(cum[:, :, :], 0.0))
            v(V.memset(LG[:, :, :], 0.0))
            v(V.memset(R2, 0.0))
            dve.wait_ge(S["hist_loaded"], 16)
            v(V.tensor_copy(xpad[:, :, TAPS + SEQ:2 * TAPS + SEQ], conv_st[:, :, :]))
            dve.wait_ge(S["consts_loaded"], 80)
            norm(0)
            for t in range(CONV_TILES):
                wv = lambda j: vec[:, V_CONV + t * CONV_W + j:V_CONV + t * CONV_W + j + 1]
                out = cvt[:, t % 2, :]
                dve.wait_ge(S["proj_evac"], t + 1)
                if t >= 2:
                    dve.wait_ge(S["conv_act"], t - 1)
                v(V.tensor_scalar(out, xpad[:, t, 0:XW], wv(0), None, ALU.mult))
                for j in range(1, CONV_W):
                    op = V.scalar_tensor_tensor(out, xpad[:, t, j:j + XW], wv(j), out, ALU.mult, ALU.add)
                    if j < CONV_W - 1:
                        v(op)
                    else:
                        op.then_inc(S["conv_out"], 1)
            V.tensor_copy(conv_new[:, 0, :, :], xpad[:, :, SEQ:SEQ + TAPS]).then_inc(S["conv_new_ready"], 1)
            V.tensor_copy(conv_new[:, 1, :, :], xpad[:, :, XP - TAPS:XP]).then_inc(S["conv_new_ready"], 1)
            for i in range(TILES):
                dve.wait_ge(S["small_ps"], i + 1)
                v(V.tensor_copy(sc[0:LEN[i], i, :], ps[0:LEN[i], 4 + i, 0:32]))
            s24 = sc[:, :, 0:SCAL]
            v(tt(s24, s24, bc(row[:, R_BIAS:R_BIAS + SCAL].unsqueeze(1), TILES, SCAL), ALU.add))
            V.scalar_tensor_tensor(spx[:, 0], s24, -1.0, s24, ALU.mult, ALU.max).then_inc(S["small_evac"], 1)
            dve.wait_ge(S["sp_exp1"], 1)
            e_, w_, d_ = spx[:, 1], spx[:, 2], spx[:, 0]
            V.tensor_scalar(w_, e_, 1.0, None, ALU.add).then_inc(S["sp_pos"], 1)
            dve.wait_ge(S["sp_pos"], 1)
            v(V.tensor_scalar(d_, w_, -1.0, None, ALU.add))
            dve.wait_ge(S["sp_ln"], 1)
            v(tt(spx[:, 3], spx[:, 3], e_, ALU.mult))
            v(V.tensor_scalar(w_, d_, 0.0, None, ALU.is_equal))
            v(tt(e_, e_, w_, ALU.mult))
            v(V.tensor_scalar(d_, d_, 1.0e-30, None, ALU.max))
            v(V.reciprocal(d_, d_))
            v(tt(spx[:, 3], spx[:, 3], d_, ALU.mult))
            v(tt(spx[:, 3], spx[:, 3], e_, ALU.add))
            v(V.scalar_tensor_tensor(dtg[:, :, :], s24, 0.0, spx[:, 3], ALU.max, ALU.add))
            dve.wait_ge(S["ea_ready"], 1)
            V.scalar_tensor_tensor(G24[:, :, :], dtg[:, :, :], -1.0, bc(eA[:, :].unsqueeze(1), TILES, SCAL),
                                   ALU.mult, ALU.mult).then_inc(S["g_ready"], 1)
            dve.wait_ge(S["cum_ps"], 1)
            for i in range(TILES):
                v(V.tensor_copy(cum[0:LEN[i], i, :], ps[0:LEN[i], 3, i * 32:i * 32 + SCAL]))

            dve.wait_ge(S["state_in"], 16)
            for u in range(2 * TILES):
                i, g = u // 2, u % 2
                L, x0, c0 = LEN[i], AX[i], AT[i]
                st = HT[1 if i == 2 else 0]
                GB = bank(0, 8, P, n=2)
                cm = cum[0:L, i, 8 * g:8 * g + 8]
                if u == 4:
                    for c in range(2):
                        dve.wait_ge(S["st_T"], c + 1)
                        v(V.tensor_copy(HT[1][:, c, :], bank(6 + c, 512)))
                    V.engine_nop().then_inc(S["st_Tevac"], 1)
                dve.wait_ge(S["ssd_in"], u + 1)
                v(tt(Xdt[0:L], bank(5, 8, 64)[0:L], bc(dtg[0:L, i, 8 * g:8 * g + 8].unsqueeze(2), 8, 64), ALU.mult))
                v(V.tensor_copy(Btok[0:L], ps[0:L, 6, 0:P]))
                v(tt(BCm[0:L, 0:L], ps[0:L, 2, 0:L], triu[0:L, 0:L], ALU.mult))
                dve.wait_ge(S["ssd_exp"], 3 * u + 1)
                v(tt(Dm[0:L, :, 0:L], GB[0:L, :, 0:L], bc(cm.unsqueeze(2), 8, L), ALU.subtract))
                V.tensor_scalar(Dm[0:L, :, 0:L], Dm[0:L, :, 0:L], 0.0, None, ALU.min).then_inc(S["ssd_diff"], 1)
                tt(tail[0:L], GB[0:L, :, L - 1], cm, ALU.subtract).then_inc(S["ssd_diff"], 1)
                v(tt(Cs[:, :, 0:L], EG[:, :, 0:L], bc(XC[:, 10 + g, x0:x0 + L].unsqueeze(1), 8, L), ALU.mult))
                dve.wait_ge(S["ssd_exp"], 3 * u + 3)
                v(tt(W8[0:L, :, 0:L], Dm[0:L, :, 0:L], bc(BCm[0:L, 0:L].unsqueeze(1), 8, L), ALU.mult))
                tt(Xtl[0:L], Xdt[0:L], bc(tail[0:L].unsqueeze(2), 8, 64), ALU.mult).then_inc(S["ssd_w"], 1)
                dve.wait_ge(S["ssd_y"], u + 1)
                for c in range(4):
                    k = 4 * g + c
                    v(V.scalar_tensor_tensor(cat[:, k, c0:c0 + L], XC[:, k, x0:x0 + L], vec[:, V_D + k:V_D + k + 1],
                                             bank(3, 4, P)[:, c, 0:L], ALU.mult, ALU.add))
                if i == 0:
                    V.tensor_copy(st[:, g, :], bank(4, 512)).then_inc(S["ssd_upd"], 1)
                else:
                    s8 = st[:, g, :].rearrange("p (a b) -> p a b", a=8)
                    v(tt(s8, s8, bc(dec.unsqueeze(2), 8, 64), ALU.mult))
                    tt(st[:, g, :], st[:, g, :], bank(4, 512), ALU.add).then_inc(S["ssd_upd"], 1)
            for n in range(2):
                if n:
                    dve.wait_ge(S["states_out"], 48)
                for c in range(2):
                    dve.wait_ge(S["st_T"], 2 + 2 * n + c + 1)
                    k = V.tensor_copy(s_stage[:, 4 * c:4 * c + 4, :], bank(6 + c, 4, P))
                    if c == 0:
                        v(k)
                    else:
                        k.then_inc(S["ssd_final"], 1)
            tt(cat[:, 0:8, :], cat[:, 0:8, :], Z[:, 0:8, :], ALU.mult).then_inc(S["yg_ready"], 1)
            dve.wait_ge(S["rs_done"], 1)
            v(V.reciprocal(rs0[:, 0:2, 0:TOK], rs0[:, 0:2, 0:TOK]))
            c4 = cat[:, 0:8, :].rearrange("p (g c) t -> p g c t", g=2)
            v(tt(c4, c4, bc(rs0[:, 0:2, 0:TOK].unsqueeze(2), 2, 4, TOK), ALU.mult))
            tt(cat[:, 0:8, :], cat[:, 0:8, :], bc(vec[:, V_SNORM:V_SNORM + 8].unsqueeze(2), 8, TOK), ALU.mult
               ).then_inc(S["nrm_done"], 1)
            for r in range(2):
                dve.wait_ge(S["rs_done"], 2 + r)
                v(V.reciprocal(rs0, rs0))
                x4 = XC[:, 12 + 4 * r:16 + 4 * r, :]
                if r == 0:
                    v(V.tensor_scalar(rs0, rs0, float(P) ** -0.5, None, ALU.mult))
                tt(x4, x4, rs0, ALU.mult).then_inc(S["nrm_done"], 1)

            for i in range(TILES):
                L, x0, c0 = LEN[i], AX[i], AT[i]
                st = GS[1 if i == 2 else 0]
                GB = bank(0, 8, P, n=2)
                cm = cum[0:L, i, SSD_HEADS:SCAL]
                bt = bc(beta[0:L, i, :].unsqueeze(2), 8, P)
                btL = bc(beta[0:L, i, :].unsqueeze(2), 8, L)
                dve.wait_ge(S["gdn_in"], i + 1)
                dve.wait_ge(S["gdn_exp"], 3 * i + 1)
                v(tt(Dm[0:L, :, 0:L], GB[0:L, :, 0:L], bc(cm.unsqueeze(2), 8, L), ALU.subtract))
                V.tensor_scalar(Dm[0:L, :, 0:L], Dm[0:L, :, 0:L], 0.0, None, ALU.min).then_inc(S["gdn_diff"], 1)
                tt(tail[0:L], GB[0:L, :, L - 1], cm, ALU.subtract).then_inc(S["gdn_diff"], 1)
                if i == 0:
                    dve.wait_ge(S["beta_ready"], 1)
                v(tt(VB[0:L], bank(4, 8, P, n=2)[0:L], bt, ALU.mult))
                v(V.tensor_copy(Ktok[0:L], bank(6, 4, P)[0:L]))
                v(V.tensor_copy(T8[0:L, :, 0:L], bc(ident[0:L, 0:L].unsqueeze(1), 8, L)))
                v(V.tensor_copy(TT8[0:L, :, 0:L], bc(ident[0:L, 0:L].unsqueeze(1), 8, L)))
                dve.wait_ge(S["gdn_exp"], 3 * i + 1)
                v(V.scalar_tensor_tensor(nbe[0:L], beta[0:L, i, :], -1.0, ecum[0:L], ALU.mult, ALU.mult))
                q4 = XC[:, 12:16, x0:x0 + L]
                for hd in range(4):
                    v(tt(qs[:, 2 * hd:2 * hd + 2, 0:L], EG[:, 2 * hd:2 * hd + 2, 0:L],
                         bc(q4[:, hd, :].unsqueeze(1), 2, L), ALU.mult))
                dve.wait_ge(S["gdn_exp"], 3 * i + 3)
                v(tt(Dm[0:L, :, 0:L], Dm[0:L, :, 0:L], bc(triu[0:L, 0:L].unsqueeze(1), 8, L), ALU.mult))
                pair = lambda ap: ap.rearrange("p (a b) c -> p a b c", b=2)
                v(tt(pair(DQK[0:L])[:, :, :, 0:L], pair(Dm[0:L])[:, :, :, 0:L],
                     bc(bank(3, 4, P)[0:L, :, 0:L].unsqueeze(2), 4, 2, L), ALU.mult))
                v(tt(pair(DKK[0:L])[:, :, :, 0:L], pair(Dm[0:L])[:, :, :, 0:L],
                     bc(bank(2, 4, P)[0:L, :, 0:L].unsqueeze(2), 4, 2, L), ALU.mult))
                v(tt(pair(Kt[0:L]), bc(Ktok[0:L].unsqueeze(2), 4, 2, P),
                     bc(tail[0:L].rearrange("p (a b) -> p a b", b=2).unsqueeze(3), 4, 2, P), ALU.mult))
                lv = [n for n, b in enumerate(LEVELS) if b < L]
                for n, b in enumerate(lv):
                    k = gdn_level(i, n)
                    tt(Bm[0:L, :, 0:L], DKK[0:L, :, 0:L], bc(mask(b)[0:L, 0:L].unsqueeze(1), 8, L), ALU.mult
                       ).then_inc(S["gdn_bm"], 1)
                    dve.wait_ge(S["gdn_pe"], 2 * k + 1)
                    tt(P8[0:L, :, 0:L], bank(4, 8, P, n=2)[0:L, :, 0:L], btL, ALU.mult).then_inc(S["gdn_p"], 1)
                    dve.wait_ge(S["gdn_pe"], 2 * k + 2)
                    if n < len(lv) - 1:
                        v(tt(T8[0:L, :, 0:L], T8[0:L, :, 0:L], bank(6, 8, P, n=2)[0:L, :, 0:L], ALU.subtract))
                    tt(TT8[0:L, :, 0:L], TT8[0:L, :, 0:L], bank(0, 8, P, n=2)[0:L, :, 0:L], ALU.subtract
                       ).then_inc(S["gdn_tu"], 1)
                if i > 0:
                    dve.wait_ge(S["gdn_ks"], i)
                    v(tt(RHS[0:L], bank(4, 8, P, n=2)[0:L], bc(nbe[0:L].unsqueeze(2), 8, P), ALU.mult))
                    tt(RHS[0:L], RHS[0:L], VB[0:L], ALU.add).then_inc(S["gdn_rhs"], 1)
                else:
                    V.tensor_copy(RHS[0:L], VB[0:L]).then_inc(S["gdn_rhs"], 1)
                dve.wait_ge(S["gdn_u"], i + 1)
                V.tensor_copy(U8[0:L], bank(6, 8, P, n=2)[0:L]).then_inc(S["gdn_ue"], 1)
                dve.wait_ge(S["gdn_o"], i + 1)
                v(V.tensor_copy(cat[:, 8:16, c0:c0 + L], bank(2, 8, P, n=2)[:, :, 0:L]))
                if i == 0:
                    V.tensor_copy(st, bank(4, 8, P, n=2)).then_inc(S["gdn_upd"], 1)
                else:
                    v(tt(st, st, bc(dec.unsqueeze(2), 8, P), ALU.mult))
                    tt(st, st, bank(4, 8, P, n=2), ALU.add).then_inc(S["gdn_upd"], 1)

            def head_norm(x, z, rs, w, ready, nrm):
                V.engine_nop().then_inc(S["yg_ready"], 1)
                for r in range(2):
                    dve.wait_ge(S["rs_done"], nrm + r)
                    v(V.reciprocal(rs[:, :, 0:TOK], rs[:, :, 0:TOK]))
                    tt(x[:, 4 * r:4 * r + 4, :], x[:, 4 * r:4 * r + 4, :], rs[:, :, 0:TOK], ALU.mult
                       ).then_inc(S["nrm_done"], 1)
                dve.wait_ge(S["nrm_done"], nrm + 1)
                V.scalar_tensor_tensor(flat(x), flat(x), w, flat(z), ALU.mult, ALU.mult).then_inc(S["cat_ready"], 1)

            def flat(ap):
                return ap.rearrange("p a b -> p (a b)")

            head_norm(cat[:, 8:16, :], Z[:, 8:16, :], rs0, vec[:, V_GNORM:V_GNORM + 1], 2, 4)

            def residual(groups, n):
                dve.wait_ge(S["out_ps"], groups)
                for i in range(TILES):
                    tt(h[0:LEN[i], i, :], h[0:LEN[i], i, :], bank(2 * i, D_MODEL, n=2)[0:LEN[i]], ALU.add
                       ).then_inc(S["h_ready"], 1)

            residual(4, 0)

            def route(l):
                B = lambda ap, *d: bc(ap, *d)
                dve.wait_ge(S["lg_ps"], l + 1)
                for i in range(TILES):
                    v(V.tensor_copy(LG[0:LEN[i], i, :], ps[0:LEN[i], 0, i * 64:i * 64 + 36]))
                v(V.memset(gl8, -3.0e38))
                v(V.tensor_copy(gl8[:, :, 0:4], LG[:, :, 0:4]))
                for i in range(TILES):
                    v(V.max(gm8[:, i, :], gl8[:, i, :]))
                    v(V.max_index(gi8[:, i, :], gm8[:, i, :], gl8[:, i, :]))
                v(V.tensor_copy(gif, gi8[:, :, 0:1]))
                tt(rt_ge, LG[:, :, 0:4], B(gm8[:, :, 0:1], 3, 4), ALU.subtract).then_inc(S["rt_diff"], 1)
                v(tt(ohg, B(iota[:, 0:4].unsqueeze(1), 3, 4), B(gif, 3, 4), ALU.is_equal))
                s4 = selm.rearrange("p i (g j) -> p i g j", g=4)
                v(tt(s4, LG[:, :, 4:36].rearrange("p i (g j) -> p i g j", g=4), B(ohg.unsqueeze(3), 3, 4, 8), ALU.mult))
                v(V.tensor_reduce(esel, selm.rearrange("p i (g j) -> p i j g", g=4), AX_X, ALU.add))
                for i in range(TILES):
                    v(V.max(ev8[:, i, :], esel[:, i, :]))
                    v(V.max_index(ei8[:, i, :], ev8[:, i, :], esel[:, i, :]))
                v(V.tensor_copy(eif, ei8[:, :, 0:2]))
                tt(rt_e2, ev8[:, :, 1:2], ev8[:, :, 0:1], ALU.subtract).then_inc(S["rt_diff"], 1)
                v(V.tensor_scalar(sgm, gif, float(E_PER), None, ALU.mult))
                v(tt(eid, eif, B(sgm, 3, 2), ALU.add))
                v(tt(O2, B(iota[:, 0:32].unsqueeze(1).unsqueeze(1), 3, 2, 32), B(eid.unsqueeze(3), 3, 2, 32), ALU.is_equal))
                tt(A2, O2[:, :, 0, :], O2[:, :, 1, :], ALU.add).then_inc(S["rt_A"], 1)
                dve.wait_ge(S["rt_exp"], 2 * l + 2)
                v(V.tensor_reduce(sgm, rt_ge, AX_X, ALU.add))
                v(V.tensor_scalar(den, rt_e2, 1.0, None, ALU.add))
                v(tt(den, den, sgm, ALU.mult))
                v(V.reciprocal(gates[:, :, 0:1], den))
                v(tt(gates[:, :, 1:2], gates[:, :, 0:1], rt_e2, ALU.mult))
                dve.wait_ge(S["rt_R"], l + 1)
                for i in range(TILES):
                    v(V.tensor_copy(R2[0:LEN[i], i, :], ps[0:LEN[i], 1, i * 32:i * 32 + 32]))
                v(V.tensor_copy(cnt, ps[:, 1, 96:128]))
                v(V.tensor_scalar(exb, cnt, float(P), None, ALU.is_gt))
                v(V.scalar_tensor_tensor(nx, cnt, float(2 * P), exb, ALU.is_gt, ALU.add))
                v(V.tensor_tensor_scan(incl, ones[:, 0:32], nx, 0.0, ALU.mult, ALU.add))
                v(tt(exb, incl, nx, ALU.subtract))
                v(V.tensor_scalar(over, R2, float(P) - 0.5, None, ALU.is_gt))
                v(V.tensor_scalar(exb, exb, float(P), float(P * (EXPERTS - 1)), ALU.mult, ALU.add))
                v(V.tensor_scalar(cnt, iota[:, 0:32], float(P), None, ALU.mult))
                v(tt(exb, exb, cnt, ALU.subtract))
                v(tt(extb, over, B(exb.unsqueeze(1), 3, 32), ALU.mult))
                v(tt(R2, R2, extb, ALU.add))
                v(tt(R2, R2, B(cnt.unsqueeze(1), 3, 32), ALU.add))
                v(tt(OD, O2, B(R2.unsqueeze(2), 3, 2, 32), ALU.mult))
                v(V.tensor_reduce(pos.rearrange("p (a b) -> p a b", a=3), OD, AX_X, ALU.add))
                v(V.tensor_copy(posi[:, 0, :], pos))
                v(V.tensor_scalar(posi[:, 1, :], posi[:, 0, :], P - 1, None, ALU.bitwise_and))
                v(V.tensor_scalar(posi[:, 2, :], posi[:, 0, :], 7, None, ALU.logical_shift_right))
                v(V.tensor_copy(p1f, posi[:, 1, :]))
                v(V.tensor_copy(b1f, posi[:, 2, :]))
                for k in range(6):
                    v(V.tensor_scalar(OPm[:, k, :], iota, p1f[:, k:k + 1], None, ALU.is_equal))
                    ob = V.tensor_scalar(OBm[:, k, :], iota[:, 0:COLS], b1f[:, k:k + 1],
                                         con[:, C_VAL + k:C_VAL + k + 1], ALU.is_equal, ALU.mult)
                    if k < 5:
                        v(ob)
                    else:
                        ob.then_inc(S["rt_OH"], 1)
                v(tt(cmp[0:1], B(incl[0:1].unsqueeze(1), EXTRA, 32), B(iota[0:1, 0:EXTRA].unsqueeze(2), EXTRA, 32), ALU.is_le))
                v(V.tensor_reduce(xe[0:1], cmp[0:1], AX_X, ALU.add))
                v(V.tensor_scalar(xe[0:1], xe[0:1], float(EXPERTS - 1), float(l * EXPERTS), ALU.min, ALU.add))
                v(V.tensor_copy(extra_e[0:1, :], xe[0:1]))
                dve.wait_ge(S["rt_tab"], l + 1)
                v(V.tensor_copy(tb, ps[:, 2, 0:COLS]))
                v(V.tensor_scalar(inv, tb, 0.5, NOWHERE, ALU.is_lt, ALU.mult))
                v(V.tensor_scalar(jj, tb, -1.0, None, ALU.add))
                v(V.tensor_scalar(c2, jj, float(TOK) - 0.5, float(TOK), ALU.is_gt, ALU.mult))
                v(tt(jj, jj, inv, ALU.add))
                v(V.tensor_copy(sidx[:, :], jj))
                v(tt(jj, jj, c2, ALU.subtract))
                V.tensor_copy(gidx[:, :], jj).then_inc(S["route_done"], 1)

            def moe_dve(l):
                if l:
                    v(V.memset(R2, 0.0))
                route(l)
                if stop <= 1:
                    return
                nw = vec[:, V_NORM + KD * (2 * l + 1):V_NORM + KD * (2 * l + 2)]

                def xT_evac(q, n):
                    for c in range(2):
                        dve.wait_ge(S["xg_T"], n * 2 + c + 1)
                        tt(xT[q][:, 4 * c:4 * c + 4, :], bank(c, 4, P),
                           bc(nw[:, 4 * c:4 * c + 4].unsqueeze(2), 4, P), ALU.mult).then_inc(S["xT_ready"], 1)

                xT_evac(0, l * (BLOCKS + 1))

                def blocks(i):
                    for q in range(2):
                        b = i * 2 + (l * BLOCKS + q)
                        dve.wait_ge(S["up_ps"], b + 1)
                        dve.wait_ge(S["sg_ready"], b + 1)
                        need(dve, S["hT_ps"], b)
                        tt(hid, sg, bank(3, 512), ALU.mult).then_inc(S["hid_ready"], 1)
                        xT_evac(1 - q, i * 2 + (l * (BLOCKS + 1) + q + 1))
                        dve.wait_ge(S["y_ps"], b * 2 + 2)
                        need(dve, S[f"scattered{q}"], i * 16 + 16 * l * PAIRS)
                        V.tensor_copy(yb[q][:, 512:1024], bank(6, 512)).then_inc(S["yB_ready"], 1)

                blocks(0)
                with dve.Fori(1, PAIRS) as i:
                    blocks(i)
                for i in range(TILES):
                    L = LEN[i]
                    dve.wait_ge(S[f"y2_loaded{i}"], 32 * (l + 1))
                    v(V.scalar_tensor_tensor(h[0:L, i, :], YL[i][0:L, 0, :], gates[0:L, i, 0:1], h[0:L, i, :],
                                             ALU.mult, ALU.add))
                    V.scalar_tensor_tensor(h[0:L, i, :], YL[i][0:L, 1, :], gates[0:L, i, 1:2], h[0:L, i, :],
                                           ALU.mult, ALU.add).then_inc(S["h_ready"], 1)

            norm(1)
            moe_dve(0)
            if stop <= 2:
                return

            norm(2)
            lg = vec[:, V_LB:V_LB + 16].rearrange("p (a b) -> p a b", a=2)
            v(tt(lbv[:, 0, :], lg[:, 0], lg[:, 1], ALU.max))
            tt(lbv[:, 1:3, :], lg, bc(lbv[:, 0:1, :], 2, HEADS), ALU.subtract).then_inc(S["lb_in"], 1)
            dve.wait_ge(S["lb_e"], 1)
            v(tt(lbv[:, 3, :], lbv[:, 1, :], lbv[:, 2, :], ALU.add))
            v(V.reciprocal(lbv[:, 3, :], lbv[:, 3, :]))
            v(tt(lbv[:, 1:3, :], lbv[:, 1:3, :], bc(lbv[:, 3:4, :], 2, HEADS), ALU.mult))
            v(tt(lbv[:, 4, :], lbv[:, 1, :], lbv[:, 2, :], ALU.add))
            v(tt(lbv[:, 4, :], lbv[:, 4, :], lbv[:, 1, :], ALU.subtract))
            v(V.tensor_scalar(lbv[:, 5, :], lbv[:, 4, :], -1.0, 1.0, ALU.mult, ALU.add))
            dve.wait_ge(S["proj_evac"], CONV_TILES + Z_TILES + 2 * HEADS)
            v(tt(hg, hg, bc(lbv[:, 5, :].unsqueeze(2), HEADS, TOK), ALU.mult))
            v(tt(hg, hg, bc(lbv[:, 4, :].unsqueeze(2), HEADS, TOK), ALU.add))
            V.tensor_scalar(hk, hg, -1.0, 1.0, ALU.mult, ALU.add).then_inc(S["lf_in"], 1)
            dve.wait_ge(S["lf_ready"], 1)
            for hd in range(HEADS):
                v(V.tensor_tensor_scan(hg[:, hd, :], con[:, C_SCAN:C_SCAN + TOK], hg[:, hd, :], 0.0,
                                       ALU.mult, ALU.add))
            n = 0
            m = 0
            dve.wait_ge(S["proj_evac"], CONV_TILES + Z_TILES + 4 * HEADS)
            for i in range(TILES):
                L, c0 = LEN[i], AT[i]
                st = hS[1 if i == 2 else 0]
                if i == 2:
                    dve.wait_ge(S["gdn_init"], 32)
                m += 1
                dve.wait_ge(S["hg_att"], m)
                v(tt(hA[0:L, :, 0:L], bank(0, 8, P, n=2)[0:L, :, 0:L], bc(ident[0:L, 0:L].unsqueeze(1), 8, L), ALU.mult))
                for lv, b in enumerate(LEVELS):
                    if b >= L:
                        continue
                    nb = L // (2 * b)
                    gv = hg[:, :, c0:c0 + L].rearrange("p a (n c) -> p a n c", c=2 * b)
                    ev = hE[:, :, 0:L].rearrange("p a (n c) -> p a n c", c=2 * b)
                    v(tt(ev, gv, bc(gv[:, :, :, b - 1:b], 8, nb, 2 * b), ALU.subtract))
                    V.scalar_tensor_tensor(hE[:, :, 0:L], hE[:, :, 0:L], -1.0, hE[:, :, 0:L], ALU.mult, ALU.max
                                           ).then_inc(S["hg_d"], 1)
                    n += 1
                    dve.wait_ge(S["hg_e"], n)
                    v(tt(hQ[:, :, 0:L], hq[:, :, c0:c0 + L], hE[:, :, 0:L], ALU.mult))
                    tt(hK[:, :, 0:L], hk[:, :, c0:c0 + L], hE[:, :, 0:L], ALU.mult).then_inc(S["hg_qk"], 1)
                    m += 1
                    dve.wait_ge(S["hg_att"], m)
                    v(tt(hVt[0:L, :, 0:L], bank(0, 8, P, n=2)[0:L, :, 0:L], bc(mask(lv)[0:L, 0:L].unsqueeze(1), 8, L),
                         ALU.mult))
                    v(tt(hA[0:L, :, 0:L], hA[0:L, :, 0:L], hVt[0:L, :, 0:L], ALU.add))
                tt(hEq[:, :, 0:L], bc(hg[:, :, c0 + L - 1:c0 + L], 8, L), hg[:, :, c0:c0 + L], ALU.subtract
                   ).then_inc(S["hg_x"], 1)
                dve.wait_ge(S["hg_ex"], i + 1)
                v(tt(hQ[:, :, 0:L], hq[:, :, c0:c0 + L], hE[:, :, 0:L], ALU.mult))
                tt(hK[:, :, 0:L], hk[:, :, c0:c0 + L], hEq[:, :, 0:L], ALU.mult).then_inc(S["hg_in"], 1)
                dve.wait_ge(S["hg_tr"], i + 1)
                v(V.tensor_copy(hKt[0:L], bank(2, 8, P, n=2)[0:L]))
                V.tensor_copy(hVt[0:L], bank(4, 8, P, n=2)[0:L]).then_inc(S["hg_acc"], 1)
                dve.wait_ge(S["hg_y"], i + 1)
                v(V.tensor_copy(hcat[:, :, c0:c0 + L], bank(6, 8, P, n=2)[:, :, 0:L]))
                if i == 0:
                    V.tensor_copy(st, bank(0, 8, P, n=2)).then_inc(S["hg_upd"], 1)
                else:
                    v(tt(st, st, bc(hDec.unsqueeze(2), 8, P), ALU.mult))
                    tt(st, st, bank(0, 8, P, n=2), ALU.add).then_inc(S["hg_upd"], 1)
            dve.wait_ge(S["hg_upd"], TILES)
            head_norm(hcat, hz, rs1, vec[:, V_HNORM:V_HNORM + 1], 3, 6)
            residual(6, 2)
            norm(3)
            moe_dve(1)
            norm(4)

        @block.tensor
        def _(pe):
            MM = nc.tensor.matmul

            def norm(n):
                for i in range(TILES):
                    pe.wait_ge(S["xn_ready"], n * TILES + i + 1)
                    L = LEN[i]
                    for c in range(2):
                        k = 2 * i + c
                        if k >= 4:
                            pe.wait_ge(S["uT_ready"], 6 * n + k - 3)
                        for j in range(4):
                            t_ = nc.tensor.transpose(bank(4 + k % 4, 4, P)[:, j, 0:L],
                                                     xn[0:L, i, 4 * c + j::KD], ident[0:L, 0:L])
                        t_.then_inc(S["xnT_ps"], 1)

            def project(tiles, first, group):
                for t in range(tiles):
                    s = (t // 4) % 3
                    if t % 4 == 0:
                        pe.wait_ge(S[f"ring{s}"], 16 * (ring_use(group, t // 4)))
                    if t >= 4:
                        pe.wait_ge(S["proj_evac"], first + t - 3)
                    for k in range(KD):
                        m_ = MM(ps[:, t % 4, 0:TOK], ring[s][:, k, (t % 4) * P:(t % 4 + 1) * P], uT[:, k, :],
                                start=(k == 0), stop=(k == KD - 1))
                    m_.then_inc(S["proj_ps"], 1)

            def decays(i, h0):
                L = LEN[i]
                for hd in range(8):
                    m_ = MM(bank(0, 8, P, n=2)[:, hd, 0:L], G24[0:L, i, h0 + hd:h0 + hd + 1].to_broadcast([L, P]),
                            triu[0:L, 0:L], start=True, stop=True)
                return m_

            pe.wait_ge(S["consts_loaded"], 80)
            norm(0)
            pe.wait_ge(S["uT_ready"], 6)
            project(CONV_TILES + Z_TILES, 0, 0)
            for i in range(TILES):
                for k in range(KD):
                    m_ = MM(ps[0:LEN[i], 4 + i, 0:32], uT[:, k, AT[i]:AT[i] + LEN[i]], wsm[:, k, :],
                            start=(k == 0), stop=(k == KD - 1))
                m_.then_inc(S["small_ps"], 1)
            pe.wait_ge(S["g_ready"], 1)
            pe.wait_ge(S["proj_evac"], CONV_TILES + Z_TILES)
            for i in range(TILES):
                m_ = MM(ps[0:LEN[i], 3, i * 32:i * 32 + SCAL], triu[0:LEN[i], 0:LEN[i]], G24[0:LEN[i], i, :],
                        start=True, stop=True)
            m_.then_inc(S["cum_ps"], 1)
            pe.wait_ge(S["conv_act"], CONV_TILES)
            for u in range(2 * TILES):
                i, g = u // 2, u % 2
                L, x0 = LEN[i], AX[i]
                st = HT[1 if i == 2 else 0]
                if u:
                    pe.wait_ge(S["ssd_upd"], u)
                    pe.wait_ge(S["ssd_exp"], 3 * u)
                if u == 4:
                    pe.wait_ge(S["state_in"], 16)
                    for c in range(2):
                        for j in range(4):
                            t_ = nc.tensor.transpose(bank(6 + c, 4, P)[:, j, :], s_load[:, 4 * c + j, :], ident)
                        t_.then_inc(S["st_T"], 1)
                    pe.wait_ge(S["st_Tevac"], 1)
                decays(i, 8 * g)
                for c in range(4):
                    nc.tensor.transpose(bank(5, 4, P)[0:L, c, :], XC[:, 4 * g + c, x0:x0 + L], ident)
                nc.tensor.transpose(ps[0:L, 6, 0:P], XC[:, 8 + g, x0:x0 + L], ident)
                MM(ps[0:L, 2, 0:L], XC[:, 8 + g, x0:x0 + L], XC[:, 10 + g, x0:x0 + L], start=True, stop=True
                   ).then_inc(S["ssd_in"], 1)
                pe.wait_ge(S["ssd_w"], u + 1)
                for hd in range(8):
                    lo = 64 * (hd % 2)
                    out = bank(3, 4, P)[lo:lo + 64, hd // 2, 0:L]
                    MM(out, Xdt[0:L, hd, :], W8[0:L, hd, 0:L], start=True, stop=(i == 0))
                    if i:
                        MM(out, st[:, g, 64 * hd:64 * hd + 64], Cs[:, hd, 0:L], start=False, stop=True)
                MM(bank(4, 512), Btok[0:L], Xtl[0:L].rearrange("p a b -> p (a b)"), start=True, stop=True
                   ).then_inc(S["ssd_y"], 1)
            pe.wait_ge(S["ssd_upd"], 2 * TILES)
            for n in range(2):
                for c in range(2):
                    if n:
                        pe.wait_ge(S["ssd_final"], n)
                    for j in range(4):
                        t_ = nc.tensor.transpose(bank(6 + c, 4, P)[:, j, :], HT[n][:, c, P * j:P * j + P], ident)
                    t_.then_inc(S["st_T"], 1)
            pe.wait_ge(S["sq2_done"], 1)
            for g in range(2):
                for c in range(4):
                    m_ = MM(ps[:, g, 0:TOK], ones, uT[:, 4 * g + c, :], start=(c == 0), stop=(c == 3))
            m_.then_inc(S["nrm_ps"], 1)
            for r in range(2):
                pe.wait_ge(S["sq2_done"], 2 + r)
                for c in range(4):
                    m_ = MM(ps[:, c, 0:XW], ones, sq4[:, c, :], start=True, stop=True)
                m_.then_inc(S["nrm_ps"], 1)
            pe.wait_ge(S["nrm_done"], 3)
            for i in range(TILES):
                L, x0 = LEN[i], AX[i]
                st = GS[1 if i == 2 else 0]
                if i:
                    pe.wait_ge(S["gdn_upd"], i)
                decays(i, SSD_HEADS)
                for j in range(4):
                    kk = XC[:, 16 + j, x0:x0 + L]
                    MM(bank(2, 4, P)[0:L, j, 0:L], kk, kk, start=True, stop=True)
                    MM(bank(3, 4, P)[0:L, j, 0:L], kk, XC[:, 12 + j, x0:x0 + L], start=True, stop=True)
                    nc.tensor.transpose(bank(6, 4, P)[0:L, j, :], kk, ident)
                for hd in range(8):
                    t_ = nc.tensor.transpose(bank(4, 8, P, n=2)[0:L, hd, :], XC[:, 20 + hd, x0:x0 + L], ident)
                t_.then_inc(S["gdn_in"], 1)
                lv = [n for n, b in enumerate(LEVELS) if b < L]
                for n, b in enumerate(lv):
                    k = gdn_level(i, n)
                    pe.wait_ge(S["gdn_bm"], k + 1)
                    if k:
                        pe.wait_ge(S["gdn_tu"], k)
                    for hd in range(8):
                        m_ = MM(bank(4, 8, P, n=2)[0:L, hd, 0:L], Bm[0:L, hd, 0:L], T8[0:L, hd, 0:L],
                                start=True, stop=True)
                    m_.then_inc(S["gdn_pe"], 1)
                    pe.wait_ge(S["gdn_p"], k + 1)
                    if n < len(lv) - 1:
                        for hd in range(8):
                            MM(bank(6, 8, P, n=2)[0:L, hd, 0:L], TT8[0:L, hd, 0:L], P8[0:L, hd, 0:L],
                               start=True, stop=True)
                    for hd in range(8):
                        m_ = MM(bank(0, 8, P, n=2)[0:L, hd, 0:L], P8[0:L, hd, 0:L], TT8[0:L, hd, 0:L],
                                start=True, stop=True)
                    m_.then_inc(S["gdn_pe"], 1)
                if i > 0:
                    if i == 2:
                        pe.wait_ge(S["gdn_init"], 16)
                    for hd in range(8):
                        m_ = MM(bank(4, 8, P, n=2)[0:L, hd, :], XC[:, 16 + hd // 2, x0:x0 + L], st[:, hd, :],
                                start=True, stop=True)
                    m_.then_inc(S["gdn_ks"], 1)
                pe.wait_ge(S["gdn_rhs"], i + 1)
                for hd in range(8):
                    m_ = MM(bank(6, 8, P, n=2)[0:L, hd, :], TT8[0:L, hd, 0:L], RHS[0:L, hd, :], start=True, stop=True)
                m_.then_inc(S["gdn_u"], 1)
                pe.wait_ge(S["gdn_ue"], i + 1)
                for hd in range(8):
                    out = bank(2, 8, P, n=2)[:, hd, 0:L]
                    MM(out, U8[0:L, hd, :], DQK[0:L, hd, 0:L], start=True, stop=(i == 0))
                    if i:
                        MM(out, st[:, hd, :], qs[:, hd, 0:L], start=False, stop=True)
                for hd in range(8):
                    m_ = MM(bank(4, 8, P, n=2)[:, hd, :], Kt[0:L, hd, :], U8[0:L, hd, :], start=True, stop=True)
                m_.then_inc(S["gdn_o"], 1)

            def head_sums(sq):
                pe.wait_ge(S["sq2_done"], sq)
                for r in range(2):
                    for c in range(4):
                        m_ = MM(ps[:, 4 * r + c, 0:TOK], ones, uT[:, 4 * r + c, :], start=True, stop=True)
                    m_.then_inc(S["nrm_ps"], 1)

            head_sums(4)

            def project_out(src, groups, first, ready):
                pe.wait_ge(S["cat_ready"], ready)
                for g in range(groups):
                    pe.wait_ge(S[f"out_loaded{g % 3}"], 16 * out_use(first, g))
                    w = ring[g % 3].rearrange("p a b -> p (a b)").rearrange("p (c d) -> p c d", c=4)
                    for c in range(4):
                        k = 4 * g + c
                        for i in range(TILES):
                            for n in range(2):
                                m_ = MM(ps[0:LEN[i], 2 * i + n, :], src[:, k, AT[i]:AT[i] + LEN[i]],
                                        w[:, c, 512 * n:512 * n + 512], start=(k == 0), stop=(k == 4 * groups - 1))
                    m_.then_inc(S["out_ps"], 1)

            project_out(cat, 4, 0, 1)

            def moe_pe(l):
                pe.wait_ge(S["uT_ready"], 6 * (2 * l + 2))
                for i in range(TILES):
                    for k in range(KD):
                        m_ = MM(ps[0:LEN[i], 0, i * 64:i * 64 + 36], uT[:, k, AT[i]:AT[i] + LEN[i]], wrt[:, l, k, :],
                                start=(k == 0), stop=(k == KD - 1))
                m_.then_inc(S["lg_ps"], 1)
                pe.wait_ge(S["rt_A"], l + 1)
                for i in range(TILES):
                    L = LEN[i]
                    for j in range(i):
                        MM(ps[0:L, 1, i * 32:i * 32 + 32], ones[:, 0:L], A2[:, j, :], start=(j == 0), stop=False)
                    MM(ps[0:L, 1, i * 32:i * 32 + 32], striu[0:L, 0:L], A2[0:L, i, :], start=(i == 0), stop=True)
                for i in range(TILES):
                    m_ = MM(ps[:, 1, 96:128], ones[0:LEN[i], :], A2[0:LEN[i], i, :], start=(i == 0), stop=(i == 2))
                m_.then_inc(S["rt_R"], 1)
                pe.wait_ge(S["rt_OH"], l + 1)
                for k in range(6):
                    L = LEN[k // 2]
                    m_ = MM(ps[:, 2, 0:COLS], OPm[0:L, k, :], OBm[0:L, k, :], start=(k == 0), stop=(k == 5))
                m_.then_inc(S["rt_tab"], 1)
                if stop <= 1:
                    return

                def turn(q, gathered, n):
                    pe.wait_ge(S[f"xgathered{q}"], gathered)
                    need(pe, S["xT_ready"], n * 2)
                    for c in range(2):
                        for j in range(4):
                            t_ = nc.tensor.transpose(bank(c, 4, P)[:, j, :], xg[q][:, 4 * c + j::KD], ident)
                        t_.then_inc(S["xg_T"], 1)

                turn(0, 16 * (l * (PAIRS + 1) + 1), l * (BLOCKS + 1))

                def blocks(i):
                    for q in range(2):
                        b = i * 2 + (l * BLOCKS + q)
                        loaded = i * 16 + 16 * (l * PAIRS + 1)
                        pe.wait_ge(S[f"wg{q}"], loaded)
                        pe.wait_ge(S["xT_ready"], i * 4 + (2 * (l * (BLOCKS + 1) + q) + 2))
                        need(pe, S["sg_ready"], b)
                        for k in range(KD):
                            m_ = MM(bank(2, 512), xT[q][:, k, :], wgb[q][:, k, :], start=(k == 0), stop=(k == KD - 1))
                        m_.then_inc(S["gate_ps"], 1)
                        pe.wait_ge(S[f"wu{q}"], loaded)
                        need(pe, S["hid_ready"], b)
                        for k in range(KD):
                            m_ = MM(bank(3, 512), xT[q][:, k, :], wub[q][:, k, :], start=(k == 0), stop=(k == KD - 1))
                        m_.then_inc(S["up_ps"], 1)
                        if q == 0:
                            turn(1, i * 16 + 16 * (l * PAIRS + 1), i * 2 + (l * (BLOCKS + 1) + 1))
                        else:
                            turn(0, i * 16 + 16 * (l * (PAIRS + 1) + 2), i * 2 + (l * (BLOCKS + 1) + 2))
                        pe.wait_ge(S["hid_ready"], b + 1)
                        need(pe, S["hidT_ready"], b)
                        for k in range(KE):
                            t_ = nc.tensor.transpose(bank(4, KE, P)[:, k, :], hid[:, k::KE], ident)
                        t_.then_inc(S["hT_ps"], 1)
                        pe.wait_ge(S["hidT_ready"], b + 1)
                        pe.wait_ge(S[f"wd{q}"], loaded)
                        for n, done in ((0, "yA_ready"), (1, "yB_ready")):
                            need(pe, S[done], b)
                            for k in range(KE):
                                m_ = MM(bank(5 + n, 512), hidT[:, k, :], wdb[q][:, k, 512 * n:512 * n + 512],
                                        start=(k == 0), stop=(k == KE - 1))
                            m_.then_inc(S["y_ps"], 1)

                blocks(0)
                with pe.Fori(1, PAIRS) as i:
                    blocks(i)

            norm(1)
            moe_pe(0)
            if stop <= 2:
                return
            norm(2)
            pe.wait_ge(S["uT_ready"], 18)
            project(4 * HEADS, CONV_TILES + Z_TILES, 1)
            pe.wait_ge(S["proj_evac"], CONV_TILES + Z_TILES + 4 * HEADS)
            pe.wait_ge(S["lf_in"], 1)
            n = 0
            for i in range(TILES):
                L, c0 = LEN[i], AT[i]
                st = hS[1 if i == 2 else 0]
                if i:
                    pe.wait_ge(S["hg_upd"], i)
                GB = bank(0, 8, P, n=2)
                for hd in range(8):
                    m_ = MM(GB[0:L, hd, 0:L], hk[:, hd, c0:c0 + L], hq[:, hd, c0:c0 + L], start=True, stop=True)
                m_.then_inc(S["hg_att"], 1)
                for b in LEVELS:
                    if b >= L:
                        continue
                    n += 1
                    pe.wait_ge(S["hg_qk"], n)
                    for hd in range(8):
                        m_ = MM(GB[0:L, hd, 0:L], hK[:, hd, 0:L], hQ[:, hd, 0:L], start=True, stop=True)
                    m_.then_inc(S["hg_att"], 1)
                pe.wait_ge(S["hg_in"], i + 1)
                for hd in range(8):
                    nc.tensor.transpose(bank(2, 8, P, n=2)[0:L, hd, :], hK[:, hd, 0:L], ident)
                    t_ = nc.tensor.transpose(bank(4, 8, P, n=2)[0:L, hd, :], hv[:, hd, c0:c0 + L], ident)
                t_.then_inc(S["hg_tr"], 1)
                pe.wait_ge(S["hg_acc"], i + 1)
                if i == 2:
                    pe.wait_ge(S["gdn_init"], 32)
                for hd in range(8):
                    out = bank(6, 8, P, n=2)[:, hd, 0:L]
                    MM(out, hVt[0:L, hd, :], hA[0:L, hd, 0:L], start=True, stop=(i == 0))
                    if i:
                        MM(out, st[:, hd, :], hQ[:, hd, 0:L], start=False, stop=True)
                for hd in range(8):
                    m_ = MM(GB[:, hd, :], hKt[0:L, hd, :], hVt[0:L, hd, :], start=True, stop=True)
                m_.then_inc(S["hg_y"], 1)
            head_sums(5)
            project_out(hcat, 2, 4, 2)
            norm(3)
            moe_pe(1)


def gdn_level(i, n):
    return sum(sum(b < LEN[j] for b in LEVELS) for j in range(i)) + n


def ring_use(projection, group):
    slot = group % 3
    before = len(range(slot, AB_GROUPS, 3)) if projection else 0
    return before + group // 3 + 1


def out_use(first, group):
    slot = group % 3
    before = len(range(slot, 4, 3)) if first else 0
    return before + group // 3 + 1


def constants():
    import numpy as np
    c = np.zeros((P, C_END), np.float32)
    i, j = np.arange(P)[:, None], np.arange(P)[None, :]
    c[:, C_ID:C_ID + P] = i == j
    c[:, C_ONES:C_ONES + P] = 1
    c[:, C_TRIU:C_TRIU + P] = i <= j
    c[:, C_STRIU:C_STRIU + P] = i < j
    for n, b in enumerate(LEVELS):
        c[:, C_MASK + n * P:C_MASK + (n + 1) * P] = (i // (2 * b) == j // (2 * b)) & (i % (2 * b) < b) & (j % (2 * b) >= b)
    c[:, C_IOTA:C_IOTA + P] = j
    for t in range(TILES):
        for k in range(2):
            c[:, C_VAL + 2 * t + k] = AT[t] + np.arange(P) + 1 + TOK * k
    c[:, C_SCAN:C_SCAN + TOK] = 1
    for t in range(TILES):
        c[:, C_SCAN + AT[t]] = 0
    c[:, C_EPS] = EPS
    return c


def lay_out(x):
    import numpy as np
    f = {n: np.asarray(a) for n, a in x.items()}
    w = f["w_in_ab"][0]
    zs, xbc, dt, qkv, zg, b, a = np.split(w, np.cumsum([1024, 1536, 16, 2048, 1024, 8])[:].tolist(), axis=1)
    main = np.concatenate([xbc, qkv, zs, zg], axis=1)
    tile = lambda m: np.ascontiguousarray(
        m.reshape(P, KD, -1, GROUP).transpose(2, 0, 1, 3)).reshape(-1, P, KD * GROUP)
    chan = lambda m: m.reshape(-1, P).T
    conv_w = np.concatenate([f["ssd_conv_w"][0], f["gdn_conv_w"][0]], axis=1).reshape(CONV_W, CONV_TILES, P)
    conv_b = np.concatenate([f["ssd_conv_b"][0], np.zeros(QKV_TILES * P, np.float32)])
    vec = np.concatenate(
        [f[n][l].reshape(P, KD) for l in range(2) for n in ("norm_mix", "norm_ffn")]
        + [conv_w.transpose(2, 1, 0).reshape(P, -1), chan(conv_b), chan(np.repeat(f["ssd_d"][0], 64)),
           chan(f["ssd_norm"][0]), f["gdn_norm"][0][:, None], f["hgrn_norm"][0][:, None],
           f["hgrn_lb_logits"].reshape(2, HEADS, P).transpose(2, 0, 1).reshape(P, -1)], axis=1)
    st = np.concatenate([f["state_ssd_conv"][0, 0], f["state_gdn_conv"][0, 0]], axis=1)
    return {
        "con": constants(), "vec": np.ascontiguousarray(vec),
        "row": np.concatenate([f["ssd_dt_bias"][0], f["gdn_dt_bias"][0], f["ssd_a_log"][0], f["gdn_a_log"][0]])[None],
        "final": np.ascontiguousarray(f["norm_final"][None]),
        "wsm": np.ascontiguousarray(np.concatenate([dt, a, b], axis=1).reshape(P, KD, 32)),
        "wrt": np.ascontiguousarray(np.concatenate([f["moe_w_group"], f["moe_w_router"]], axis=2)
                                    .reshape(2, P, KD, 36).transpose(1, 0, 2, 3)),
        "wA": tile(main), "wC": tile(f["w_in_c"][0]),
        "w_out_ab": f["w_out_ab"][0], "w_out_c": f["w_out_c"][0],
        "wg": f["moe_w_gate"], "wu": f["moe_w_up"], "wd": f["moe_w_down"],
        "xp": f["x_prompt"][0], "xs": f["x_sample"][0],
        "conv_st": np.ascontiguousarray(st.reshape(TAPS, CONV_TILES, P).transpose(2, 1, 0)),
        "st_ssd": f["state_ssd"].reshape(SSD_HEADS * 64, 128), "st_gdn": f["state_gdn"][0, 0],
        "st_hgrn": f["state_hgrn"][0, 0],
    }


OUTS = {"y_p": (SEQ, D_MODEL), "y_s": (DEC_SEQ, D_MODEL), "conv": (2, P, CONV_TILES, TAPS),
        "ssd_p": (SSD_HEADS * 64, P), "ssd_s": (SSD_HEADS * 64, P), "gdn_p": (8, P, P), "gdn_s": (8, P, P),
        "hgrn_p": (8, P, P), "hgrn_s": (8, P, P)}


def kernel(**inputs):
    import concourse.bacc as _bacc
    from concourse import mybir as _mybir
    from concourse.bass_utils import run_bass_kernel_spmd as _run

    arrays = lay_out(inputs)
    nc = _bacc.Bacc("TRN2", target_bir_lowering=False, num_devices=1)
    ins = {n: nc.dram_tensor(f"in_{n}", a.shape, _mybir.dt.from_np(a.dtype), kind="ExternalInput").ap()
           for n, a in arrays.items()}
    outs = {n: nc.dram_tensor(f"out_{n}", s, _mybir.dt.float32, kind="ExternalOutput").ap() for n, s in OUTS.items()}
    build(nc, ins, outs)
    r = _run(nc, [{f"in_{n}": a for n, a in arrays.items()}], core_ids=[0]).results[0]
    out = {n: r[f"out_{n}"] for n in OUTS}
    conv = out["conv"].transpose(0, 3, 2, 1).reshape(2, 1, 1, TAPS, CONV_TILES * P)
    cut = XBC_TILES * P
    ssd = lambda a: a.reshape(1, 1, SSD_HEADS, 64, P)
    hd = lambda a: a.reshape(1, 1, 8, P, P)
    return (out["y_p"][None], out["y_s"][None],
            ssd(out["ssd_p"]), conv[0, ..., :cut], hd(out["gdn_p"]), conv[0, ..., cut:], hd(out["hgrn_p"]),
            ssd(out["ssd_s"]), conv[1, ..., :cut], hd(out["gdn_s"]), conv[1, ..., cut:], hd(out["hgrn_s"]))
```

```python
import concourse.bass as bass
from concourse import mybir
from contextlib import ExitStack

D_MODEL = 1024
SEQ, DEC_SEQ = 256, 32
TOK = SEQ + DEC_SEQ
P = 128
KD = D_MODEL // P
TILES = 3
LEN = [P, P, DEC_SEQ]
AT = [0, P, 2 * P]
CONV_W = 4
TAPS = CONV_W - 1
XW = TOK + TAPS
AX = [0, P, SEQ + TAPS]
XP = XW + TAPS
EPS = 1e-6
SSD_HEADS, SSD_GROUPS, SSD_TILES = 16, 2, 8
XBC_TILES, QKV_TILES = 12, 16
CONV_TILES = XBC_TILES + QKV_TILES
GDN_HEADS, GDN_K_HEADS = 8, 4
Z_TILES = 16
HEADS = 8
SCAL = SSD_HEADS + GDN_HEADS
GROUP = 512
AB_GROUPS = (CONV_TILES + Z_TILES) * P // GROUP
C_GROUPS = 4 * D_MODEL // GROUP
EXPERTS, E_GROUPS, E_PER, D_EXP = 32, 4, 8, 512
KE = D_EXP // P
SLOTS = 64
EXTRA = (2 * TOK - 1) // SLOTS
SHIFT = SLOTS.bit_length() - 1
HALVES = P // SLOTS
PAIRS = EXPERTS // 2
COLS = EXPERTS + EXTRA
NOWHERE = 1.0e6
LEVELS = [1, 2, 4, 8, 16, 32, 64]

C_ID, C_ONES, C_TRIU, C_STRIU, C_MASK = 0, P, 2 * P, 3 * P, 4 * P
C_IOTA = C_MASK + len(LEVELS) * P
C_VAL = C_IOTA + P
C_SCAN = C_VAL + TILES * 2
C_EPS = C_SCAN + TOK
C_HALF = C_EPS + 1
C_SLOT = C_HALF + 1
C_EPSQ = C_SLOT + P
C_END = C_EPSQ + 1
V_NORM, V_CONV, V_BIAS = 0, 4 * KD, 4 * KD + CONV_TILES * CONV_W
V_D = V_BIAS + CONV_TILES
V_SNORM = V_D + SSD_TILES
V_GNORM = V_SNORM + SSD_TILES
V_HNORM = V_GNORM + 1
V_LB = V_HNORM + 1
V_END = V_LB + 2 * HEADS
R_BIAS, R_ALOG, R_END = 0, SCAL, 2 * SCAL


def build(nc, ins, outs, stop=99):
    F, I32, U32 = mybir.dt.float32, mybir.dt.int32, mybir.dt.uint32
    ACT, ALU, AX_X = mybir.ActivationFunctionType, mybir.AluOpType, mybir.AxisListType.X

    xn_dram = nc.dram_tensor("xn_rows", [TOK, D_MODEL], F, kind="Internal").ap()
    y2_dram = nc.dram_tensor("expert_rows", [2 * TOK * HALVES, D_MODEL // HALVES], F, kind="Internal").ap()
    wg_dram = ins["wg"].rearrange("l e (p k) f -> (l e) p (k f)", p=P)
    wu_dram = ins["wu"].rearrange("l e (p k) f -> (l e) p (k f)", p=P)
    wd_dram = ins["wd"].rearrange("l e (k p) f -> (l e) p k f", p=P)

    ctx = ExitStack()
    with ctx:
        def sb(name, shape, dt=F):
            return ctx.enter_context(nc.sbuf_tensor(name, shape, dt))

        def sem(name):
            return ctx.enter_context(nc.semaphore(name))

        h = sb("h", [P, TILES, D_MODEL])
        xn = sb("xn", [P, TILES, D_MODEL])
        uT = sb("uT", [P, KD, TOK])
        con = sb("con", [P, C_END])
        vec = sb("vec", [P, V_END])
        row = sb("row", [P, R_END])
        wsm = sb("wsm", [P, KD, 32])
        wrt = sb("wrt", [P, 2, KD, 36])
        ss = sb("ss", [P, 5, TILES])
        rstd = sb("rstd", [P, 5, TILES])
        ps = ctx.enter_context(nc.psum_tensor("ps", [P, 8, 512], F))
        ARENA = 37900
        arena = sb("arena", [P, ARENA])

        def at(off, *dims):
            n = 1
            for d in dims:
                n *= d
            assert off + n <= ARENA, (off, dims)
            flat = arena[:, off:off + n]
            if len(dims) == 1:
                return flat
            names = ["a", "b", "c", "d"][:len(dims)]
            return flat.rearrange("p (" + " ".join(names) + ") -> p " + " ".join(names),
                                  **dict(zip(names[1:], dims[1:])))

        def bank(b, *dims, n=1):
            flat = ps[:, b:b + n, :].rearrange("p a b -> p (a b)")
            size = 1
            for d in dims:
                size *= d
            names = ["a", "b", "c"][:len(dims)]
            if len(dims) == 1:
                return flat[:, 0:size]
            return flat[:, 0:size].rearrange("p (" + " ".join(names) + ") -> p " + " ".join(names),
                                             **dict(zip(names[1:], dims[1:])))

        ident = con[:, C_ID:C_ID + P]
        ones = con[:, C_ONES:C_ONES + P]
        triu = con[:, C_TRIU:C_TRIU + P]
        striu = con[:, C_STRIU:C_STRIU + P]
        eps = con[:, C_EPS:C_EPS + 1]
        iota = con[:, C_IOTA:C_IOTA + P]

        def mask(n):
            return con[:, C_MASK + n * P:C_MASK + (n + 1) * P]

        def take(cursor, end, *dims):
            n = 1
            for d in dims:
                n *= d
            off = cursor[0]
            cursor[0] += n
            assert cursor[0] <= end, (cursor, end)
            return at(off, *dims)

        RING = 3 * KD * GROUP
        ring = [at(s * KD * GROUP, KD, GROUP) for s in range(3)]
        cur = [RING]
        XC = take(cur, ARENA, CONV_TILES, XW)
        Z = take(cur, ARENA, Z_TILES, TOK)
        cat = take(cur, ARENA, 16, TOK)
        in_pad = cur[0]
        xpad = take(cur, ARENA, CONV_TILES, XP)
        STAGE = RING - 1024
        s_stage = at(STAGE, 8, P)
        cur = [0]
        Xdt, Xtl = take(cur, STAGE, 8, 64), take(cur, STAGE, 8, 64)
        Btok, BCm = take(cur, STAGE, P), take(cur, STAGE, P)
        HT = [take(cur, STAGE, 2, 512) for _ in range(2)]
        s_load = take(cur, STAGE, 8, P)
        cur = [in_pad]
        Dm, EG, W8, Cs = [take(cur, ARENA, 8, P) for _ in range(4)]
        DQK, DKK = take(cur, ARENA, 8, P), take(cur, ARENA, 8, P)
        tail, dec, ecum, nbe = [take(cur, ARENA, 8) for _ in range(4)]
        qs = W8
        cur = [0]
        GS = [take(cur, STAGE, 8, P) for _ in range(2)]
        T8, TT8, P8, VB, U8, Bm0, Kt, Bm1 = [take(cur, STAGE, 8, P) for _ in range(8)]
        Ktok = take(cur, STAGE, 4, P)
        Bm, RHS = [Bm0, Bm1], P8
        conv_st = sb("conv_st", [P, CONV_TILES, TAPS])
        conv_new = sb("conv_new", [P, 2, CONV_TILES, TAPS])
        cvt = sb("cvt", [P, 2, XW])
        sc = sb("sc", [P, TILES, 32])
        spx = sb("spx", [P, 4, TILES, SCAL])
        dtg = sb("dtg", [P, TILES, SCAL])
        G24 = sb("G24", [P, TILES, SCAL])
        cum = sb("cum", [P, TILES, SCAL])
        eA = sb("eA", [P, SCAL])
        beta = sb("beta", [P, TILES, 8])
        cur = [RING]
        hq, hk, hg, hv, hz, hcat = [take(cur, ARENA, HEADS, TOK) for _ in range(6)]
        in_hE = cur[0]
        hE, hQ, hK, hA, hVt, hKt, hEq = [take(cur, ARENA, 8, P) for _ in range(7)]
        hD = [at(2048, 8, P), at(3072, 8, P)]
        hR = [at(4096, 8, P), at(5120, 8, P)]
        hDec = take(cur, ARENA, 8)
        hS = [at(0, 8, P), at(1024, 8, P)]
        lbv = sb("lbv", [P, 6, HEADS])
        cur = [0]
        wgb = [take(cur, ARENA, KD, D_EXP) for _ in range(2)]
        wub = [take(cur, ARENA, KD, D_EXP) for _ in range(2)]
        wdb = [take(cur, ARENA, KE, D_MODEL) for _ in range(2)]
        in_xg = cur[0]
        xg = [take(cur, ARENA, D_MODEL) for _ in range(2)]
        xT = [take(cur, ARENA, KD, SLOTS) for _ in range(2)]
        hid, sg = take(cur, ARENA, D_EXP // HALVES), take(cur, ARENA, D_EXP // HALVES)
        hidT = take(cur, ARENA, KE // HALVES, P)
        yb = [take(cur, ARENA, D_MODEL // HALVES) for _ in range(2)]
        in_yl = cur[0]
        YL = [take(cur, ARENA, 2, D_MODEL) for _ in range(2)] + [at(in_xg, 2, D_MODEL)]
        OPm, OBm = at(in_yl, 6, P), at(in_yl + 6 * P, 6, COLS)
        LG = sb("LG", [P, TILES, 36])
        RT = sb("rt", [P, 1720])
        rcur = [0]

        def small(*dims):
            n = 1
            for d in dims:
                n *= d
            off = rcur[0]
            rcur[0] += n
            assert rcur[0] <= 1720
            flat = RT[:, off:off + n]
            if len(dims) == 1:
                return flat
            names = ["a", "b", "c"][:len(dims)]
            return flat.rearrange("p (" + " ".join(names) + ") -> p " + " ".join(names),
                                  **dict(zip(names[1:], dims[1:])))

        gl8, gm8 = small(3, 8), small(3, 8)
        gif, sgm, den = small(3, 1), small(3, 1), small(3, 1)
        rt_ge, ohg = small(3, 4), small(3, 4)
        selm, esel, ev8 = small(3, 32), small(3, 8), small(3, 8)
        eif, eid, rt_e2 = small(3, 2), small(3, 2), small(3, 1)
        O2, OD = small(3, 2, 32), small(3, 2, 32)
        A2, R2, over, extb = small(3, 32), small(3, 32), small(3, 32), small(3, 32)
        cnt, nx, incl, exb = small(32), small(32), small(32), small(32)
        pos, p1f, b1f = small(6), small(6), small(6)
        tb, inv, jj, c2 = small(COLS), small(COLS), small(COLS), small(COLS)
        xe = small(EXTRA + 1)
        cmp = small(EXTRA, 32)
        gi8 = sb("gi8", [P, 3, 8], U32)
        ei8 = sb("ei8", [P, 3, 8], U32)
        posi = sb("posi", [P, 3, 6], I32)
        gates = sb("gates", [P, TILES, 2])
        gidx = sb("gidx", [P, COLS], U32)
        sidx = sb("sidx", [P, COLS], U32)
        extra_e = sb("extra_e", [1, 2, EXTRA + 1], I32)

        uT_flat = uT[:, :, :].rearrange("p a b -> p (a b)")
        sq4 = uT_flat[:, 0:4 * XW].rearrange("p (a b) -> p a b", a=4)
        final_w = uT_flat[:, 0:D_MODEL]
        rs0 = at(in_pad, 4, XW)
        rs1 = at(in_hE, 4, XW)
        S = {}

        def s_(name):
            if name not in S:
                S[name] = sem(name)
            return S[name]

        for name in ("x_loaded consts_loaded h_ready sq_done xn_ready xnT_ps uT_ready dve_step act_step proj_ps proj_evac "
                     "conv_out conv_act z_act small_ps small_evac sp_exp1 sp_pos sp_ln g_ready ea_ready cum_ps "
                     "cum_ready ssd_in ssd_diff ssd_exp ssd_w ssd_y ssd_upd st_T st_Tevac state_in ssd_final "
                     "yg_ready sq2_done nrm_ps nrm_done qk_sq qk_ps qk_done gdn_in gdn_diff gdn_exp gdn_mats "
                     "gdn_bm gdn_p gdn_pe gdn_pt gdn_tu gdn_ks gdn_rhs gdn_u gdn_ue gdn_o gdn_upd gdn_init gdn_final "
                     "cat_ready out_ps out_loaded0 out_loaded1 out_loaded2 states_out conv_new_ready beta_ready "
                     "ring0 ring1 ring2 lf_in lf_ready lb_e lb_in hg_keep hg_d hg_e hg_qk hg_att hg_acc hg_in hg_x hg_y hg_ex hg_upd hg_tr "
                     "lg_ps rt_diff rt_exp rt_A rt_R rt_OH rt_tab route_done xn_stored "
                     "xgathered0 xgathered1 xg_T xT_ready wg0 wg1 wu0 wu1 wd0 wd1 gate_ps up_ps sg_ready "
                     "hid_ready hT_ps hidT_ready y_ps y_ready scattered0 scattered1 "
                     "xg_zero y2_loaded0 y2_loaded1 y2_loaded2 y_out act_tmp hist_loaded final_loaded rs_done rs_done").split():
            s_(name)
        extra_signals = [{n: sem(f"extra{l}_{n}") for n in
                          ("wg", "wu", "wd", "xgathered", "scattered", "xg_T", "xT_ready", "gate_ps", "up_ps", "sg_ready",
                           "hid_ready", "hT_ps", "hidT_ready", "y_ps", "y_ready")} for l in range(2)]

        def need(eng, semaphore, value):
            if not isinstance(value, int) or value > 0:
                eng.wait_ge(semaphore, value)

        block = ctx.enter_context(nc.Block())

        @block.sync
        def _(sp):
            sp.dma_start(con[:, :], ins["con"]).then_inc(S["consts_loaded"], 16)
            sp.dma_start(vec[:, :], ins["vec"]).then_inc(S["consts_loaded"], 16)
            sp.dma_start(row[:, :], ins["row"].to_broadcast([P, R_END])).then_inc(S["consts_loaded"], 16)
            sp.dma_start(wsm[:, :, :], ins["wsm"]).then_inc(S["consts_loaded"], 16)
            sp.dma_start(wrt[:, :, :, :], ins["wrt"]).then_inc(S["consts_loaded"], 16)
            sp.dma_start(h[:, 0:2, :], ins["xp"].rearrange("(t p) d -> p t d", p=P)).then_inc(S["x_loaded"], 16)
            sp.dma_start(h[0:DEC_SEQ, 2, :], ins["xs"]).then_inc(S["x_loaded"], 16)
            sp.dma_start(conv_st[:, :, :], ins["conv_st"]).then_inc(S["hist_loaded"], 16)

            def load_ring(src, groups, first, evac_base):
                for g in range(groups):
                    if g >= 3:
                        sp.wait_ge(S["proj_ps"], evac_base + 4 * (g - 2))
                    n = first + g
                    sp.dma_start(ring[g % 3].rearrange("p a b -> p (a b)"), src[g]).then_inc(S[f"ring{g % 3}"], 16)

            load_ring(ins["wA"], AB_GROUPS, 0, 0)
            sp.wait_ge(S["proj_ps"], AB_GROUPS * 4)
            sp.dma_start(s_load, ins["st_ssd"].rearrange("(c q) n -> q c n", q=P)).then_inc(S["state_in"], 16)
            sp.wait_ge(S["conv_new_ready"], 2)
            for j in range(2):
                sp.dma_start(outs["conv"][j], conv_new[:, j]).then_inc(S["states_out"], 16)
            for n, name in enumerate(("ssd_p", "ssd_s")):
                sp.wait_ge(S["ssd_final"], n + 1)
                sp.dma_start(outs[name].rearrange("(c q) n -> q c n", q=P), s_stage).then_inc(S["states_out"], 16)
            sp.wait_ge(S["nrm_done"], 3)
            sp.dma_start(GS[1], ins["st_gdn"].rearrange("h k v -> k h v")).then_inc(S["gdn_init"], 16)
            for n, name in enumerate(("gdn_p", "gdn_s")):
                sp.wait_ge(S["gdn_upd"], 2 + n)
                sp.dma_start(outs[name].rearrange("h k v -> k h v"), GS[n]).then_inc(S["states_out"], 16)
            sp.wait_ge(S["states_out"], 16 * 6)

            def load_out(src, groups, first):
                for g in range(groups):
                    if g >= 3:
                        sp.wait_ge(S["out_ps"], first + g - 2)
                    sp.dma_start(ring[g % 3].rearrange("p a b -> p (a b)").rearrange("p (c d) -> p c d", c=4),
                                 src[g * 4 * P:(g + 1) * 4 * P, :].rearrange("(c p) d -> p c d", p=P)
                                 ).then_inc(S[f"out_loaded{g % 3}"], 16)

            sp.wait_ge(S["cat_ready"], 1)
            load_out(ins["w_out_ab"], 4, 0)

            def load_expert(q, e, free, signals):
                for buf, w, name in ((wgb, wg_dram, "wg"), (wub, wu_dram, "wu"), (wdb, wd_dram, "wd")):
                    if free is not None:
                        sp.wait_ge(S[{"wg": "gate_ps", "wu": "up_ps", "wd": "y_ps"}[name]], free)
                    if name == "wd":
                        src, dst = w[bass.ds(e, 1)].rearrange("a p k f -> p (a k) f"), buf[q]
                    else:
                        src, dst = w[bass.ds(e, 1)].rearrange("a p f -> p (a f)"), buf[q].rearrange("p a b -> p (a b)")
                    sp.dma_start(dst, src).then_inc(signals[name], 16)

            def moe_loads(l):
                slots = [{n: S[f"{n}{q}"] for n in ("wg", "wu", "wd")} for q in range(2)]
                for q in range(2):
                    load_expert(q, l * EXPERTS + q, None, slots[q])
                with sp.Fori(1, PAIRS) as i:
                    for q in range(2):
                        load_expert(q, i * 2 + (l * EXPERTS + q), i * 2 + (l * EXPERTS + q - 1), slots[q])
                for q in range(2):
                    sp.wait_ge(S[f"scattered{q}"], 16 * PAIRS * (l + 1))
                sp.wait_ge(S["route_done"], l + 1)
                count = sp.value_load(extra_e[0:1, l, EXTRA:EXTRA + 1], min_val=0, max_val=EXTRA)
                X = extra_signals[l]
                for x in range(EXTRA):
                    with sp.If(count > x):
                        e = sp.value_load(extra_e[0:1, l, x:x + 1], min_val=0, max_val=2 * EXPERTS - 1)
                        load_expert(0, e, None, X)
                        sp.wait_ge(X["scattered"], 16 * (x + 1))
                for i in range(TILES):
                    for c in range(2):
                        sp.dma_start(YL[i][0:LEN[i], c, :],
                                     y2_dram.rearrange("(r g) d -> r (g d)", g=HALVES)[c * TOK + AT[i]:c * TOK + AT[i] + LEN[i], :]
                                     ).then_inc(S[f"y2_loaded{i}"], 16)

            def store_rows(l):
                for i in range(TILES):
                    sp.wait_ge(S["xn_ready"], (2 * l + 1) * TILES + i + 1)
                    sp.dma_start(xn_dram[AT[i]:AT[i] + LEN[i], :], xn[0:LEN[i], i, :]).then_inc(S["xn_stored"], 16)

            sp.wait_ge(S["h_ready"], TILES)
            store_rows(0)
            if stop > 1:
                moe_loads(0)
            if stop > 2:
                sp.wait_ge(S["h_ready"], 2 * TILES)
                load_ring(ins["wC"], C_GROUPS, AB_GROUPS, AB_GROUPS * 4)
                sp.wait_ge(S["proj_ps"], (AB_GROUPS + C_GROUPS) * 4)
                sp.dma_start(hS[1], ins["st_hgrn"].rearrange("h k v -> k h v")).then_inc(S["gdn_init"], 16)
                for n, name in enumerate(("hgrn_p", "hgrn_s")):
                    sp.wait_ge(S["hg_upd"], 2 + n)
                    sp.dma_start(outs[name].rearrange("h k v -> k h v"), hS[n]).then_inc(S["states_out"], 16)
                sp.wait_ge(S["states_out"], 16 * 8)
                sp.wait_ge(S["cat_ready"], 2)
                load_out(ins["w_out_c"], 2, 4)
                sp.wait_ge(S["h_ready"], 3 * TILES)
                store_rows(1)
                moe_loads(1)
                sp.dma_start(final_w, ins["final"].to_broadcast([P, D_MODEL])).then_inc(S["final_loaded"], 16)
                for i in range(TILES):
                    sp.wait_ge(S["xn_ready"], 4 * TILES + i + 1)
                    dst = outs["y_p"][AT[i]:AT[i] + P, :] if i < 2 else outs["y_s"]
                    sp.dma_start(dst, xn[0:LEN[i], i, :]).then_inc(S["y_out"], 16)
                sp.wait_ge(S["y_out"], 16 * TILES)

        @block.gpsimd
        def _(pool):
            for i in range(TILES):
                L = LEN[i]
                for n in range(sum(b < L for b in LEVELS)):
                    k = gdn_level(i, n)
                    pool.wait_ge(S["gdn_mats"], i + 1)
                    if k >= 2:
                        pool.wait_ge(S["gdn_pe"], 2 * (k - 1))
                    nc.gpsimd.tensor_tensor(Bm[k % 2][0:L, :, 0:L], DKK[0:L, :, 0:L],
                                            mask(n)[0:L, 0:L].unsqueeze(1).to_broadcast([L, 8, L]), ALU.mult
                                            ).then_inc(S["gdn_bm"], 1)
            if stop > 1:
                for l in range(2 if stop > 2 else 1):
                    pool.wait_ge(S["h_ready"], (2 * l + 1) * TILES)
                    nc.gpsimd.memset(xg[0], 0.0).then_inc(S["xg_zero"], 1)
                    nc.gpsimd.memset(xg[1], 0.0).then_inc(S["xg_zero"], 1)
                    pool.wait_ge(S["xg_zero"], 2 * l + 2)
                    pool.wait_ge(S["xn_stored"], 16 * TILES * (l + 1))
                    pool.wait_ge(S["route_done"], l + 1)

                    def gather(b, q, done):
                        nc.gpsimd.indirect_dma_start(
                            out=xg[q][0:SLOTS], out_offset=None, in_=xn_dram,
                            in_offset=bass.IndirectOffsetOnAxis(ap=gidx[0:SLOTS, b:b + 1], axis=0),
                            bounds_check=TOK - 1, oob_is_err=False).then_inc(done, 16)

                    def scatter(b, q, done):
                        nc.gpsimd.indirect_dma_start(
                            out=y2_dram, out_offset=bass.IndirectOffsetOnAxis(ap=sidx[:, b:b + 1], axis=0),
                            in_=yb[q], in_offset=None,
                            bounds_check=2 * TOK * HALVES - 1, oob_is_err=False).then_inc(done, 16)

                    gather(0, 0, S["xgathered0"])
                    gather(1, 1, S["xgathered1"])
                    for b in range(EXPERTS):
                        if b + 2 <= EXPERTS:
                            pool.wait_ge(S["xg_T"], l * (EXPERTS + 1) + b + 1)
                            gather(b + 2, b % 2, S[f"xgathered{b % 2}"])
                        pool.wait_ge(S["y_ready"], l * EXPERTS + b + 1)
                        scatter(b, b % 2, S[f"scattered{b % 2}"])
                    X = extra_signals[l]
                    count = pool.value_load(extra_e[0:1, l, EXTRA:EXTRA + 1], min_val=0, max_val=EXTRA)
                    for x in range(EXTRA):
                        with pool.If(count > x):
                            if x == 0:
                                pool.wait_ge(S["xg_T"], (l + 1) * (EXPERTS + 1))
                            gather(EXPERTS + x, 0, X["xgathered"])
                            pool.wait_ge(X["y_ready"], x + 1)
                            scatter(EXPERTS + x, 0, X["scattered"])

        @block.scalar
        def _(act):
            na = [0]

            def a(ins_):
                na[0] += 1
                ins_.then_inc(S["act_step"], 1)
                act.wait_ge(S["act_step"], na[0])

            def inv_root(out, in_, scale, bias, done):
                a(nc.scalar.activation(out, in_, ACT.Ln, scale=scale, bias=bias))
                nc.scalar.activation(out, out, ACT.Exp, scale=-0.5).then_inc(S[done], 1)

            def squares(n):
                for i in range(TILES):
                    if n == 0:
                        act.wait_ge(S["x_loaded"], 32)
                    else:
                        act.wait_ge(S["h_ready"], (n - 1) * TILES + i + 1)
                    L = LEN[i]
                    a(nc.scalar.activation(xn[0:L, i, :], h[0:L, i, :], ACT.Square,
                                           accum_out=ss[0:L, n, i:i + 1]))
                    inv_root(rstd[0:L, n, i:i + 1], ss[0:L, n, i:i + 1], 1.0 / D_MODEL, eps[0:L], "sq_done")

            act.wait_ge(S["consts_loaded"], 80)
            squares(0)
            for t in range(CONV_TILES + Z_TILES):
                b = t % 4
                act.wait_ge(S["proj_ps"], t + 1)
                if t < CONV_TILES:
                    nc.scalar.activation(xpad[:, t, TAPS:TAPS + SEQ], ps[:, b, 0:SEQ], ACT.Copy)
                    nc.scalar.activation(xpad[:, t, SEQ + 2 * TAPS:XP], ps[:, b, SEQ:TOK], ACT.Copy
                                         ).then_inc(S["proj_evac"], 1)
                else:
                    nc.scalar.activation(Z[:, t - CONV_TILES, :], ps[:, b, 0:TOK], ACT.Silu
                                         ).then_inc(S["proj_evac"], 1)
                u = t - 2
                if 0 <= u < CONV_TILES:
                    act.wait_ge(S["conv_out"], u + 1)
                    nc.scalar.activation(XC[:, u, :], cvt[:, u % 2, :], ACT.Silu,
                                         bias=vec[:, V_BIAS + u:V_BIAS + u + 1]).then_inc(S["conv_act"], 1)
            act.wait_ge(S["small_evac"], 1)
            nc.scalar.activation(beta[:, :, :], sc[:, :, SCAL:SCAL + 8], ACT.Sigmoid).then_inc(S["beta_ready"], 1)
            nc.scalar.activation(spx[:, 1], spx[:, 0], ACT.Exp, scale=-1.0).then_inc(S["sp_exp1"], 1)
            nc.scalar.activation(eA[:, :], row[:, R_ALOG:R_ALOG + SCAL], ACT.Exp).then_inc(S["ea_ready"], 1)
            act.wait_ge(S["sp_pos"], 1)
            nc.scalar.activation(spx[:, 3], spx[:, 2], ACT.Ln).then_inc(S["sp_ln"], 1)
            for u in range(2 * TILES):
                i = u // 2
                L = LEN[i]
                GB = bank(0, 8, P, n=2)
                act.wait_ge(S["ssd_in"], u + 1)
                if u:
                    act.wait_ge(S["ssd_upd"], u)
                nc.scalar.activation(EG[:, :, 0:L], GB[:, :, 0:L], ACT.Exp)
                nc.scalar.activation(dec, GB[:, :, L - 1], ACT.Exp).then_inc(S["ssd_exp"], 1)
                act.wait_ge(S["ssd_diff"], 2 * u + 1)
                nc.scalar.activation(Dm[0:L, :, 0:L], Dm[0:L, :, 0:L], ACT.Exp).then_inc(S["ssd_exp"], 1)
                act.wait_ge(S["ssd_diff"], 2 * u + 2)
                nc.scalar.activation(tail[0:L], tail[0:L], ACT.Exp).then_inc(S["ssd_exp"], 1)
            act.wait_ge(S["yg_ready"], 1)
            nc.scalar.activation(uT[:, :, :], cat[:, 0:8, :], ACT.Square).then_inc(S["sq2_done"], 1)
            act.wait_ge(S["nrm_ps"], 1)
            inv_root(rs0[:, 0:2, 0:TOK], ps[:, 0:2, 0:TOK], 1.0 / 512, eps, "rs_done")
            for r in range(2):
                act.wait_ge(S["nrm_done"], r + 1)
                nc.scalar.activation(sq4, XC[:, 12 + 4 * r:16 + 4 * r, :], ACT.Square
                                     ).then_inc(S["sq2_done"], 1)
                act.wait_ge(S["nrm_ps"], 2 + r)
                inv_root(rs0, ps[:, 0:4, 0:XW], 1.0 if r else float(P), eps if r else con[:, C_EPSQ:C_EPSQ + 1], "rs_done")
            for i in range(TILES):
                L = LEN[i]
                GB = bank(0, 8, P, n=2)
                act.wait_ge(S["gdn_in"], i + 1)
                if i:
                    act.wait_ge(S["gdn_upd"], i)
                nc.scalar.activation(EG[:, :, 0:L], GB[:, :, 0:L], ACT.Exp)
                nc.scalar.activation(dec, GB[:, :, L - 1], ACT.Exp)
                nc.scalar.activation(ecum[0:L], cum[0:L, i, SSD_HEADS:SCAL], ACT.Exp).then_inc(S["gdn_exp"], 1)
                act.wait_ge(S["gdn_diff"], 2 * i + 1)
                nc.scalar.activation(Dm[0:L, :, 0:L], Dm[0:L, :, 0:L], ACT.Exp).then_inc(S["gdn_exp"], 1)
                act.wait_ge(S["gdn_diff"], 2 * i + 2)
                nc.scalar.activation(tail[0:L], tail[0:L], ACT.Exp).then_inc(S["gdn_exp"], 1)
                for n in range(sum(b < L for b in LEVELS)):
                    k = gdn_level(i, n)
                    for f in range(2):
                        act.wait_ge(S["gdn_pe"], 2 * k + f + 1)
                        if k:
                            act.wait_ge(S["gdn_pt"], 2 * k - 1 + f)
                        for j in range(4):
                            hd = 4 * f + j
                            e_ = nc.scalar.activation(P8[0:L, hd, 0:L], bank(4 + f, 4, P)[0:L, j, 0:L], ACT.Copy,
                                                      scale=beta[0:L, i, hd:hd + 1])
                        e_.then_inc(S["gdn_p"], 1)

            def head_roots(src, rs, ready, sq, nrm):
                act.wait_ge(S["yg_ready"], ready)
                nc.scalar.activation(uT[:, :, :], src, ACT.Square).then_inc(S["sq2_done"], 1)
                for r in range(2):
                    act.wait_ge(S["nrm_ps"], nrm + r)
                    if r:
                        act.wait_ge(S["nrm_done"], nrm)
                    inv_root(rs[:, :, 0:TOK], ps[:, 4 * r:4 * r + 4, 0:TOK], 1.0 / P, eps, "rs_done")

            head_roots(cat[:, 8:16, :], rs0, 2, 4, 4)

            def moe_act(l):
                squares(2 * l + 1)
                act.wait_ge(S["rt_diff"], 2 * l + 1)
                nc.scalar.activation(rt_ge, rt_ge, ACT.Exp).then_inc(S["rt_exp"], 1)
                act.wait_ge(S["rt_diff"], 2 * l + 2)
                nc.scalar.activation(rt_e2, rt_e2, ACT.Exp).then_inc(S["rt_exp"], 1)
                act.wait_ge(S["route_done"], l + 1)
                if stop <= 1:
                    return
                def work(N, q, b, before):
                    act.wait_ge(N["gate_ps"], b + 1)
                    if before:
                        need(act, N["hid_ready"], b)
                    nc.scalar.activation(sg, bank(2, D_EXP // HALVES), ACT.Silu).then_inc(N["sg_ready"], 1)
                    act.wait_ge(N["hT_ps"], b + 1)
                    if before:
                        need(act, N["y_ps"], b)
                    nc.scalar.activation(hidT, bank(4, KE // HALVES, P), ACT.Copy).then_inc(N["hidT_ready"], 1)

                def rows_out(N, q, b):
                    act.wait_ge(N["y_ps"], b + 1)
                    nc.scalar.activation(yb[q], bank(5 + q, 512), ACT.Copy).then_inc(N["y_ready"], 1)

                def blocks(i):
                    for q in range(2):
                        b = i * 2 + (l * EXPERTS + q)
                        work(S, q, b, True)
                        need(act, S[f"scattered{q}"], i * 16 + 16 * l * PAIRS)
                        rows_out(S, q, b)

                blocks(0)
                with act.Fori(1, PAIRS) as i:
                    blocks(i)
                X = extra_signals[l]
                count = act.value_load(extra_e[0:1, l, EXTRA:EXTRA + 1], min_val=0, max_val=EXTRA)
                for x in range(EXTRA):
                    with act.If(count > x):
                        if x == 0:
                            act.wait_ge(S["scattered0"], 16 * (l + 1) * PAIRS)
                        work(X, 0, x, False)
                        rows_out(X, 0, x)
                        act.wait_ge(X["scattered"], 16 * (x + 1))

            moe_act(0)
            if stop <= 2:
                return
            squares(2)
            base = CONV_TILES + Z_TILES
            for t in range(4 * HEADS):
                act.wait_ge(S["proj_ps"], base + t + 1)
                part, hd = t // HEADS, t % HEADS
                dst = (hq, hg, hv, hz)[part]
                fn = (ACT.Silu, ACT.Sigmoid, ACT.Copy, ACT.Silu)[part]
                nc.scalar.activation(dst[:, hd, :], ps[:, t % 4, 0:TOK], fn).then_inc(S["proj_evac"], 1)
            act.wait_ge(S["lb_in"], 1)
            nc.scalar.activation(lbv[:, 1:3, :], lbv[:, 1:3, :], ACT.Exp).then_inc(S["lb_e"], 1)
            act.wait_ge(S["lf_in"], 1)
            nc.scalar.activation(hg, hg, ACT.Ln).then_inc(S["lf_ready"], 1)
            n = 0
            for i in range(TILES):
                L = LEN[i]
                c0 = AT[i]
                for n in range(sum(b < L for b in LEVELS)):
                    k = gdn_level(i, n)
                    act.wait_ge(S["hg_d"], k + 1)
                    nc.scalar.activation(hD[k % 2][:, :, 0:L], hD[k % 2][:, :, 0:L], ACT.Exp).then_inc(S["hg_e"], 1)
                act.wait_ge(S["hg_x"], i + 1)
                nc.scalar.activation(hE[:, :, 0:L], hg[:, :, c0:c0 + L], ACT.Exp)
                nc.scalar.activation(hEq[:, :, 0:L], hEq[:, :, 0:L], ACT.Exp)
                nc.scalar.activation(hDec, hg[:, :, c0 + L - 1], ACT.Exp).then_inc(S["hg_ex"], 1)
            head_roots(hcat, rs1, 3, 5, 6)
            moe_act(1)
            squares(4)

        @block.vector
        def _(dve):
            nv = [0]

            def v(ins_):
                nv[0] += 1
                ins_.then_inc(S["dve_step"], 1)
                dve.wait_ge(S["dve_step"], nv[0])

            V = nc.vector

            def tt(out, a, b, op):
                return V.tensor_tensor(out, a, b, op)

            def bc(ap, *dims):
                return ap.to_broadcast([ap.shape[0], *dims])

            def norm(n):
                for i in range(TILES):
                    L = LEN[i]
                    r = rstd[0:L, n, i:i + 1]
                    dve.wait_ge(S["sq_done"], n * TILES + i + 1)
                    if n < 4:
                        V.tensor_scalar(xn[0:L, i, :], h[0:L, i, :], r, None, ALU.mult).then_inc(S["xn_ready"], 1)
                    else:
                        v(V.tensor_scalar(xn[0:L, i, :], h[0:L, i, :], r, None, ALU.mult))
                        dve.wait_ge(S["final_loaded"], 16)
                        tt(xn[0:L, i, :], xn[0:L, i, :], final_w[0:L], ALU.mult).then_inc(S["xn_ready"], 1)
                if n == 4:
                    return
                for i in range(TILES):
                    for c in range(2):
                        k = 2 * i + c
                        w = vec[:, V_NORM + KD * n + 4 * c:V_NORM + KD * n + 4 * c + 4]
                        dve.wait_ge(S["xnT_ps"], 6 * n + k + 1)
                        tt(uT[:, 4 * c:4 * c + 4, AT[i]:AT[i] + LEN[i]], bank(4 + k % 4, 4, P)[:, :, 0:LEN[i]],
                           bc(w.unsqueeze(2), 4, LEN[i]), ALU.mult).then_inc(S["uT_ready"], 1)

            v(V.memset(xpad[:, :, 0:TAPS], 0.0))
            v(V.memset(sc[:, :, :], 0.0))
            v(V.memset(cum[:, :, :], 0.0))
            v(V.memset(LG[:, :, :], 0.0))
            v(V.memset(R2, 0.0))
            dve.wait_ge(S["hist_loaded"], 16)
            v(V.tensor_copy(xpad[:, :, TAPS + SEQ:2 * TAPS + SEQ], conv_st[:, :, :]))
            dve.wait_ge(S["consts_loaded"], 80)
            norm(0)
            for t in range(CONV_TILES):
                wv = lambda j: vec[:, V_CONV + t * CONV_W + j:V_CONV + t * CONV_W + j + 1]
                out = cvt[:, t % 2, :]
                dve.wait_ge(S["proj_evac"], t + 1)
                if t >= 2:
                    dve.wait_ge(S["conv_act"], t - 1)
                v(V.tensor_scalar(out, xpad[:, t, 0:XW], wv(0), None, ALU.mult))
                for j in range(1, CONV_W):
                    op = V.scalar_tensor_tensor(out, xpad[:, t, j:j + XW], wv(j), out, ALU.mult, ALU.add)
                    if j < CONV_W - 1:
                        v(op)
                    else:
                        op.then_inc(S["conv_out"], 1)
            V.tensor_copy(conv_new[:, 0, :, :], xpad[:, :, SEQ:SEQ + TAPS]).then_inc(S["conv_new_ready"], 1)
            V.tensor_copy(conv_new[:, 1, :, :], xpad[:, :, XP - TAPS:XP]).then_inc(S["conv_new_ready"], 1)
            for i in range(TILES):
                dve.wait_ge(S["small_ps"], i + 1)
                v(V.tensor_copy(sc[0:LEN[i], i, :], ps[0:LEN[i], 4 + i, 0:32]))
            s24 = sc[:, :, 0:SCAL]
            v(tt(s24, s24, bc(row[:, R_BIAS:R_BIAS + SCAL].unsqueeze(1), TILES, SCAL), ALU.add))
            V.scalar_tensor_tensor(spx[:, 0], s24, -1.0, s24, ALU.mult, ALU.max).then_inc(S["small_evac"], 1)
            dve.wait_ge(S["sp_exp1"], 1)
            e_, w_, d_ = spx[:, 1], spx[:, 2], spx[:, 0]
            V.tensor_scalar(w_, e_, 1.0, None, ALU.add).then_inc(S["sp_pos"], 1)
            dve.wait_ge(S["sp_pos"], 1)
            v(V.tensor_scalar(d_, w_, -1.0, None, ALU.add))
            dve.wait_ge(S["sp_ln"], 1)
            v(tt(spx[:, 3], spx[:, 3], e_, ALU.mult))
            v(V.tensor_scalar(w_, d_, 0.0, None, ALU.is_equal))
            v(tt(e_, e_, w_, ALU.mult))
            v(V.tensor_scalar(d_, d_, 1.0e-30, None, ALU.max))
            v(V.reciprocal(d_, d_))
            v(tt(spx[:, 3], spx[:, 3], d_, ALU.mult))
            v(tt(spx[:, 3], spx[:, 3], e_, ALU.add))
            v(V.scalar_tensor_tensor(dtg[:, :, :], s24, 0.0, spx[:, 3], ALU.max, ALU.add))
            dve.wait_ge(S["ea_ready"], 1)
            V.scalar_tensor_tensor(G24[:, :, :], dtg[:, :, :], -1.0, bc(eA[:, :].unsqueeze(1), TILES, SCAL),
                                   ALU.mult, ALU.mult).then_inc(S["g_ready"], 1)
            dve.wait_ge(S["cum_ps"], 1)
            for i in range(TILES):
                v(V.tensor_copy(cum[0:LEN[i], i, :], ps[0:LEN[i], 3, i * 32:i * 32 + SCAL]))

            dve.wait_ge(S["state_in"], 16)
            for u in range(2 * TILES):
                i, g = u // 2, u % 2
                L, x0, c0 = LEN[i], AX[i], AT[i]
                st = HT[1 if i == 2 else 0]
                GB = bank(0, 8, P, n=2)
                cm = cum[0:L, i, 8 * g:8 * g + 8]
                if u == 4:
                    for c in range(2):
                        dve.wait_ge(S["st_T"], c + 1)
                        v(V.tensor_copy(HT[1][:, c, :], bank(6 + c, 512)))
                    V.engine_nop().then_inc(S["st_Tevac"], 1)
                dve.wait_ge(S["ssd_in"], u + 1)
                v(tt(Xdt[0:L], bank(5, 8, 64)[0:L], bc(dtg[0:L, i, 8 * g:8 * g + 8].unsqueeze(2), 8, 64), ALU.mult))
                v(V.tensor_copy(Btok[0:L], ps[0:L, 6, 0:P]))
                v(tt(BCm[0:L, 0:L], ps[0:L, 2, 0:L], triu[0:L, 0:L], ALU.mult))
                dve.wait_ge(S["ssd_exp"], 3 * u + 1)
                v(tt(Dm[0:L, :, 0:L], GB[0:L, :, 0:L], bc(cm.unsqueeze(2), 8, L), ALU.subtract))
                V.tensor_scalar(Dm[0:L, :, 0:L], Dm[0:L, :, 0:L], 0.0, None, ALU.min).then_inc(S["ssd_diff"], 1)
                tt(tail[0:L], GB[0:L, :, L - 1], cm, ALU.subtract).then_inc(S["ssd_diff"], 1)
                v(tt(Cs[:, :, 0:L], EG[:, :, 0:L], bc(XC[:, 10 + g, x0:x0 + L].unsqueeze(1), 8, L), ALU.mult))
                dve.wait_ge(S["ssd_exp"], 3 * u + 3)
                v(tt(W8[0:L, :, 0:L], Dm[0:L, :, 0:L], bc(BCm[0:L, 0:L].unsqueeze(1), 8, L), ALU.mult))
                tt(Xtl[0:L], Xdt[0:L], bc(tail[0:L].unsqueeze(2), 8, 64), ALU.mult).then_inc(S["ssd_w"], 1)
                dve.wait_ge(S["ssd_y"], u + 1)
                for c in range(4):
                    k = 4 * g + c
                    v(V.scalar_tensor_tensor(cat[:, k, c0:c0 + L], XC[:, k, x0:x0 + L], vec[:, V_D + k:V_D + k + 1],
                                             bank(3, 4, P)[:, c, 0:L], ALU.mult, ALU.add))
                if i == 0:
                    V.tensor_copy(st[:, g, :], bank(4, 512)).then_inc(S["ssd_upd"], 1)
                else:
                    s8 = st[:, g, :].rearrange("p (a b) -> p a b", a=8)
                    v(tt(s8, s8, bc(dec.unsqueeze(2), 8, 64), ALU.mult))
                    tt(st[:, g, :], st[:, g, :], bank(4, 512), ALU.add).then_inc(S["ssd_upd"], 1)
            for n in range(2):
                if n:
                    dve.wait_ge(S["states_out"], 48)
                for c in range(2):
                    dve.wait_ge(S["st_T"], 2 + 2 * n + c + 1)
                    k = V.tensor_copy(s_stage[:, 4 * c:4 * c + 4, :], bank(6 + c, 4, P))
                    if c == 0:
                        v(k)
                    else:
                        k.then_inc(S["ssd_final"], 1)
            tt(cat[:, 0:8, :], cat[:, 0:8, :], Z[:, 0:8, :], ALU.mult).then_inc(S["yg_ready"], 1)
            dve.wait_ge(S["rs_done"], 1)
            c4 = cat[:, 0:8, :].rearrange("p (g c) t -> p g c t", g=2)
            v(tt(c4, c4, bc(rs0[:, 0:2, 0:TOK].unsqueeze(2), 2, 4, TOK), ALU.mult))
            tt(cat[:, 0:8, :], cat[:, 0:8, :], bc(vec[:, V_SNORM:V_SNORM + 8].unsqueeze(2), 8, TOK), ALU.mult
               ).then_inc(S["nrm_done"], 1)
            for r in range(2):
                dve.wait_ge(S["rs_done"], 2 + r)
                x4 = XC[:, 12 + 4 * r:16 + 4 * r, :]
                tt(x4, x4, rs0, ALU.mult).then_inc(S["nrm_done"], 1)

            for i in range(TILES):
                L, x0, c0 = LEN[i], AX[i], AT[i]
                st = GS[1 if i == 2 else 0]
                GB = bank(0, 8, P, n=2)
                cm = cum[0:L, i, SSD_HEADS:SCAL]
                bt = bc(beta[0:L, i, :].unsqueeze(2), 8, P)
                btL = bc(beta[0:L, i, :].unsqueeze(2), 8, L)
                dve.wait_ge(S["gdn_in"], i + 1)
                dve.wait_ge(S["gdn_exp"], 3 * i + 1)
                v(tt(Dm[0:L, :, 0:L], GB[0:L, :, 0:L], bc(cm.unsqueeze(2), 8, L), ALU.subtract))
                V.tensor_scalar(Dm[0:L, :, 0:L], Dm[0:L, :, 0:L], 0.0, None, ALU.min).then_inc(S["gdn_diff"], 1)
                tt(tail[0:L], GB[0:L, :, L - 1], cm, ALU.subtract).then_inc(S["gdn_diff"], 1)
                if i == 0:
                    dve.wait_ge(S["beta_ready"], 1)
                v(tt(VB[0:L], bank(4, 8, P, n=2)[0:L], bt, ALU.mult))
                v(V.tensor_copy(Ktok[0:L], bank(6, 4, P)[0:L]))
                v(V.tensor_copy(T8[0:L, :, 0:L], bc(ident[0:L, 0:L].unsqueeze(1), 8, L)))
                v(V.tensor_copy(TT8[0:L, :, 0:L], bc(ident[0:L, 0:L].unsqueeze(1), 8, L)))
                dve.wait_ge(S["gdn_exp"], 3 * i + 1)
                v(V.scalar_tensor_tensor(nbe[0:L], beta[0:L, i, :], -1.0, ecum[0:L], ALU.mult, ALU.mult))
                q4 = XC[:, 12:16, x0:x0 + L]
                for hd in range(4):
                    v(tt(qs[:, 2 * hd:2 * hd + 2, 0:L], EG[:, 2 * hd:2 * hd + 2, 0:L],
                         bc(q4[:, hd, :].unsqueeze(1), 2, L), ALU.mult))
                dve.wait_ge(S["gdn_exp"], 3 * i + 3)
                v(tt(Dm[0:L, :, 0:L], Dm[0:L, :, 0:L], bc(triu[0:L, 0:L].unsqueeze(1), 8, L), ALU.mult))
                pair = lambda ap: ap.rearrange("p (a b) c -> p a b c", b=2)
                v(tt(pair(DQK[0:L])[:, :, :, 0:L], pair(Dm[0:L])[:, :, :, 0:L],
                     bc(bank(3, 4, P)[0:L, :, 0:L].unsqueeze(2), 4, 2, L), ALU.mult))
                v(tt(pair(DKK[0:L])[:, :, :, 0:L], pair(Dm[0:L])[:, :, :, 0:L],
                     bc(bank(2, 4, P)[0:L, :, 0:L].unsqueeze(2), 4, 2, L), ALU.mult))
                v(tt(pair(Kt[0:L]), bc(Ktok[0:L].unsqueeze(2), 4, 2, P),
                     bc(tail[0:L].rearrange("p (a b) -> p a b", b=2).unsqueeze(3), 4, 2, P), ALU.mult))
                V.engine_nop().then_inc(S["gdn_mats"], 1)
                lv = [n for n, b in enumerate(LEVELS) if b < L]
                for n in range(len(lv)):
                    k = gdn_level(i, n)
                    for f in range(2):
                        hh = slice(4 * f, 4 * f + 4)
                        dve.wait_ge(S["gdn_pt"], 2 * k + f + 1)
                        if n < len(lv) - 1:
                            tt(T8[0:L, hh, 0:L], T8[0:L, hh, 0:L], bank(6 + f, 4, P)[0:L, :, 0:L], ALU.subtract)
                        tt(TT8[0:L, hh, 0:L], TT8[0:L, hh, 0:L], bank(f, 4, P)[0:L, :, 0:L], ALU.subtract
                           ).then_inc(S["gdn_tu"], 1)
                k = gdn_level(i, len(lv))
                dve.wait_ge(S["gdn_pt"], 2 * k)
                if i > 0:
                    dve.wait_ge(S["gdn_ks"], i)
                    v(tt(RHS[0:L], bank(4, 8, P, n=2)[0:L], bc(nbe[0:L].unsqueeze(2), 8, P), ALU.mult))
                    tt(RHS[0:L], RHS[0:L], VB[0:L], ALU.add).then_inc(S["gdn_rhs"], 1)
                else:
                    V.tensor_copy(RHS[0:L], VB[0:L]).then_inc(S["gdn_rhs"], 1)
                dve.wait_ge(S["gdn_u"], i + 1)
                V.tensor_copy(U8[0:L], bank(6, 8, P, n=2)[0:L]).then_inc(S["gdn_ue"], 1)
                dve.wait_ge(S["gdn_o"], i + 1)
                v(V.tensor_copy(cat[:, 8:16, c0:c0 + L], bank(2, 8, P, n=2)[:, :, 0:L]))
                if i == 0:
                    V.tensor_copy(st, bank(4, 8, P, n=2)).then_inc(S["gdn_upd"], 1)
                else:
                    v(tt(st, st, bc(dec.unsqueeze(2), 8, P), ALU.mult))
                    tt(st, st, bank(4, 8, P, n=2), ALU.add).then_inc(S["gdn_upd"], 1)

            def head_norm(x, z, rs, w, ready, nrm):
                V.engine_nop().then_inc(S["yg_ready"], 1)
                for r in range(2):
                    dve.wait_ge(S["rs_done"], nrm + r)
                    tt(x[:, 4 * r:4 * r + 4, :], x[:, 4 * r:4 * r + 4, :], rs[:, :, 0:TOK], ALU.mult
                       ).then_inc(S["nrm_done"], 1)
                dve.wait_ge(S["nrm_done"], nrm + 1)
                V.scalar_tensor_tensor(flat(x), flat(x), w, flat(z), ALU.mult, ALU.mult).then_inc(S["cat_ready"], 1)

            def flat(ap):
                return ap.rearrange("p a b -> p (a b)")

            head_norm(cat[:, 8:16, :], Z[:, 8:16, :], rs0, vec[:, V_GNORM:V_GNORM + 1], 2, 4)

            def residual(groups, n):
                dve.wait_ge(S["out_ps"], groups)
                for i in range(2):
                    tt(h[:, i, :], h[:, i, :], bank(2 * i, D_MODEL, n=2), ALU.add).then_inc(S["h_ready"], 1)
                for j in range(4):
                    t_ = tt(h[0:DEC_SEQ, 2, 256 * j:256 * j + 256], h[0:DEC_SEQ, 2, 256 * j:256 * j + 256],
                            ps[32 * j:32 * j + 32, 4, 0:256], ALU.add)
                t_.then_inc(S["h_ready"], 1)

            residual(4, 0)

            def route(l):
                B = lambda ap, *d: bc(ap, *d)
                dve.wait_ge(S["lg_ps"], l + 1)
                for i in range(TILES):
                    v(V.tensor_copy(LG[0:LEN[i], i, :], ps[0:LEN[i], 0, i * 64:i * 64 + 36]))
                v(V.memset(gl8, -3.0e38))
                v(V.tensor_copy(gl8[:, :, 0:4], LG[:, :, 0:4]))
                for i in range(TILES):
                    v(V.max(gm8[:, i, :], gl8[:, i, :]))
                    v(V.max_index(gi8[:, i, :], gm8[:, i, :], gl8[:, i, :]))
                v(V.tensor_copy(gif, gi8[:, :, 0:1]))
                tt(rt_ge, LG[:, :, 0:4], B(gm8[:, :, 0:1], 3, 4), ALU.subtract).then_inc(S["rt_diff"], 1)
                v(tt(ohg, B(iota[:, 0:4].unsqueeze(1), 3, 4), B(gif, 3, 4), ALU.is_equal))
                s4 = selm.rearrange("p i (g j) -> p i g j", g=4)
                v(tt(s4, LG[:, :, 4:36].rearrange("p i (g j) -> p i g j", g=4), B(ohg.unsqueeze(3), 3, 4, 8), ALU.mult))
                v(V.tensor_reduce(esel, selm.rearrange("p i (g j) -> p i j g", g=4), AX_X, ALU.add))
                for i in range(TILES):
                    v(V.max(ev8[:, i, :], esel[:, i, :]))
                    v(V.max_index(ei8[:, i, :], ev8[:, i, :], esel[:, i, :]))
                v(V.tensor_copy(eif, ei8[:, :, 0:2]))
                tt(rt_e2, ev8[:, :, 1:2], ev8[:, :, 0:1], ALU.subtract).then_inc(S["rt_diff"], 1)
                v(V.tensor_scalar(sgm, gif, float(E_PER), None, ALU.mult))
                v(tt(eid, eif, B(sgm, 3, 2), ALU.add))
                v(tt(O2, B(iota[:, 0:32].unsqueeze(1).unsqueeze(1), 3, 2, 32), B(eid.unsqueeze(3), 3, 2, 32), ALU.is_equal))
                tt(A2, O2[:, :, 0, :], O2[:, :, 1, :], ALU.add).then_inc(S["rt_A"], 1)
                dve.wait_ge(S["rt_exp"], 2 * l + 2)
                v(V.tensor_reduce(sgm, rt_ge, AX_X, ALU.add))
                v(V.tensor_scalar(den, rt_e2, 1.0, None, ALU.add))
                v(tt(den, den, sgm, ALU.mult))
                v(V.reciprocal(gates[:, :, 0:1], den))
                v(tt(gates[:, :, 1:2], gates[:, :, 0:1], rt_e2, ALU.mult))
                dve.wait_ge(S["rt_R"], l + 1)
                for i in range(TILES):
                    v(V.tensor_copy(R2[0:LEN[i], i, :], ps[0:LEN[i], 1, i * 32:i * 32 + 32]))
                v(V.tensor_copy(cnt, ps[:, 1, 96:128]))
                v(V.tensor_scalar(nx, cnt, float(SLOTS), None, ALU.is_gt))
                for full in range(2 * SLOTS, TOK, SLOTS):
                    v(V.scalar_tensor_tensor(nx, cnt, float(full), nx, ALU.is_gt, ALU.add))
                v(V.tensor_tensor_scan(incl, ones[:, 0:32], nx, 0.0, ALU.mult, ALU.add))
                v(tt(exb, incl, nx, ALU.subtract))
                v(V.tensor_scalar(over, R2, float(SLOTS) - 0.5, None, ALU.is_gt))
                v(V.tensor_scalar(exb, exb, float(SLOTS), float(SLOTS * (EXPERTS - 1)), ALU.mult, ALU.add))
                v(V.tensor_scalar(cnt, iota[:, 0:32], float(SLOTS), None, ALU.mult))
                v(tt(exb, exb, cnt, ALU.subtract))
                v(tt(extb, over, B(exb.unsqueeze(1), 3, 32), ALU.mult))
                v(tt(R2, R2, extb, ALU.add))
                v(tt(R2, R2, B(cnt.unsqueeze(1), 3, 32), ALU.add))
                v(tt(OD, O2, B(R2.unsqueeze(2), 3, 2, 32), ALU.mult))
                v(V.tensor_reduce(pos.rearrange("p (a b) -> p a b", a=3), OD, AX_X, ALU.add))
                v(V.tensor_copy(posi[:, 0, :], pos))
                v(V.tensor_scalar(posi[:, 1, :], posi[:, 0, :], SLOTS - 1, None, ALU.bitwise_and))
                v(V.tensor_scalar(posi[:, 2, :], posi[:, 0, :], SHIFT, None, ALU.logical_shift_right))
                v(V.tensor_copy(p1f, posi[:, 1, :]))
                v(V.tensor_copy(b1f, posi[:, 2, :]))
                for k in range(6):
                    v(V.tensor_scalar(OPm[:, k, :], con[:, C_SLOT:C_SLOT + P], p1f[:, k:k + 1], None, ALU.is_equal))
                    ob = V.tensor_scalar(OBm[:, k, :], iota[:, 0:COLS], b1f[:, k:k + 1],
                                         con[:, C_VAL + k:C_VAL + k + 1], ALU.is_equal, ALU.mult)
                    if k < 5:
                        v(ob)
                    else:
                        ob.then_inc(S["rt_OH"], 1)
                v(tt(cmp[0:1], B(incl[0:1].unsqueeze(1), EXTRA, 32), B(iota[0:1, 0:EXTRA].unsqueeze(2), EXTRA, 32), ALU.is_le))
                v(V.tensor_reduce(xe[0:1, 0:EXTRA], cmp[0:1], AX_X, ALU.add))
                v(V.tensor_scalar(xe[0:1, 0:EXTRA], xe[0:1, 0:EXTRA], float(EXPERTS - 1), float(l * EXPERTS),
                                  ALU.min, ALU.add))
                v(V.tensor_copy(xe[0:1, EXTRA:EXTRA + 1], incl[0:1, 31:32]))
                v(V.tensor_copy(extra_e[0:1, l, :], xe[0:1]))
                dve.wait_ge(S["rt_tab"], l + 1)
                v(V.tensor_copy(tb, ps[:, 2, 0:COLS]))
                v(V.tensor_scalar(inv, tb, 0.5, NOWHERE, ALU.is_lt, ALU.mult))
                v(V.tensor_scalar(jj, tb, -1.0, None, ALU.add))
                v(V.tensor_scalar(c2, jj, float(TOK) - 0.5, float(TOK), ALU.is_gt, ALU.mult))
                v(tt(jj, jj, inv, ALU.add))
                v(V.tensor_scalar(tb, jj, float(HALVES), con[:, C_HALF:C_HALF + 1], ALU.mult, ALU.add))
                v(V.tensor_copy(sidx[:, :], tb))
                v(tt(jj, jj, c2, ALU.subtract))
                V.tensor_copy(gidx[:, :], jj).then_inc(S["route_done"], 1)

            def moe_dve(l):
                if l:
                    v(V.memset(R2, 0.0))
                route(l)
                if stop <= 1:
                    return
                nw = vec[:, V_NORM + KD * (2 * l + 1):V_NORM + KD * (2 * l + 2)]

                def xT_evac(N, q, n):
                    dve.wait_ge(N["xg_T"], n + 1)
                    tt(xT[q], bank(q, KD, SLOTS), bc(nw.unsqueeze(2), KD, SLOTS), ALU.mult).then_inc(N["xT_ready"], 1)

                def gated(N, b):
                    dve.wait_ge(N["up_ps"], b + 1)
                    dve.wait_ge(N["sg_ready"], b + 1)
                    tt(hid, sg, bank(3, D_EXP // HALVES), ALU.mult).then_inc(N["hid_ready"], 1)

                def blocks(i):
                    for q in range(2):
                        b = i * 2 + (l * EXPERTS + q)
                        need(dve, S["hT_ps"], b)
                        gated(S, b)
                        xT_evac(S, 1 - q, i * 2 + (l * (EXPERTS + 1) + q + 1))

                xT_evac(S, 0, l * (EXPERTS + 1))
                blocks(0)
                with dve.Fori(1, PAIRS) as i:
                    blocks(i)
                X = extra_signals[l]
                count = dve.value_load(extra_e[0:1, l, EXTRA:EXTRA + 1], min_val=0, max_val=EXTRA)
                for x in range(EXTRA):
                    with dve.If(count > x):
                        if x == 0:
                            dve.wait_ge(S["hT_ps"], (l + 1) * EXPERTS)
                        xT_evac(X, 0, x)
                        gated(X, x)
                        dve.wait_ge(X["hT_ps"], x + 1)
                for i in range(TILES):
                    L = LEN[i]
                    dve.wait_ge(S[f"y2_loaded{i}"], 32 * (l + 1))
                    v(V.scalar_tensor_tensor(h[0:L, i, :], YL[i][0:L, 0, :], gates[0:L, i, 0:1], h[0:L, i, :],
                                             ALU.mult, ALU.add))
                    V.scalar_tensor_tensor(h[0:L, i, :], YL[i][0:L, 1, :], gates[0:L, i, 1:2], h[0:L, i, :],
                                           ALU.mult, ALU.add).then_inc(S["h_ready"], 1)

            norm(1)
            moe_dve(0)
            if stop <= 2:
                return

            norm(2)
            lg = vec[:, V_LB:V_LB + 16].rearrange("p (a b) -> p a b", a=2)
            v(tt(lbv[:, 0, :], lg[:, 0], lg[:, 1], ALU.max))
            tt(lbv[:, 1:3, :], lg, bc(lbv[:, 0:1, :], 2, HEADS), ALU.subtract).then_inc(S["lb_in"], 1)
            dve.wait_ge(S["lb_e"], 1)
            v(tt(lbv[:, 3, :], lbv[:, 1, :], lbv[:, 2, :], ALU.add))
            v(V.reciprocal(lbv[:, 3, :], lbv[:, 3, :]))
            v(tt(lbv[:, 1:3, :], lbv[:, 1:3, :], bc(lbv[:, 3:4, :], 2, HEADS), ALU.mult))
            v(tt(lbv[:, 4, :], lbv[:, 1, :], lbv[:, 2, :], ALU.add))
            v(tt(lbv[:, 4, :], lbv[:, 4, :], lbv[:, 1, :], ALU.subtract))
            v(V.tensor_scalar(lbv[:, 5, :], lbv[:, 4, :], -1.0, 1.0, ALU.mult, ALU.add))
            dve.wait_ge(S["proj_evac"], CONV_TILES + Z_TILES + 2 * HEADS)
            v(tt(hg, hg, bc(lbv[:, 5, :].unsqueeze(2), HEADS, TOK), ALU.mult))
            v(tt(hg, hg, bc(lbv[:, 4, :].unsqueeze(2), HEADS, TOK), ALU.add))
            V.tensor_scalar(hk, hg, -1.0, 1.0, ALU.mult, ALU.add).then_inc(S["lf_in"], 1)
            dve.wait_ge(S["lf_ready"], 1)
            for hd in range(HEADS):
                v(V.tensor_tensor_scan(hg[:, hd, :], con[:, C_SCAN:C_SCAN + TOK], hg[:, hd, :], 0.0,
                                       ALU.mult, ALU.add))
            dve.wait_ge(S["proj_evac"], CONV_TILES + Z_TILES + 4 * HEADS)
            for i in range(TILES):
                L, c0 = LEN[i], AT[i]
                st = hS[1 if i == 2 else 0]
                if i == 2:
                    dve.wait_ge(S["gdn_init"], 32)
                if i:
                    dve.wait_ge(S["hg_upd"], i)
                v(V.memset(hA, 0.0))
                lv = [n for n, b in enumerate(LEVELS) if b < L]

                def halves(ap, b):
                    w_ = ap.rearrange("p a (n c) -> p a n c", c=2 * b)
                    return w_[:, :, :, 0:b], w_[:, :, :, b:2 * b]

                def to_middle(n):
                    b, k = LEVELS[n], gdn_level(i, n)
                    (glo, ghi), (lo, hi) = halves(hg[:, :, c0:c0 + L], b), halves(hD[k % 2][:, :, 0:L], b)
                    mid = bc(glo[:, :, :, b - 1:b], 8, L // (2 * b), b)
                    need(dve, S["hg_qk"], k - 1)
                    tt(lo, mid, glo, ALU.subtract)
                    tt(hi, ghi, mid, ALU.subtract).then_inc(S["hg_d"], 1)

                def scaled(n):
                    b, k = LEVELS[n], gdn_level(i, n)
                    dve.wait_ge(S["hg_e"], k + 1)
                    (klo, _), (_, qhi) = halves(hk[:, :, c0:c0 + L], b), halves(hq[:, :, c0:c0 + L], b)
                    (dlo, dhi), (rlo, rhi) = halves(hD[k % 2][:, :, 0:L], b), halves(hR[k % 2][:, :, 0:L], b)
                    tt(rlo, klo, dlo, ALU.mult)
                    tt(rhi, qhi, dhi, ALU.mult).then_inc(S["hg_qk"], 1)

                def keep(n):
                    m = gdn_level(i, n) + i
                    msk = ident if n == 0 else mask(n - 1)
                    dve.wait_ge(S["hg_att"], m + 1)
                    need(dve, S["hg_keep"], m)
                    V.copy_predicated(hA[0:L, :, 0:L], bc(msk[0:L, 0:L].bitcast(U32).unsqueeze(1), 8, L),
                                      bank(2 * (m % 2), 8, P, n=2)[0:L, :, 0:L]).then_inc(S["hg_keep"], 1)

                to_middle(0)
                for n in range(len(lv)):
                    if n + 1 < len(lv):
                        to_middle(n + 1)
                    scaled(n)
                    keep(n)
                keep(len(lv))
                dve.wait_ge(S["hg_keep"], gdn_level(i, len(lv)) + i + 1)
                tt(hEq[:, :, 0:L], bc(hg[:, :, c0 + L - 1:c0 + L], 8, L), hg[:, :, c0:c0 + L], ALU.subtract
                   ).then_inc(S["hg_x"], 1)
                dve.wait_ge(S["hg_ex"], i + 1)
                v(tt(hQ[:, :, 0:L], hq[:, :, c0:c0 + L], hE[:, :, 0:L], ALU.mult))
                tt(hK[:, :, 0:L], hk[:, :, c0:c0 + L], hEq[:, :, 0:L], ALU.mult).then_inc(S["hg_in"], 1)
                dve.wait_ge(S["hg_tr"], i + 1)
                v(V.tensor_copy(hKt[0:L], bank(2, 8, P, n=2)[0:L]))
                V.tensor_copy(hVt[0:L], bank(4, 8, P, n=2)[0:L]).then_inc(S["hg_acc"], 1)
                dve.wait_ge(S["hg_y"], i + 1)
                v(V.tensor_copy(hcat[:, :, c0:c0 + L], bank(6, 8, P, n=2)[:, :, 0:L]))
                if i == 0:
                    V.tensor_copy(st, bank(0, 8, P, n=2)).then_inc(S["hg_upd"], 1)
                else:
                    v(tt(st, st, bc(hDec.unsqueeze(2), 8, P), ALU.mult))
                    tt(st, st, bank(0, 8, P, n=2), ALU.add).then_inc(S["hg_upd"], 1)
            dve.wait_ge(S["hg_upd"], TILES)
            head_norm(hcat, hz, rs1, vec[:, V_HNORM:V_HNORM + 1], 3, 6)
            residual(6, 2)
            norm(3)
            moe_dve(1)
            norm(4)

        @block.tensor
        def _(pe):
            MM = nc.tensor.matmul

            def norm(n):
                for i in range(TILES):
                    pe.wait_ge(S["xn_ready"], n * TILES + i + 1)
                    L = LEN[i]
                    for c in range(2):
                        k = 2 * i + c
                        if k >= 4:
                            pe.wait_ge(S["uT_ready"], 6 * n + k - 3)
                        for j in range(4):
                            t_ = nc.tensor.transpose(bank(4 + k % 4, 4, P)[:, j, 0:L],
                                                     xn[0:L, i, 4 * c + j::KD], ident[0:L, 0:L])
                        t_.then_inc(S["xnT_ps"], 1)

            def project(tiles, first, group):
                for t in range(tiles):
                    s = (t // 4) % 3
                    if t % 4 == 0:
                        pe.wait_ge(S[f"ring{s}"], 16 * (ring_use(group, t // 4)))
                    if t >= 4:
                        pe.wait_ge(S["proj_evac"], first + t - 3)
                    for k in range(KD):
                        m_ = MM(ps[:, t % 4, 0:TOK], ring[s][:, k, (t % 4) * P:(t % 4 + 1) * P], uT[:, k, :],
                                start=(k == 0), stop=(k == KD - 1))
                    m_.then_inc(S["proj_ps"], 1)

            def decays(i, h0):
                L = LEN[i]
                for hd in range(8):
                    m_ = MM(bank(0, 8, P, n=2)[:, hd, 0:L], G24[0:L, i, h0 + hd:h0 + hd + 1].to_broadcast([L, P]),
                            triu[0:L, 0:L], start=True, stop=True)
                return m_

            pe.wait_ge(S["consts_loaded"], 80)
            norm(0)
            pe.wait_ge(S["uT_ready"], 6)
            project(CONV_TILES + Z_TILES, 0, 0)
            for i in range(TILES):
                for k in range(KD):
                    m_ = MM(ps[0:LEN[i], 4 + i, 0:32], uT[:, k, AT[i]:AT[i] + LEN[i]], wsm[:, k, :],
                            start=(k == 0), stop=(k == KD - 1))
                m_.then_inc(S["small_ps"], 1)
            pe.wait_ge(S["g_ready"], 1)
            pe.wait_ge(S["proj_evac"], CONV_TILES + Z_TILES)
            for i in range(TILES):
                m_ = MM(ps[0:LEN[i], 3, i * 32:i * 32 + SCAL], triu[0:LEN[i], 0:LEN[i]], G24[0:LEN[i], i, :],
                        start=True, stop=True)
            m_.then_inc(S["cum_ps"], 1)
            pe.wait_ge(S["conv_act"], CONV_TILES)
            for u in range(2 * TILES):
                i, g = u // 2, u % 2
                L, x0 = LEN[i], AX[i]
                st = HT[1 if i == 2 else 0]
                if u:
                    pe.wait_ge(S["ssd_exp"], 3 * u)
                if u == 4:
                    pe.wait_ge(S["state_in"], 16)
                    for c in range(2):
                        for j in range(4):
                            t_ = nc.tensor.transpose(bank(6 + c, 4, P)[:, j, :], s_load[:, 4 * c + j, :], ident)
                        t_.then_inc(S["st_T"], 1)
                    pe.wait_ge(S["st_Tevac"], 1)
                decays(i, 8 * g)
                for c in range(4):
                    nc.tensor.transpose(bank(5, 4, P)[0:L, c, :], XC[:, 4 * g + c, x0:x0 + L], ident)
                nc.tensor.transpose(ps[0:L, 6, 0:P], XC[:, 8 + g, x0:x0 + L], ident)
                MM(ps[0:L, 2, 0:L], XC[:, 8 + g, x0:x0 + L], XC[:, 10 + g, x0:x0 + L], start=True, stop=True
                   ).then_inc(S["ssd_in"], 1)
                pe.wait_ge(S["ssd_w"], u + 1)
                if u:
                    pe.wait_ge(S["ssd_upd"], u)
                for hd in range(8):
                    lo = 64 * (hd % 2)
                    out = bank(3, 4, P)[lo:lo + 64, hd // 2, 0:L]
                    MM(out, Xdt[0:L, hd, :], W8[0:L, hd, 0:L], start=True, stop=(i == 0))
                    if i:
                        MM(out, st[:, g, 64 * hd:64 * hd + 64], Cs[:, hd, 0:L], start=False, stop=True)
                MM(bank(4, 512), Btok[0:L], Xtl[0:L].rearrange("p a b -> p (a b)"), start=True, stop=True
                   ).then_inc(S["ssd_y"], 1)
            pe.wait_ge(S["ssd_upd"], 2 * TILES)
            for n in range(2):
                for c in range(2):
                    if n:
                        pe.wait_ge(S["ssd_final"], n)
                    for j in range(4):
                        t_ = nc.tensor.transpose(bank(6 + c, 4, P)[:, j, :], HT[n][:, c, P * j:P * j + P], ident)
                    t_.then_inc(S["st_T"], 1)
            pe.wait_ge(S["sq2_done"], 1)
            for g in range(2):
                for c in range(4):
                    m_ = MM(ps[:, g, 0:TOK], ones, uT[:, 4 * g + c, :], start=(c == 0), stop=(c == 3))
            m_.then_inc(S["nrm_ps"], 1)
            for r in range(2):
                pe.wait_ge(S["sq2_done"], 2 + r)
                for c in range(4):
                    m_ = MM(ps[:, c, 0:XW], ones, sq4[:, c, :], start=True, stop=True)
                m_.then_inc(S["nrm_ps"], 1)
            pe.wait_ge(S["nrm_done"], 3)
            for i in range(TILES):
                L, x0 = LEN[i], AX[i]
                st = GS[1 if i == 2 else 0]
                if i:
                    pe.wait_ge(S["gdn_upd"], i)
                decays(i, SSD_HEADS)
                for j in range(4):
                    kk = XC[:, 16 + j, x0:x0 + L]
                    MM(bank(2, 4, P)[0:L, j, 0:L], kk, kk, start=True, stop=True)
                    MM(bank(3, 4, P)[0:L, j, 0:L], kk, XC[:, 12 + j, x0:x0 + L], start=True, stop=True)
                    nc.tensor.transpose(bank(6, 4, P)[0:L, j, :], kk, ident)
                for hd in range(8):
                    t_ = nc.tensor.transpose(bank(4, 8, P, n=2)[0:L, hd, :], XC[:, 20 + hd, x0:x0 + L], ident)
                t_.then_inc(S["gdn_in"], 1)
                lv = [n for n, b in enumerate(LEVELS) if b < L]
                for n in range(len(lv)):
                    k = gdn_level(i, n)
                    pe.wait_ge(S["gdn_bm"], k + 1)
                    for f in range(2):
                        if k:
                            pe.wait_ge(S["gdn_tu"], 2 * k - 1 + f)
                        for j in range(4):
                            hd = 4 * f + j
                            m_ = MM(bank(4 + f, 4, P)[0:L, j, 0:L], Bm[k % 2][0:L, hd, 0:L], T8[0:L, hd, 0:L],
                                    start=True, stop=True)
                        m_.then_inc(S["gdn_pe"], 1)
                    for f in range(2):
                        pe.wait_ge(S["gdn_p"], 2 * k + f + 1)
                        if n < len(lv) - 1:
                            for j in range(4):
                                hd = 4 * f + j
                                MM(bank(6 + f, 4, P)[0:L, j, 0:L], TT8[0:L, hd, 0:L], P8[0:L, hd, 0:L],
                                   start=True, stop=True)
                        for j in range(4):
                            hd = 4 * f + j
                            m_ = MM(bank(f, 4, P)[0:L, j, 0:L], P8[0:L, hd, 0:L], TT8[0:L, hd, 0:L],
                                    start=True, stop=True)
                        m_.then_inc(S["gdn_pt"], 1)
                k = gdn_level(i, len(lv))
                pe.wait_ge(S["gdn_tu"], 2 * k)
                if i > 0:
                    if i == 2:
                        pe.wait_ge(S["gdn_init"], 16)
                    for hd in range(8):
                        m_ = MM(bank(4, 8, P, n=2)[0:L, hd, :], XC[:, 16 + hd // 2, x0:x0 + L], st[:, hd, :],
                                start=True, stop=True)
                    m_.then_inc(S["gdn_ks"], 1)
                pe.wait_ge(S["gdn_rhs"], i + 1)
                for hd in range(8):
                    m_ = MM(bank(6, 8, P, n=2)[0:L, hd, :], TT8[0:L, hd, 0:L], RHS[0:L, hd, :], start=True, stop=True)
                m_.then_inc(S["gdn_u"], 1)
                pe.wait_ge(S["gdn_ue"], i + 1)
                for hd in range(8):
                    out = bank(2, 8, P, n=2)[:, hd, 0:L]
                    MM(out, U8[0:L, hd, :], DQK[0:L, hd, 0:L], start=True, stop=(i == 0))
                    if i:
                        MM(out, st[:, hd, :], qs[:, hd, 0:L], start=False, stop=True)
                for hd in range(8):
                    m_ = MM(bank(4, 8, P, n=2)[:, hd, :], Kt[0:L, hd, :], U8[0:L, hd, :], start=True, stop=True)
                m_.then_inc(S["gdn_o"], 1)

            def head_sums(sq):
                pe.wait_ge(S["sq2_done"], sq)
                for r in range(2):
                    for c in range(4):
                        m_ = MM(ps[:, 4 * r + c, 0:TOK], ones, uT[:, 4 * r + c, :], start=True, stop=True)
                    m_.then_inc(S["nrm_ps"], 1)

            head_sums(4)

            def project_out(src, groups, first, ready):
                pe.wait_ge(S["cat_ready"], ready)
                for g in range(groups):
                    pe.wait_ge(S[f"out_loaded{g % 3}"], 16 * out_use(first, g))
                    w = ring[g % 3].rearrange("p a b -> p (a b)").rearrange("p (c d) -> p c d", c=4)
                    for c in range(4):
                        k = 4 * g + c
                        for i in range(2):
                            for n in range(2):
                                MM(ps[:, 2 * i + n, :], src[:, k, AT[i]:AT[i] + P],
                                   w[:, c, 512 * n:512 * n + 512], start=(k == 0), stop=(k == 4 * groups - 1))
                    for c in range(4):
                        k = 4 * g + c
                        for j in range(4):
                            m_ = MM(ps[32 * j:32 * j + 32, 4, 0:256], src[:, k, AT[2]:AT[2] + DEC_SEQ],
                                    w[:, c, 256 * j:256 * j + 256], start=(k == 0), stop=(k == 4 * groups - 1))
                    m_.then_inc(S["out_ps"], 1)

            project_out(cat, 4, 0, 1)

            def moe_pe(l):
                pe.wait_ge(S["uT_ready"], 6 * (2 * l + 2))
                for i in range(TILES):
                    for k in range(KD):
                        m_ = MM(ps[0:LEN[i], 0, i * 64:i * 64 + 36], uT[:, k, AT[i]:AT[i] + LEN[i]], wrt[:, l, k, :],
                                start=(k == 0), stop=(k == KD - 1))
                m_.then_inc(S["lg_ps"], 1)
                pe.wait_ge(S["rt_A"], l + 1)
                for i in range(TILES):
                    L = LEN[i]
                    for j in range(i):
                        MM(ps[0:L, 1, i * 32:i * 32 + 32], ones[:, 0:L], A2[:, j, :], start=(j == 0), stop=False)
                    MM(ps[0:L, 1, i * 32:i * 32 + 32], striu[0:L, 0:L], A2[0:L, i, :], start=(i == 0), stop=True)
                for i in range(TILES):
                    m_ = MM(ps[:, 1, 96:128], ones[0:LEN[i], :], A2[0:LEN[i], i, :], start=(i == 0), stop=(i == 2))
                m_.then_inc(S["rt_R"], 1)
                pe.wait_ge(S["rt_OH"], l + 1)
                for k in range(6):
                    L = LEN[k // 2]
                    m_ = MM(ps[:, 2, 0:COLS], OPm[0:L, k, :], OBm[0:L, k, :], start=(k == 0), stop=(k == 5))
                m_.then_inc(S["rt_tab"], 1)
                if stop <= 1:
                    return

                def turn(N, q):
                    for k in range(KD):
                        t_ = nc.tensor.transpose(bank(q, KD, SLOTS)[:, k, :], xg[q][0:SLOTS, k::KD],
                                                 ident[0:SLOTS, 0:SLOTS])
                    t_.then_inc(N["xg_T"], 1)

                def up(N, q, w, out, done):
                    n_ = D_EXP // HALVES
                    for k in range(KD):
                        for g in range(HALVES):
                            m_ = MM(ps[SLOTS * g:SLOTS * (g + 1), out, 0:n_], xT[q][:, k, :],
                                    w[q][:, k, n_ * g:n_ * (g + 1)], start=(k == 0), stop=(k == KD - 1))
                    m_.then_inc(done, 1)

                def turn_hidden(N):
                    for m in range(KE // HALVES):
                        t_ = nc.tensor.transpose(bank(4, KE // HALVES, P)[:, m, :], hid[:, m * P:(m + 1) * P], ident)
                    t_.then_inc(N["hT_ps"], 1)

                def down(N, q):
                    n_ = D_MODEL // HALVES
                    for k in range(KE):
                        src, m = k // (KE // HALVES), k % (KE // HALVES)
                        for g in range(HALVES):
                            m_ = MM(ps[SLOTS * g:SLOTS * (g + 1), 5 + q, 0:n_], hidT[:, m, SLOTS * src:SLOTS * (src + 1)],
                                    wdb[q][:, k, n_ * g:n_ * (g + 1)], start=(k == 0), stop=(k == KE - 1))
                    m_.then_inc(N["y_ps"], 1)

                def blocks(i):
                    for q in range(2):
                        b = i * 2 + (l * EXPERTS + q)
                        loaded = i * 16 + 16 * (l * PAIRS + 1)
                        pe.wait_ge(S[f"wg{q}"], loaded)
                        pe.wait_ge(S["xT_ready"], i * 2 + (l * (EXPERTS + 1) + q + 1))
                        need(pe, S["sg_ready"], b)
                        up(S, q, wgb, 2, S["gate_ps"])
                        pe.wait_ge(S[f"wu{q}"], loaded)
                        need(pe, S["hid_ready"], b)
                        if q == 0:
                            pe.wait_ge(S["xgathered1"], i * 16 + 16 * (l * PAIRS + 1))
                        else:
                            pe.wait_ge(S["xgathered0"], i * 16 + 16 * (l * (PAIRS + 1) + 2))
                        up(S, q, wub, 3, S["up_ps"])
                        turn(S, 1 - q)
                        pe.wait_ge(S["hid_ready"], b + 1)
                        need(pe, S["hidT_ready"], b)
                        turn_hidden(S)
                        pe.wait_ge(S["hidT_ready"], b + 1)
                        pe.wait_ge(S[f"wd{q}"], loaded)
                        if not isinstance(b, int) or b > 1:
                            pe.wait_ge(S["y_ready"], b - 1)
                        down(S, q)

                pe.wait_ge(S["xgathered0"], 16 * (l * (PAIRS + 1) + 1))
                turn(S, 0)
                blocks(0)
                with pe.Fori(1, PAIRS) as i:
                    blocks(i)
                X = extra_signals[l]
                count = pe.value_load(extra_e[0:1, l, EXTRA:EXTRA + 1], min_val=0, max_val=EXTRA)
                for x in range(EXTRA):
                    with pe.If(count > x):
                        if x == 0:
                            pe.wait_ge(S["y_ready"], (l + 1) * EXPERTS)
                            pe.wait_ge(S["xT_ready"], (l + 1) * (EXPERTS + 1))
                        pe.wait_ge(X["xgathered"], 16 * (x + 1))
                        turn(X, 0)
                        pe.wait_ge(X["wg"], 16 * (x + 1))
                        pe.wait_ge(X["xT_ready"], x + 1)
                        up(X, 0, wgb, 2, X["gate_ps"])
                        pe.wait_ge(X["wu"], 16 * (x + 1))
                        up(X, 0, wub, 3, X["up_ps"])
                        pe.wait_ge(X["hid_ready"], x + 1)
                        turn_hidden(X)
                        pe.wait_ge(X["hidT_ready"], x + 1)
                        pe.wait_ge(X["wd"], 16 * (x + 1))
                        down(X, 0)
                        pe.wait_ge(X["y_ready"], x + 1)

            norm(1)
            moe_pe(0)
            if stop <= 2:
                return
            norm(2)
            pe.wait_ge(S["uT_ready"], 18)
            project(4 * HEADS, CONV_TILES + Z_TILES, 1)
            pe.wait_ge(S["proj_evac"], CONV_TILES + Z_TILES + 4 * HEADS)
            pe.wait_ge(S["lf_in"], 1)
            n = 0
            for i in range(TILES):
                L, c0 = LEN[i], AT[i]
                st = hS[1 if i == 2 else 0]
                if i:
                    pe.wait_ge(S["hg_upd"], i)
                GB = bank(0, 8, P, n=2)
                for n in range(1 + sum(b < L for b in LEVELS)):
                    m = gdn_level(i, n) + i
                    if m >= 2:
                        pe.wait_ge(S["hg_keep"], m - 1)
                    if n:
                        pe.wait_ge(S["hg_qk"], gdn_level(i, n))
                    for hd in range(8):
                        R = hR[(gdn_level(i, n) - 1) % 2][:, hd, 0:L]
                        a_, b_ = (R, R) if n else (hk[:, hd, c0:c0 + L], hq[:, hd, c0:c0 + L])
                        m_ = MM(bank(2 * (m % 2), 8, P, n=2)[0:L, hd, 0:L], a_, b_, start=True, stop=True)
                    m_.then_inc(S["hg_att"], 1)
                pe.wait_ge(S["hg_in"], i + 1)
                for hd in range(8):
                    nc.tensor.transpose(bank(2, 8, P, n=2)[0:L, hd, :], hK[:, hd, 0:L], ident)
                    t_ = nc.tensor.transpose(bank(4, 8, P, n=2)[0:L, hd, :], hv[:, hd, c0:c0 + L], ident)
                t_.then_inc(S["hg_tr"], 1)
                pe.wait_ge(S["hg_acc"], i + 1)
                if i == 2:
                    pe.wait_ge(S["gdn_init"], 32)
                for hd in range(8):
                    out = bank(6, 8, P, n=2)[:, hd, 0:L]
                    MM(out, hVt[0:L, hd, :], hA[0:L, hd, 0:L], start=True, stop=(i == 0))
                    if i:
                        MM(out, st[:, hd, :], hQ[:, hd, 0:L], start=False, stop=True)
                for hd in range(8):
                    m_ = MM(GB[:, hd, :], hKt[0:L, hd, :], hVt[0:L, hd, :], start=True, stop=True)
                m_.then_inc(S["hg_y"], 1)
            head_sums(5)
            project_out(hcat, 2, 4, 2)
            norm(3)
            moe_pe(1)


def gdn_level(i, n):
    return sum(sum(b < LEN[j] for b in LEVELS) for j in range(i)) + n


def ring_use(projection, group):
    slot = group % 3
    before = len(range(slot, AB_GROUPS, 3)) if projection else 0
    return before + group // 3 + 1


def out_use(first, group):
    slot = group % 3
    before = len(range(slot, 4, 3)) if first else 0
    return before + group // 3 + 1


def constants():
    import numpy as np
    c = np.zeros((P, C_END), np.float32)
    i, j = np.arange(P)[:, None], np.arange(P)[None, :]
    c[:, C_ID:C_ID + P] = i == j
    c[:, C_ONES:C_ONES + P] = 1
    c[:, C_TRIU:C_TRIU + P] = i <= j
    c[:, C_STRIU:C_STRIU + P] = i < j
    for n, b in enumerate(LEVELS):
        c[:, C_MASK + n * P:C_MASK + (n + 1) * P] = (i // (2 * b) == j // (2 * b)) & (i % (2 * b) < b) & (j % (2 * b) >= b)
    c[:, C_IOTA:C_IOTA + P] = j
    for t in range(TILES):
        for k in range(2):
            c[:, C_VAL + 2 * t + k] = AT[t] + np.arange(P) + 1 + TOK * k
    c[:, C_SCAN:C_SCAN + TOK] = 1
    for t in range(TILES):
        c[:, C_SCAN + AT[t]] = 0
    c[:, C_EPS] = EPS
    c[:, C_EPSQ] = EPS * P
    c[:, C_HALF] = np.arange(P) // SLOTS
    c[:, C_SLOT:C_SLOT + P] = j % SLOTS
    return c


def lay_out(x):
    import numpy as np
    f = {n: np.asarray(a) for n, a in x.items()}
    w = f["w_in_ab"][0]
    zs, xbc, dt, qkv, zg, b, a = np.split(w, np.cumsum([1024, 1536, 16, 2048, 1024, 8])[:].tolist(), axis=1)
    main = np.concatenate([xbc, qkv, zs, zg], axis=1)
    tile = lambda m: np.ascontiguousarray(
        m.reshape(P, KD, -1, GROUP).transpose(2, 0, 1, 3)).reshape(-1, P, KD * GROUP)
    chan = lambda m: m.reshape(-1, P).T
    conv_w = np.concatenate([f["ssd_conv_w"][0], f["gdn_conv_w"][0]], axis=1).reshape(CONV_W, CONV_TILES, P)
    conv_b = np.concatenate([f["ssd_conv_b"][0], np.zeros(QKV_TILES * P, np.float32)])
    vec = np.concatenate(
        [f[n][l].reshape(P, KD) for l in range(2) for n in ("norm_mix", "norm_ffn")]
        + [conv_w.transpose(2, 1, 0).reshape(P, -1), chan(conv_b), chan(np.repeat(f["ssd_d"][0], 64)),
           chan(f["ssd_norm"][0]), f["gdn_norm"][0][:, None], f["hgrn_norm"][0][:, None],
           f["hgrn_lb_logits"].reshape(2, HEADS, P).transpose(2, 0, 1).reshape(P, -1)], axis=1)
    st = np.concatenate([f["state_ssd_conv"][0, 0], f["state_gdn_conv"][0, 0]], axis=1)
    return {
        "con": constants(), "vec": np.ascontiguousarray(vec),
        "row": np.concatenate([f["ssd_dt_bias"][0], f["gdn_dt_bias"][0], f["ssd_a_log"][0], f["gdn_a_log"][0]])[None],
        "final": np.ascontiguousarray(f["norm_final"][None]),
        "wsm": np.ascontiguousarray(np.concatenate([dt, a, b], axis=1).reshape(P, KD, 32)),
        "wrt": np.ascontiguousarray(np.concatenate([f["moe_w_group"], f["moe_w_router"]], axis=2)
                                    .reshape(2, P, KD, 36).transpose(1, 0, 2, 3)),
        "wA": tile(main), "wC": tile(f["w_in_c"][0]),
        "w_out_ab": f["w_out_ab"][0], "w_out_c": f["w_out_c"][0],
        "wg": f["moe_w_gate"], "wu": f["moe_w_up"], "wd": f["moe_w_down"],
        "xp": f["x_prompt"][0], "xs": f["x_sample"][0],
        "conv_st": np.ascontiguousarray(st.reshape(TAPS, CONV_TILES, P).transpose(2, 1, 0)),
        "st_ssd": f["state_ssd"].reshape(SSD_HEADS * 64, 128), "st_gdn": f["state_gdn"][0, 0],
        "st_hgrn": f["state_hgrn"][0, 0],
    }


OUTS = {"y_p": (SEQ, D_MODEL), "y_s": (DEC_SEQ, D_MODEL), "conv": (2, P, CONV_TILES, TAPS),
        "ssd_p": (SSD_HEADS * 64, P), "ssd_s": (SSD_HEADS * 64, P), "gdn_p": (8, P, P), "gdn_s": (8, P, P),
        "hgrn_p": (8, P, P), "hgrn_s": (8, P, P)}


def kernel(**inputs):
    import concourse.bacc as _bacc
    from concourse import mybir as _mybir
    from concourse.bass_utils import run_bass_kernel_spmd as _run

    arrays = lay_out(inputs)
    nc = _bacc.Bacc("TRN2", target_bir_lowering=False, num_devices=1)
    ins = {n: nc.dram_tensor(f"in_{n}", a.shape, _mybir.dt.from_np(a.dtype), kind="ExternalInput").ap()
           for n, a in arrays.items()}
    outs = {n: nc.dram_tensor(f"out_{n}", s, _mybir.dt.float32, kind="ExternalOutput").ap() for n, s in OUTS.items()}
    build(nc, ins, outs)
    r = _run(nc, [{f"in_{n}": a for n, a in arrays.items()}], core_ids=[0]).results[0]
    out = {n: r[f"out_{n}"] for n in OUTS}
    conv = out["conv"].transpose(0, 3, 2, 1).reshape(2, 1, 1, TAPS, CONV_TILES * P)
    cut = XBC_TILES * P
    ssd = lambda a: a.reshape(1, 1, SSD_HEADS, 64, P)
    hd = lambda a: a.reshape(1, 1, 8, P, P)
    return (out["y_p"][None], out["y_s"][None],
            ssd(out["ssd_p"]), conv[0, ..., :cut], hd(out["gdn_p"]), conv[0, ..., cut:], hd(out["hgrn_p"]),
            ssd(out["ssd_s"]), conv[1, ..., :cut], hd(out["gdn_s"]), conv[1, ..., cut:], hd(out["hgrn_s"]))
```

```python
import concourse.bass as bass
from concourse import mybir
from contextlib import ExitStack

D_MODEL = 1024
SEQ, DEC_SEQ = 256, 32
TOK = SEQ + DEC_SEQ
P = 128
KD = D_MODEL // P
TILES = 3
LEN = [P, P, DEC_SEQ]
AT = [0, P, 2 * P]
CONV_W = 4
TAPS = CONV_W - 1
XW = TOK + TAPS
AX = [0, P, SEQ + TAPS]
XP = XW + TAPS
EPS = 1e-6
SSD_HEADS, SSD_TILES = 16, 8
XBC_TILES, QKV_TILES = 12, 16
CONV_TILES = XBC_TILES + QKV_TILES
GDN_HEADS = 8
Z_TILES = 16
LEVELS = [1, 2, 4, 8, 16, 32, 64]
HEADS = 8
SCAL = SSD_HEADS + GDN_HEADS
GROUP = 512
AB_GROUPS = (CONV_TILES + Z_TILES) * P // GROUP
C_GROUPS = 4 * D_MODEL // GROUP
EXPERTS, E_PER, D_EXP = 32, 8, 512
KE = D_EXP // P
SLOTS = 64
EXTRA = (2 * TOK - 1) // SLOTS
SHIFT = SLOTS.bit_length() - 1
HALVES = P // SLOTS
BUFFERS = 3
PEELED = 2
ROUND = 2 * BUFFERS
HEAD_ROUNDS = [(0, 3), (3, 6), (6, 8)]
AT_SMALL, AT_DECAY, AT_QUERY, AT_KEY = CONV_TILES + 1, CONV_TILES + 4, CONV_TILES + 7, CONV_TILES + 10
NORM_LEVEL = 2
AT_FORGET = HEADS + 3
HG_STEPS = [(i, n) for i in range(TILES) for n in range(1 + sum(b < LEN[i] for b in LEVELS))]
STEP_AT = [2 * HEADS + j * (2 * HEADS - 1) // (len(HG_STEPS) - 1) for j in range(len(HG_STEPS))]
LAST_BANKS = [6, 2, 4]
ROUNDS = (EXPERTS - PEELED) // ROUND
AHEAD = 3
NOWHERE = 1.0e6
PAIRS = EXPERTS // 2
COLS = EXPERTS + EXTRA

C_ID, C_ONES, C_TRIU, C_STRIU, C_MASK = 0, P, 2 * P, 3 * P, 4 * P
C_IOTA = C_MASK + len(LEVELS) * P
C_VAL = C_IOTA + P
C_SCAN = C_VAL + TILES
C_EPS = C_SCAN + TOK
C_SLOT = C_EPS + 1
C_EPSQ = C_SLOT + P
C_END = C_EPSQ + 1
V_NORM, V_CONV, V_BIAS = 0, 4 * KD, 4 * KD + CONV_TILES * CONV_W
V_D = V_BIAS + CONV_TILES
V_SNORM = V_D + SSD_TILES
V_GNORM = V_SNORM + SSD_TILES
V_HNORM = V_GNORM + 1
V_LB = V_HNORM + 1
V_END = V_LB + 2 * HEADS
R_BIAS, R_ALOG, R_END = 0, SCAL, 2 * SCAL


def build(nc, ins, outs):
    F, I32, U32 = mybir.dt.float32, mybir.dt.int32, mybir.dt.uint32
    ACT, ALU, AX_X = mybir.ActivationFunctionType, mybir.AluOpType, mybir.AxisListType.X

    xn_dram = nc.dram_tensor("xn_rows", [TOK, D_MODEL], F, kind="Internal").ap()
    wg_dram = ins["wg"].rearrange("l e (p k) f -> (l e) p (k f)", p=P)
    wu_dram = ins["wu"].rearrange("l e (p k) f -> (l e) p (k f)", p=P)
    wd_dram = ins["wd"].rearrange("l e (k p) f -> (l e) p k f", p=P)

    ctx = ExitStack()
    with ctx:
        def sb(name, shape, dt=F):
            return ctx.enter_context(nc.sbuf_tensor(name, shape, dt))

        def sem(name):
            return ctx.enter_context(nc.semaphore(name))

        h = sb("h", [P, TILES, D_MODEL])
        xn = sb("xn", [P, TILES, D_MODEL])
        uT = sb("uT", [P, KD, TOK])
        con = sb("con", [P, C_END])
        vec = sb("vec", [P, V_END])
        row = sb("row", [P, R_END])
        wsm = sb("wsm", [P, KD, 32])
        wrt = sb("wrt", [P, 2, KD, 36])
        ss = sb("ss", [P, 5, TILES])
        rstd = sb("rstd", [P, 5, TILES])
        ps = ctx.enter_context(nc.psum_tensor("ps", [P, 8, 512], F))
        ARENA = 37900
        arena = sb("arena", [P, ARENA])

        def at(off, *dims):
            n = 1
            for d in dims:
                n *= d
            assert off + n <= ARENA, (off, dims)
            flat = arena[:, off:off + n]
            if len(dims) == 1:
                return flat
            names = ["a", "b", "c", "d"][:len(dims)]
            return flat.rearrange("p (" + " ".join(names) + ") -> p " + " ".join(names),
                                  **dict(zip(names[1:], dims[1:])))

        def bank(b, *dims, n=1):
            flat = ps[:, b:b + n, :].rearrange("p a b -> p (a b)")
            size = 1
            for d in dims:
                size *= d
            names = ["a", "b", "c"][:len(dims)]
            if len(dims) == 1:
                return flat[:, 0:size]
            return flat[:, 0:size].rearrange("p (" + " ".join(names) + ") -> p " + " ".join(names),
                                             **dict(zip(names[1:], dims[1:])))

        ident = con[:, C_ID:C_ID + P]
        ones = con[:, C_ONES:C_ONES + P]
        triu = con[:, C_TRIU:C_TRIU + P]
        striu = con[:, C_STRIU:C_STRIU + P]
        eps = con[:, C_EPS:C_EPS + 1]
        iota = con[:, C_IOTA:C_IOTA + P]

        def mask(n):
            return con[:, C_MASK + n * P:C_MASK + (n + 1) * P]

        def take(cursor, end, *dims):
            n = 1
            for d in dims:
                n *= d
            off = cursor[0]
            cursor[0] += n
            assert cursor[0] <= end, (cursor, end)
            return at(off, *dims)

        RING = 3 * KD * GROUP
        ring = [at(s * KD * GROUP, KD, GROUP) for s in range(3)]
        cur = [RING]
        XC = take(cur, ARENA, CONV_TILES, XW)
        Z = take(cur, ARENA, Z_TILES, TOK)
        cat = take(cur, ARENA, 16, TOK)
        in_pad = cur[0]
        xpad = take(cur, ARENA, CONV_TILES, XP)
        STAGE = RING - 1024
        s_stage = at(STAGE, 8, P)
        cur = [0]
        Xdt2, Xtl2 = [[take(cur, STAGE, 8, 64) for _ in range(2)] for _ in range(2)]
        Btok2, BCm = [take(cur, STAGE, P) for _ in range(2)], take(cur, STAGE, P)
        HT = [take(cur, STAGE, 2, 512) for _ in range(2)]
        s_load = take(cur, STAGE, 8, P)
        ssd_more = cur[0]
        assert ssd_more + 3 * 8 * P <= STAGE
        cur = [in_pad]
        Dm, EG, W8, Cs = [take(cur, ARENA, 8, P) for _ in range(4)]
        W82, Cs2, EG2 = [W8, at(ssd_more, 8, P)], [Cs, at(ssd_more + 1024, 8, P)], [EG, at(ssd_more + 2048, 8, P)]
        DQK, DKK = take(cur, ARENA, 8, P), take(cur, ARENA, 8, P)
        tail, dec, ecum, nbe, dec_b = [take(cur, ARENA, 8) for _ in range(5)]
        dec2 = [dec, dec_b]
        qs = W8
        cur = [0]
        GS = [take(cur, STAGE, 8, P) for _ in range(2)]
        T8, TT8, P8, VB, U8, Bm0, Kt, Bm1 = [take(cur, STAGE, 8, P) for _ in range(8)]
        Ktok = take(cur, STAGE, 4, P)
        Bm, RHS = [Bm0, Bm1], P8
        conv_st = sb("conv_st", [P, CONV_TILES, TAPS])
        conv_new = sb("conv_new", [P, 2, CONV_TILES, TAPS])
        cvt = sb("cvt", [P, 2, XW])
        sc = sb("sc", [P, TILES, 32])
        spx = sb("spx", [P, 4, TILES, SCAL])
        dtg = sb("dtg", [P, TILES, SCAL])
        G24 = sb("G24", [P, TILES, SCAL])
        cum = sb("cum", [P, TILES, SCAL])
        eA = sb("eA", [P, SCAL])
        beta = sb("beta", [P, TILES, 8])
        cur = [RING]
        hq, hk, hg, hv, hz = [take(cur, ARENA, HEADS, TOK) for _ in range(5)]
        in_hE = cur[0]
        hE, hQ0, hK0, hA0, hVt, hKt, hEq = [take(cur, ARENA, 8, P) for _ in range(7)]
        hcat = take(cur, ARENA, HEADS, TOK)
        hD = [take(cur, ARENA, 8, P) for _ in range(2)]
        hR = [take(cur, ARENA, 8, P) for _ in range(2)]
        xn_tile = [xn[:, q, :].rearrange("p (a b) -> p a b", a=8) for q in range(TILES)]
        cvt_flat = cvt[:, :, :].rearrange("p a b -> p (a b)")
        hA = [hA0, xn_tile[0], cvt_flat[:, 0:8 * DEC_SEQ].rearrange("p (a b) -> p a b", a=8)]
        hQ = [hQ0, xn_tile[1], take(cur, ARENA, 8, DEC_SEQ)]
        hK = [hK0, xn_tile[2], take(cur, ARENA, 8, DEC_SEQ)]
        hDec = [cvt_flat[:, 8 * (DEC_SEQ + q):8 * (DEC_SEQ + q + 1)] for q in range(TILES)]
        tok_rows = [(hKt, hVt), (hE, hEq)]
        hS = [at(2 * KD * GROUP, 8, P), at(2 * KD * GROUP + 1024, 8, P)]
        lbv = sb("lbv", [P, 6, HEADS])
        EXPERT = 3 * KD * D_EXP
        bases = [RING, 2 * EXPERT, 0]
        wgb = [at(o, KD, D_EXP) for o in bases]
        wub = [at(o + KD * D_EXP, KD, D_EXP) for o in bases]
        wdb = [at(o + 2 * KD * D_EXP, KE, D_MODEL) for o in bases]
        final_w = at(0, D_MODEL)
        uT_flat = uT[:, :, :].rearrange("p a b -> p (a b)")
        ucur = [0]

        def in_uT(*dims):
            n = 1
            for d in dims:
                n *= d
            off = ucur[0]
            ucur[0] += n
            assert ucur[0] <= KD * TOK
            flat = uT_flat[:, off:off + n]
            return flat if len(dims) == 1 else flat.rearrange("p (a b) -> p a b", a=dims[0])

        in_uT(TOK)
        OPm, OBm, OBg = in_uT(6, P), in_uT(6, COLS), in_uT(6, COLS)
        ucur = [0]
        tokens = in_uT(TOK)
        xT = in_uT(KD, SLOTS)
        hid, sg = in_uT(D_EXP // HALVES), in_uT(D_EXP // HALVES)
        hidT = in_uT(KE // HALVES, P)
        weight = in_uT(TOK)
        xg = [xn[:, q, :] for q in range(2)]
        yb = xn[:, 2, :]
        LG = sb("LG", [P, TILES, 36])
        RT = sb("rt", [P, 1720])
        rcur = [0]

        def small(*dims):
            n = 1
            for d in dims:
                n *= d
            off = rcur[0]
            rcur[0] += n
            assert rcur[0] <= 1720
            flat = RT[:, off:off + n]
            if len(dims) == 1:
                return flat
            names = ["a", "b", "c"][:len(dims)]
            return flat.rearrange("p (" + " ".join(names) + ") -> p " + " ".join(names),
                                  **dict(zip(names[1:], dims[1:])))

        gl8, gm8 = small(3, 8), small(3, 8)
        gif, sgm, den = small(3, 1), small(3, 1), small(3, 1)
        rt_ge, ohg = small(3, 4), small(3, 4)
        selm, esel, ev8 = small(3, 32), small(3, 8), small(3, 8)
        eif, eid, rt_e2 = small(3, 2), small(3, 2), small(3, 1)
        O2, OD = small(3, 2, 32), small(3, 2, 32)
        A2, R2, over, extb = small(3, 32), small(3, 32), small(3, 32), small(3, 32)
        cnt, nx, incl, exb = small(32), small(32), small(32), small(32)
        pos, p1f, b1f = small(6), small(6), small(6)
        none, rows = small(COLS), small(COLS)
        xe = small(EXTRA + 1)
        cmp = small(EXTRA, 32)
        gi8 = sb("gi8", [P, 3, 8], U32)
        ei8 = sb("ei8", [P, 3, 8], U32)
        posi = sb("posi", [P, 3, 6], I32)
        gates = sb("gates", [P, TILES, 2])
        gidx = sb("gidx", [P, COLS], U32)
        slot_token = sb("slot_token", [P, COLS])
        slot_gate = sb("slot_gate", [P, COLS])
        extra_e = sb("extra_e", [1, 2, EXTRA + 1], I32)

        xn_flat = xn[:, :, :].rearrange("p a b -> p (a b)")
        sq4 = xn_flat[:, 0:4 * XW].rearrange("p (a b) -> p a b", a=4)
        rsq = xn_flat[:, 4 * XW:8 * XW].rearrange("p (a b) -> p a b", a=4)
        rs0 = rsq
        rs1 = at(in_hE, 4, XW)
        S = {}

        def s_(name):
            if name not in S:
                S[name] = sem(name)
            return S[name]

        for name in ("x_loaded consts_loaded h_ready sq_done xn_ready xnT_ps uT_ready dve_step act_step "
                     "proj_ps proj_evac conv_out conv_act small_ps small_evac sp_exp1 sp_pos sp_ln g_ready "
                     "ea_ready cum_ps cum_ready ssd_in ssd_diff ssd_exp ssd_w ssd_y ssd_upd st_T st_Tevac "
                     "state_in ssd_final yg_ready sq2_done nrm_ps nrm_done gdn_in gdn_diff gdn_exp gdn_mats "
                     "gdn_bm gdn_p gdn_pe gdn_pt gdn_tu gdn_ks gdn_rhs gdn_u gdn_ue gdn_o gdn_upd gdn_out "
                     "state_loaded gdn_unit gdn_vb gdn_side cat_ready out_ps out_loaded0 out_loaded1 out_loaded2 "
                     "states_out conv_new_ready beta_ready ring0 ring1 ring2 decay_in decay_act hg_keep hg_d "
                     "hg_e hg_qk hg_att hg_acc hg_in hg_x hg_y hg_ex hg_upd hg_tr hg_out lg_ps rt_diff rt_exp "
                     "rt_A rt_R rt_OH rt_tab route_done xn_stored xg_zero xgathered0 xgathered1 weight_ready "
                     "xg_T xT_ready wg0 wg1 wg2 wu0 wu1 wu2 wd0 wd1 wd2 gate_ps up_ps sg_ready hid_ready "
                     "hT_ps hidT_ready y_ps y_ready placed_ps h_added y_out hist_loaded ss_set small_loaded "
                     "final_loaded rs_done").split():
            s_(name)
        extra_signals = [{n: sem(f"extra{l}_{n}") for n in
                          ("wg", "wu", "wd", "xgathered", "weight_ready", "xg_T", "xT_ready", "gate_ps",
                           "up_ps", "sg_ready", "hid_ready", "hT_ps", "hidT_ready", "y_ps", "y_ready", "placed_ps", "h_added")}
                         for l in range(2)]

        def need(eng, semaphore, value):
            if not isinstance(value, int) or value > 0:
                eng.wait_ge(semaphore, value)

        def peeled(l, b):
            return b % BUFFERS, b, lambda k=1: int(k * (l * EXPERTS + b))

        def looped(l, i, j):
            b = i * ROUND + (PEELED + j)
            return ((PEELED + j) % BUFFERS, b,
                    lambda k=1: i * int(ROUND * k) + int(k * (l * EXPERTS + PEELED + j)))

        def loads_before(l, s):
            return l * len(range(s, EXPERTS, BUFFERS))

        block = ctx.enter_context(nc.Block())

        @block.sync
        def _(sp):
            sp.dma_start(h[:, 0:2, :], ins["xp"].rearrange("(t p) d -> p t d", p=P)).then_inc(S["x_loaded"], 16)
            sp.dma_start(h[0:DEC_SEQ, 2, :], ins["xs"]).then_inc(S["x_loaded"], 16)
            sp.dma_start(con[:, :], ins["con"]).then_inc(S["consts_loaded"], 16)
            sp.dma_start(vec[:, :], ins["vec"]).then_inc(S["consts_loaded"], 16)
            sp.dma_start(conv_st[:, :, :], ins["conv_st"]).then_inc(S["hist_loaded"], 16)

            def load_ring(src, groups, first, evac_base, after_first):
                for g in range(groups):
                    if g == 1:
                        after_first()
                    if g >= 3:
                        sp.wait_ge(S["proj_ps"], evac_base + 4 * (g - 2))
                    n = first + g
                    sp.dma_start(ring[g % 3].rearrange("p a b -> p (a b)"), src[g]).then_inc(S[f"ring{g % 3}"], 16)

            def small_loads():
                sp.dma_start(row[:, :], ins["row"].to_broadcast([P, R_END])).then_inc(S["small_loaded"], 16)
                sp.dma_start(wsm[:, :, :], ins["wsm"]).then_inc(S["small_loaded"], 16)
                sp.dma_start(wrt[:, :, :, :], ins["wrt"]).then_inc(S["small_loaded"], 16)

            load_ring(ins["wA"], AB_GROUPS, 0, 0, small_loads)
            sp.wait_ge(S["proj_ps"], AB_GROUPS * 4)
            sp.dma_start(s_load, ins["st_ssd"].rearrange("(c q) n -> q c n", q=P)).then_inc(S["state_in"], 16)
            sp.wait_ge(S["conv_new_ready"], 2)
            for j in range(2):
                sp.dma_start(outs["conv"][j], conv_new[:, j]).then_inc(S["states_out"], 16)
            for n, name in enumerate(("ssd_p", "ssd_s")):
                sp.wait_ge(S["ssd_final"], n + 1)
                sp.dma_start(outs[name].rearrange("(c q) n -> q c n", q=P), s_stage).then_inc(S["states_out"], 16)
            sp.wait_ge(S["ssd_final"], 2)
            sp.dma_start(GS[1], ins["st_gdn"].rearrange("h k v -> k h v")).then_inc(S["state_loaded"], 16)
            for n, name in enumerate(("gdn_p", "gdn_s")):
                sp.wait_ge(S["gdn_upd"], 2 + n)
                sp.dma_start(outs[name].rearrange("h k v -> k h v"), GS[n]).then_inc(S["states_out"], 16)
            sp.wait_ge(S["states_out"], 16 * 6)

            def load_out(src, groups, first):
                for g in range(groups):
                    if g >= 3:
                        sp.wait_ge(S["out_ps"], first + g - 2)
                    sp.dma_start(ring[g % 3].rearrange("p a b -> p (a b)").rearrange("p (c d) -> p c d", c=4),
                                 src[g * 4 * P:(g + 1) * 4 * P, :].rearrange("(c p) d -> p c d", p=P)
                                 ).then_inc(S[f"out_loaded{g % 3}"], 16)

            sp.wait_ge(S["yg_ready"], 2)
            load_out(ins["w_out_ab"], 4, 0)

            def load_expert(s, e, free, signals):
                for buf, w, name, done in ((wgb, wg_dram, "wg", "gate_ps"), (wub, wu_dram, "wu", "up_ps"),
                                           (wdb, wd_dram, "wd", "y_ps")):
                    if free is not None:
                        sp.wait_ge(S[done], free)
                    if name == "wd":
                        src, dst = w[bass.ds(e, 1)].rearrange("a p k f -> p (a k) f"), buf[s]
                    else:
                        src, dst = w[bass.ds(e, 1)].rearrange("a p f -> p (a f)"), buf[s].rearrange("p a b -> p (a b)")
                    sp.dma_start(dst, src).then_inc(signals[name], 16)

            slots = [{n: S[f"{n}{s}"] for n in ("wg", "wu", "wd")} for s in range(BUFFERS)]

            def store_rows(l):
                for i in range(TILES):
                    sp.wait_ge(S["xn_ready"], (2 * l + 1) * TILES + i + 1)
                    sp.dma_start(xn_dram[AT[i]:AT[i] + LEN[i], :], xn[0:LEN[i], i, :]).then_inc(S["xn_stored"], 16)

            def moe_loads(l, next_loads):
                load_expert(1, l * EXPERTS + 1, None, slots[1])
                store_rows(l)
                for b in range(2, BUFFERS):
                    load_expert(b, l * EXPERTS + b, None, slots[b])
                for b in range(BUFFERS, PEELED + BUFFERS):
                    load_expert(b % BUFFERS, l * EXPERTS + b, l * EXPERTS + b - 2, slots[b % BUFFERS])
                last = ROUND - BUFFERS
                with sp.Fori(0, ROUNDS - 1) as i:
                    for j in range(ROUND):
                        s, b, n = looped(l, i, j)
                        load_expert(s, b + (l * EXPERTS + BUFFERS), n() + 1, slots[s])
                for b in range(EXPERTS - last, EXPERTS):
                    load_expert(b % BUFFERS, l * EXPERTS + b, l * EXPERTS + b - 2, slots[b % BUFFERS])
                sp.wait_ge(S["y_ps"], (l + 1) * EXPERTS - 2)
                next_loads()
                sp.wait_ge(S["y_ps"], (l + 1) * EXPERTS)
                count = sp.value_load(extra_e[0:1, l, EXTRA:EXTRA + 1], min_val=0, max_val=EXTRA)
                X = extra_signals[l]
                for x in range(EXTRA):
                    with sp.If(count > x):
                        e = sp.value_load(extra_e[0:1, l, x:x + 1], min_val=0, max_val=2 * EXPERTS - 1)
                        load_expert(0, e, None, X)
                        sp.wait_ge(X["y_ps"], x + 1)

            sp.wait_ge(S["cat_ready"], 3)
            load_expert(0, 0, None, slots[0])
            sp.wait_ge(S["h_ready"], TILES)

            def first_groups():
                for g in range(3):
                    sp.dma_start(ring[g].rearrange("p a b -> p (a b)"), ins["wC"][g]).then_inc(S[f"ring{g}"], 16)

            def final_loads():
                sp.dma_start(final_w, ins["final"].to_broadcast([P, D_MODEL])).then_inc(S["final_loaded"], 16)

            moe_loads(0, first_groups)
            for g in range(3, C_GROUPS):
                sp.wait_ge(S["proj_ps"], (AB_GROUPS + g - 2) * 4)
                sp.dma_start(ring[g % 3].rearrange("p a b -> p (a b)"), ins["wC"][g]).then_inc(S[f"ring{g % 3}"], 16)
            sp.wait_ge(S["proj_ps"], (AB_GROUPS + C_GROUPS) * 4)
            sp.dma_start(hS[1], ins["st_hgrn"].rearrange("h k v -> k h v")).then_inc(S["state_loaded"], 16)
            load_out(ins["w_out_c"], 2, 4)
            for n, name in enumerate(("hgrn_p", "hgrn_s")):
                sp.wait_ge(S["hg_upd"], 2 + n)
                sp.dma_start(outs[name].rearrange("h k v -> k h v"), hS[n]).then_inc(S["states_out"], 16)
            sp.wait_ge(S["states_out"], 16 * 8)
            sp.wait_ge(S["cat_ready"], 6)
            load_expert(0, EXPERTS, None, slots[0])
            sp.wait_ge(S["h_ready"], 3 * TILES)
            moe_loads(1, final_loads)
            for i in range(TILES):
                sp.wait_ge(S["xn_ready"], 4 * TILES + i + 1)
                dst = outs["y_p"][AT[i]:AT[i] + P, :] if i < 2 else outs["y_s"]
                sp.dma_start(dst, xn[0:LEN[i], i, :]).then_inc(S["y_out"], 16)
            sp.wait_ge(S["y_out"], 16 * TILES)

        @block.gpsimd
        def _(pool):
            for i in range(TILES):
                L = LEN[i]
                x0 = AX[i]
                pool.wait_ge(S["ssd_final"], 2)
                if i:
                    pool.wait_ge(S["gdn_upd"], i)
                unit = ident[0:L, 0:L].unsqueeze(1).to_broadcast([L, 8, L])
                nc.gpsimd.tensor_copy(T8[0:L, :, 0:L], unit)
                nc.gpsimd.tensor_copy(TT8[0:L, :, 0:L], unit).then_inc(S["gdn_unit"], 1)
                for n in range(sum(b < L for b in LEVELS)):
                    k = gdn_level(i, n)
                    pool.wait_ge(S["gdn_mats"], i + 1)
                    if k >= 2:
                        pool.wait_ge(S["gdn_pe"], 2 * (k - 1))
                    nc.gpsimd.tensor_tensor(Bm[k % 2][0:L, :, 0:L], DKK[0:L, :, 0:L],
                                            mask(n)[0:L, 0:L].unsqueeze(1).to_broadcast([L, 8, L]), ALU.mult
                                            ).then_inc(S["gdn_bm"], 1)
                    if n == 1:
                        pool.wait_ge(S["gdn_exp"], 3 * i + 3)
                        nc.gpsimd.tensor_tensor(
                            qs.rearrange("p (a b) c -> p a b c", b=2)[:, :, :, 0:L],
                            EG.rearrange("p (a b) c -> p a b c", b=2)[:, :, :, 0:L],
                            XC[:, 12:16, x0:x0 + L].unsqueeze(2).to_broadcast([P, 4, 2, L]), ALU.mult)
                        pool.wait_ge(S["gdn_vb"], i + 1)
                        nc.gpsimd.tensor_tensor(
                            Kt[0:L].rearrange("p (a b) c -> p a b c", b=2),
                            Ktok[0:L].unsqueeze(2).to_broadcast([L, 4, 2, P]),
                            tail[0:L].rearrange("p (a b) -> p a b", b=2).unsqueeze(3).to_broadcast([L, 4, 2, P]),
                            ALU.mult).then_inc(S["gdn_side"], 1)
            for l in range(2):
                pool.wait_ge(S["xn_stored"], 16 * TILES * (l + 1))
                pool.wait_ge(S["xnT_ps"], 6 * (2 * l + 2))
                nc.gpsimd.memset(xg[0], 0.0).then_inc(S["xg_zero"], 1)
                nc.gpsimd.memset(xg[1], 0.0).then_inc(S["xg_zero"], 1)
                pool.wait_ge(S["xg_zero"], 2 * l + 2)
                pool.wait_ge(S["route_done"], 2 * l + 1)

                def gather(b, q, done):
                    nc.gpsimd.indirect_dma_start(
                        out=xg[q][0:SLOTS], out_offset=None, in_=xn_dram,
                        in_offset=bass.IndirectOffsetOnAxis(ap=gidx[0:SLOTS, b:b + 1], axis=0),
                        bounds_check=TOK - 1, oob_is_err=False).then_inc(done, 16)

                gather(0, 0, S["xgathered0"])
                gather(1, 1, S["xgathered1"])
                for b in range(2, EXPERTS + 1):
                    pool.wait_ge(S["xg_T"], l * (EXPERTS + 1) + b - 1)
                    gather(b, b % 2, S[f"xgathered{b % 2}"])
                X = extra_signals[l]
                count = pool.value_load(extra_e[0:1, l, EXTRA:EXTRA + 1], min_val=0, max_val=EXTRA)
                for x in range(EXTRA):
                    with pool.If(count > x):
                        if x:
                            pool.wait_ge(X["xg_T"], x)
                        else:
                            pool.wait_ge(S["xg_T"], (l + 1) * (EXPERTS + 1))
                        gather(EXPERTS + x, 0, X["xgathered"])
                if l == 0:
                    for i in range(TILES):
                        L, c0 = LEN[i], AT[i]
                        pool.wait_ge(S["hg_ex"], i + 1)
                        nc.gpsimd.tensor_tensor(hK[i][:, :, 0:L], hk[:, :, c0:c0 + L], hEq[:, :, 0:L], ALU.mult)
                        nc.gpsimd.tensor_tensor(hQ[i][:, :, 0:L], hq[:, :, c0:c0 + L], hE[:, :, 0:L], ALU.mult
                                                ).then_inc(S["hg_in"], 1)

        @block.scalar
        def _(act):
            na = [0]

            def a(ins_):
                na[0] += 1
                ins_.then_inc(S["act_step"], 1)
                act.wait_ge(S["act_step"], na[0])

            def inv_root(out, in_, scale, bias, done):
                a(nc.scalar.activation(out, in_, ACT.Ln, scale=scale, bias=bias))
                nc.scalar.activation(out, out, ACT.Exp, scale=-0.5).then_inc(S[done], 1)

            def squares(n):
                for i in range(TILES):
                    if n == 0:
                        act.wait_ge(S["x_loaded"], 32)
                        act.wait_ge(S["ss_set"], 1)
                    else:
                        act.wait_ge(S["h_ready"], (n - 1) * TILES + i + 1)
                    L = LEN[i]
                    sq_ = nc.scalar.activation(xn[0:L, i, :], h[0:L, i, :], ACT.Square,
                                               accum_out=ss[0:L, n, i:i + 1])
                a(sq_)
                if n == 0:
                    act.wait_ge(S["consts_loaded"], 32)
                inv_root(rstd[:, n, :], ss[:, n, :], 1.0 / D_MODEL, eps, "sq_done")

            squares(0)
            for t in range(CONV_TILES + Z_TILES):
                b = t % 4
                act.wait_ge(S["proj_ps"], t + 1)
                if t < CONV_TILES:
                    nc.scalar.activation(xpad[:, t, TAPS:TAPS + SEQ], ps[:, b, 0:SEQ], ACT.Copy)
                    nc.scalar.activation(xpad[:, t, SEQ + 2 * TAPS:XP], ps[:, b, SEQ:TOK], ACT.Copy
                                         ).then_inc(S["proj_evac"], 1)
                else:
                    nc.scalar.activation(Z[:, t - CONV_TILES, :], ps[:, b, 0:TOK], ACT.Silu
                                         ).then_inc(S["proj_evac"], 1)
                u = t - 2
                if 0 <= u < CONV_TILES:
                    act.wait_ge(S["conv_out"], u + 1)
                    nc.scalar.activation(XC[:, u, :], cvt[:, u % 2, :], ACT.Silu,
                                         bias=vec[:, V_BIAS + u:V_BIAS + u + 1]).then_inc(S["conv_act"], 1)
                if t == AT_SMALL:
                    act.wait_ge(S["small_evac"], 1)
                    nc.scalar.activation(beta[:, :, :], sc[:, :, SCAL:SCAL + 8], ACT.Sigmoid
                                         ).then_inc(S["beta_ready"], 1)
                    nc.scalar.activation(spx[:, 1], spx[:, 0], ACT.Exp, scale=-1.0).then_inc(S["sp_exp1"], 1)
                    nc.scalar.activation(eA[:, :], row[:, R_ALOG:R_ALOG + SCAL], ACT.Exp).then_inc(S["ea_ready"], 1)
                    act.wait_ge(S["sp_pos"], 1)
                    nc.scalar.activation(spx[:, 3], spx[:, 2], ACT.Ln).then_inc(S["sp_ln"], 1)
                if t == AT_DECAY:
                    act.wait_ge(S["conv_act"], CONV_TILES)
                    act.wait_ge(S["xnT_ps"], 6)
                    nc.scalar.activation(sq4, XC[:, 12:16, :], ACT.Square).then_inc(S["sq2_done"], 1)
                if t == AT_QUERY:
                    act.wait_ge(S["nrm_ps"], 1)
                    inv_root(rsq, ps[:, 4:8, 0:XW], float(P), con[:, C_EPSQ:C_EPSQ + 1], "rs_done")
                    nc.scalar.activation(sq4, XC[:, 16:20, :], ACT.Square).then_inc(S["sq2_done"], 1)
                if t == AT_KEY:
                    act.wait_ge(S["nrm_ps"], 2)
                    act.wait_ge(S["nrm_done"], 1)
                    inv_root(rsq, ps[:, 4:8, 0:XW], 1.0, eps, "rs_done")
            for u in range(2 * TILES):
                i = u // 2
                L = LEN[i]
                GB = bank(0, 8, P, n=2)
                act.wait_ge(S["ssd_in"], u + 1)
                if u >= 2:
                    act.wait_ge(S["ssd_upd"], u - 1)
                nc.scalar.activation(EG2[u % 2][:, :, 0:L], GB[:, :, 0:L], ACT.Exp)
                nc.scalar.activation(dec2[u % 2], GB[:, :, L - 1], ACT.Exp).then_inc(S["ssd_exp"], 1)
                act.wait_ge(S["ssd_diff"], 2 * u + 1)
                nc.scalar.activation(Dm[0:L, :, 0:L], Dm[0:L, :, 0:L], ACT.Exp).then_inc(S["ssd_exp"], 1)
                act.wait_ge(S["ssd_diff"], 2 * u + 2)
                nc.scalar.activation(tail[0:L], tail[0:L], ACT.Exp).then_inc(S["ssd_exp"], 1)
            act.wait_ge(S["yg_ready"], 1)
            nc.scalar.activation(uT[:, :, :], cat[:, 0:8, :], ACT.Square).then_inc(S["sq2_done"], 1)
            for i in range(TILES):
                L = LEN[i]
                GB = bank(0, 8, P, n=2)
                act.wait_ge(S["gdn_in"], i + 1)
                if i:
                    act.wait_ge(S["gdn_upd"], i)
                nc.scalar.activation(EG[:, :, 0:L], GB[:, :, 0:L], ACT.Exp)
                nc.scalar.activation(dec, GB[:, :, L - 1], ACT.Exp)
                nc.scalar.activation(ecum[0:L], cum[0:L, i, SSD_HEADS:SCAL], ACT.Exp).then_inc(S["gdn_exp"], 1)
                act.wait_ge(S["gdn_diff"], 2 * i + 1)
                nc.scalar.activation(Dm[0:L, :, 0:L], Dm[0:L, :, 0:L], ACT.Exp).then_inc(S["gdn_exp"], 1)
                act.wait_ge(S["gdn_diff"], 2 * i + 2)
                nc.scalar.activation(tail[0:L], tail[0:L], ACT.Exp).then_inc(S["gdn_exp"], 1)
                act.wait_ge(S["beta_ready"], 1)
                for hd in range(8):
                    nc.scalar.activation(VB[0:L, hd, :], bank(4, 8, P, n=2)[0:L, hd, :], ACT.Copy,
                                         scale=beta[0:L, i, hd:hd + 1])
                nc.scalar.activation(Ktok[0:L], bank(6, 4, P)[0:L], ACT.Copy).then_inc(S["gdn_vb"], 1)
                for n in range(sum(b < L for b in LEVELS)):
                    k = gdn_level(i, n)
                    for f in range(2):
                        act.wait_ge(S["gdn_pe"], 2 * k + f + 1)
                        if k:
                            act.wait_ge(S["gdn_pt"], 2 * k - 1 + f)
                        for j in range(4):
                            hd = 4 * f + j
                            e_ = nc.scalar.activation(P8[0:L, hd, 0:L], bank(4 + f, 4, P)[0:L, j, 0:L], ACT.Copy,
                                                      scale=beta[0:L, i, hd:hd + 1])
                        e_.then_inc(S["gdn_p"], 1)
                    if (i, n) == (0, NORM_LEVEL + 1):
                        act.wait_ge(S["nrm_ps"], 3)
                        act.wait_ge(S["nrm_done"], 2)
                        inv_root(rs0[:, 0:2, 0:TOK], ps[:, 2:4, 0:TOK], 1.0 / 512, eps, "rs_done")
                act.wait_ge(S["gdn_o"], i + 1)
                nc.scalar.activation(cat[:, 8:16, AT[i]:AT[i] + L], bank(2, 8, P, n=2)[:, :, 0:L], ACT.Copy
                                     ).then_inc(S["gdn_out"], 1)

            def head_roots(l, src, rs):
                act.wait_ge(S["yg_ready"], 2 + l)
                for h0, h1 in HEAD_ROUNDS:
                    nc.scalar.activation(uT[:, h0:h1, :], src[:, h0:h1, :], ACT.Square).then_inc(S["sq2_done"], 1)
                for r, (h0, h1) in enumerate(HEAD_ROUNDS):
                    act.wait_ge(S["nrm_ps"], 4 + 3 * l + r)
                    act.wait_ge(S["nrm_done"], 3 + 3 * l + r)
                    inv_root(rs[:, 0:h1 - h0, 0:TOK], ps[:, 5:5 + h1 - h0, 0:TOK], 1.0 / P, eps, "rs_done")

            act.wait_ge(S["gdn_out"], TILES)
            head_roots(0, cat[:, 8:16, :], rs0)

            def moe_act(l):
                squares(2 * l + 1)
                act.wait_ge(S["rt_diff"], 2 * l + 1)
                nc.scalar.activation(rt_ge, rt_ge, ACT.Exp).then_inc(S["rt_exp"], 1)
                act.wait_ge(S["rt_diff"], 2 * l + 2)
                nc.scalar.activation(rt_e2, rt_e2, ACT.Exp).then_inc(S["rt_exp"], 1)
                act.wait_ge(S["route_done"], 2 * l + 2)
                def work(N, q, n):
                    act.wait_ge(N["gate_ps"], n + 1)
                    need(act, N["hid_ready"], n)
                    nc.scalar.activation(sg, bank(2, D_EXP // HALVES), ACT.Silu).then_inc(N["sg_ready"], 1)
                    act.wait_ge(N["hT_ps"], n + 1)
                    need(act, N["y_ps"], n)
                    nc.scalar.activation(hidT, bank(4, KE // HALVES, P), ACT.Copy).then_inc(N["hidT_ready"], 1)
                    act.wait_ge(N["y_ps"], n + 1)
                    for g in range(HALVES):
                        y_ = nc.scalar.activation(yb[SLOTS * q:SLOTS * (q + 1), 512 * g:512 * (g + 1)],
                                                  ps[SLOTS * g:SLOTS * (g + 1), 5, :], ACT.Copy)
                    y_.then_inc(N["y_ready"], 1)

                for b in range(PEELED):
                    work(S, b % 2, l * EXPERTS + b)
                with act.Fori(0, ROUNDS) as i:
                    for j in range(ROUND):
                        s, b, n = looped(l, i, j)
                        work(S, j % 2, n())
                X = extra_signals[l]
                count = act.value_load(extra_e[0:1, l, EXTRA:EXTRA + 1], min_val=0, max_val=EXTRA)
                for x in range(EXTRA):
                    with act.If(count > x):
                        work(X, 0, x)

            moe_act(0)
            squares(2)
            base = CONV_TILES + Z_TILES

            def hg_exps(i, n):
                L, c0, k = LEN[i], AT[i], gdn_level(i, n)
                act.wait_ge(S["hg_d"], k + 1)
                nc.scalar.activation(hD[k % 2][:, :, 0:L], hD[k % 2][:, :, 0:L], ACT.Exp).then_inc(S["hg_e"], 1)
                if n == 1:
                    act.wait_ge(S["hg_x"], i + 1)
                    nc.scalar.activation(hE[:, :, 0:L], hg[:, :, c0:c0 + L], ACT.Exp)
                    nc.scalar.activation(hEq[:, :, 0:L], hEq[:, :, 0:L], ACT.Exp)
                    nc.scalar.activation(hDec[i], hg[:, :, c0 + L - 1], ACT.Exp).then_inc(S["hg_ex"], 1)

            def hg_rows(i):
                L = LEN[i]
                kt, vt = tok_rows[i % 2]
                act.wait_ge(S["hg_tr"], i + 1)
                if i == 1:
                    act.wait_ge(S["hg_in"], TILES)
                elif i == 2:
                    act.wait_ge(S["hg_y"], 1)
                nc.scalar.activation(kt[0:L], bank(4, 8, P, n=2)[0:L], ACT.Copy)
                nc.scalar.activation(vt[0:L], bank(6, 8, P, n=2)[0:L], ACT.Copy).then_inc(S["hg_acc"], 1)

            act.wait_ge(S["decay_in"], 1)
            nc.scalar.activation(lbv[:, 1:3, :], lbv[:, 1:3, :], ACT.Exp).then_inc(S["decay_act"], 1)
            for t in range(4 * HEADS):
                act.wait_ge(S["proj_ps"], base + t + 1)
                part, hd = t // HEADS, t % HEADS
                dst = (hg, hq, hv, hz)[part]
                fn = (ACT.Sigmoid, ACT.Silu, ACT.Copy, ACT.Silu)[part]
                nc.scalar.activation(dst[:, hd, :], ps[:, t % 4, 0:TOK], fn).then_inc(S["proj_evac"], 1)
                if t == AT_FORGET:
                    act.wait_ge(S["decay_in"], 2)
                    nc.scalar.activation(hg, hg, ACT.Ln).then_inc(S["decay_act"], 1)
                for (i, n), at_tile in zip(HG_STEPS, STEP_AT[:1] + STEP_AT):
                    if at_tile == t and n < sum(b < LEN[i] for b in LEVELS):
                        hg_exps(i, n)
            for i in range(TILES):
                L = LEN[i]
                c0 = AT[i]
                if i == 0:
                    hg_rows(0)
                if i + 1 < TILES:
                    hg_rows(i + 1)
                act.wait_ge(S["hg_y"], i + 1)
                nc.scalar.activation(hcat[:, :, c0:c0 + L], bank(2, 8, P, n=2)[:, :, 0:L], ACT.Copy
                                     ).then_inc(S["hg_out"], 1)
            act.wait_ge(S["hg_out"], TILES)
            head_roots(1, hcat, rs1)
            moe_act(1)
            squares(4)

        @block.vector
        def _(dve):
            nv = [0]

            def v(ins_):
                nv[0] += 1
                ins_.then_inc(S["dve_step"], 1)
                dve.wait_ge(S["dve_step"], nv[0])

            V = nc.vector

            def tt(out, a, b, op):
                return V.tensor_tensor(out, a, b, op)

            def bc(ap, *dims):
                return ap.to_broadcast([ap.shape[0], *dims])

            def norm(n):
                for i in range(TILES):
                    L = LEN[i]
                    r = rstd[0:L, n, i:i + 1]
                    dve.wait_ge(S["sq_done"], n + 1)
                    if n < 4:
                        V.tensor_scalar(xn[0:L, i, :], h[0:L, i, :], r, None, ALU.mult).then_inc(S["xn_ready"], 1)
                    else:
                        dve.wait_ge(S["final_loaded"], 16)
                        V.scalar_tensor_tensor(xn[0:L, i, :], h[0:L, i, :], r, final_w[0:L], ALU.mult, ALU.mult
                                               ).then_inc(S["xn_ready"], 1)
                if n == 4:
                    return
                for i in range(TILES):
                    for c in range(2):
                        k = 2 * i + c
                        w = vec[:, V_NORM + KD * n + 4 * c:V_NORM + KD * n + 4 * c + 4]
                        dve.wait_ge(S["xnT_ps"], 6 * n + k + 1)
                        tt(uT[:, 4 * c:4 * c + 4, AT[i]:AT[i] + LEN[i]], bank(4 + k % 4, 4, P)[:, :, 0:LEN[i]],
                           bc(w.unsqueeze(2), 4, LEN[i]), ALU.mult).then_inc(S["uT_ready"], 1)

            V.memset(ss[:, :, :], 1.0).then_inc(S["ss_set"], 1)
            v(V.memset(xpad[:, :, 0:TAPS], 0.0))
            v(V.memset(sc[:, :, :], 0.0))
            v(V.memset(cum[:, :, :], 0.0))
            v(V.memset(LG[:, :, :], 0.0))
            v(V.memset(R2, 0.0))
            dve.wait_ge(S["hist_loaded"], 16)
            v(V.tensor_copy(xpad[:, :, TAPS + SEQ:2 * TAPS + SEQ], conv_st[:, :, :]))
            dve.wait_ge(S["consts_loaded"], 32)
            norm(0)
            for t in range(CONV_TILES):
                wv = lambda j: vec[:, V_CONV + t * CONV_W + j:V_CONV + t * CONV_W + j + 1]
                out = cvt[:, t % 2, :]
                dve.wait_ge(S["proj_evac"], t + 1)
                if t >= 2:
                    dve.wait_ge(S["conv_act"], t - 1)
                v(V.tensor_scalar(out, xpad[:, t, 0:XW], wv(0), None, ALU.mult))
                for j in range(1, CONV_W):
                    op = V.scalar_tensor_tensor(out, xpad[:, t, j:j + XW], wv(j), out, ALU.mult, ALU.add)
                    if j < CONV_W - 1:
                        v(op)
                    else:
                        op.then_inc(S["conv_out"], 1)
            V.tensor_copy(conv_new[:, 0, :, :], xpad[:, :, SEQ:SEQ + TAPS]).then_inc(S["conv_new_ready"], 1)
            V.tensor_copy(conv_new[:, 1, :, :], xpad[:, :, XP - TAPS:XP]).then_inc(S["conv_new_ready"], 1)
            dve.wait_ge(S["small_loaded"], 48)
            for i in range(TILES):
                dve.wait_ge(S["small_ps"], i + 1)
                v(V.tensor_copy(sc[0:LEN[i], i, :], ps[0:LEN[i], 4 + i, 0:32]))
            s24 = sc[:, :, 0:SCAL]
            v(tt(s24, s24, bc(row[:, R_BIAS:R_BIAS + SCAL].unsqueeze(1), TILES, SCAL), ALU.add))
            V.scalar_tensor_tensor(spx[:, 0], s24, -1.0, s24, ALU.mult, ALU.max).then_inc(S["small_evac"], 1)
            dve.wait_ge(S["sp_exp1"], 1)
            e_, w_, d_ = spx[:, 1], spx[:, 2], spx[:, 0]
            V.tensor_scalar(w_, e_, 1.0, None, ALU.add).then_inc(S["sp_pos"], 1)
            dve.wait_ge(S["sp_pos"], 1)
            v(V.tensor_scalar(d_, w_, -1.0, None, ALU.add))
            dve.wait_ge(S["sp_ln"], 1)
            v(tt(spx[:, 3], spx[:, 3], e_, ALU.mult))
            v(V.tensor_scalar(w_, d_, 0.0, None, ALU.is_equal))
            v(tt(e_, e_, w_, ALU.mult))
            v(V.tensor_scalar(d_, d_, 1.0e-30, None, ALU.max))
            v(V.reciprocal(d_, d_))
            v(tt(spx[:, 3], spx[:, 3], d_, ALU.mult))
            v(tt(spx[:, 3], spx[:, 3], e_, ALU.add))
            v(V.scalar_tensor_tensor(dtg[:, :, :], s24, 0.0, spx[:, 3], ALU.max, ALU.add))
            dve.wait_ge(S["ea_ready"], 1)
            V.scalar_tensor_tensor(G24[:, :, :], dtg[:, :, :], -1.0, bc(eA[:, :].unsqueeze(1), TILES, SCAL),
                                   ALU.mult, ALU.mult).then_inc(S["g_ready"], 1)
            dve.wait_ge(S["cum_ps"], 1)
            for i in range(TILES):
                c_ = V.tensor_copy(cum[0:LEN[i], i, :], ps[0:LEN[i], 7, i * 32:i * 32 + SCAL])
                if i < TILES - 1:
                    v(c_)
                else:
                    c_.then_inc(S["cum_ready"], 1)
            dve.wait_ge(S["cum_ready"], 1)
            for r in range(2):
                dve.wait_ge(S["rs_done"], 1 + r)
                x4 = XC[:, 12 + 4 * r:16 + 4 * r, :]
                tt(x4, x4, rsq, ALU.mult).then_inc(S["nrm_done"], 1)

            def ssd_before(u):
                i, g = u // 2, u % 2
                L, x0, c0 = LEN[i], AX[i], AT[i]
                GB = bank(0, 8, P, n=2)
                Xdt, Xtl, Btok, W8, Cs, EG = [two[u % 2] for two in (Xdt2, Xtl2, Btok2, W82, Cs2, EG2)]
                cm = cum[0:L, i, 8 * g:8 * g + 8]
                if u == 4:
                    for c in range(2):
                        dve.wait_ge(S["st_T"], c + 1)
                        v(V.tensor_copy(HT[1][:, c, :], bank(6 + c, 512)))
                    V.engine_nop().then_inc(S["st_Tevac"], 1)
                dve.wait_ge(S["ssd_in"], u + 1)
                v(tt(Xdt[0:L], bank(5, 8, 64)[0:L], bc(dtg[0:L, i, 8 * g:8 * g + 8].unsqueeze(2), 8, 64), ALU.mult))
                v(V.tensor_copy(Btok[0:L], ps[0:L, 6, 0:P]))
                v(tt(BCm[0:L, 0:L], ps[0:L, 2, 0:L], triu[0:L, 0:L], ALU.mult))
                dve.wait_ge(S["ssd_exp"], 3 * u + 1)
                v(tt(Dm[0:L, :, 0:L], GB[0:L, :, 0:L], bc(cm.unsqueeze(2), 8, L), ALU.subtract))
                V.tensor_scalar(Dm[0:L, :, 0:L], Dm[0:L, :, 0:L], 0.0, None, ALU.min).then_inc(S["ssd_diff"], 1)
                tt(tail[0:L], GB[0:L, :, L - 1], cm, ALU.subtract).then_inc(S["ssd_diff"], 1)
                v(tt(Cs[:, :, 0:L], EG[:, :, 0:L], bc(XC[:, 10 + g, x0:x0 + L].unsqueeze(1), 8, L), ALU.mult))
                dve.wait_ge(S["ssd_exp"], 3 * u + 3)
                v(tt(W8[0:L, :, 0:L], Dm[0:L, :, 0:L], bc(BCm[0:L, 0:L].unsqueeze(1), 8, L), ALU.mult))
                tt(Xtl[0:L], Xdt[0:L], bc(tail[0:L].unsqueeze(2), 8, 64), ALU.mult).then_inc(S["ssd_w"], 1)

            def ssd_after(u):
                i, g = u // 2, u % 2
                L, x0, c0 = LEN[i], AX[i], AT[i]
                st, dec = HT[1 if i == 2 else 0], dec2[u % 2]
                dve.wait_ge(S["ssd_y"], u + 1)
                for c in range(4):
                    k = 4 * g + c
                    v(V.scalar_tensor_tensor(cat[:, k, c0:c0 + L], XC[:, k, x0:x0 + L], vec[:, V_D + k:V_D + k + 1],
                                             bank(3, 4, P)[:, c, 0:L], ALU.mult, ALU.add))
                if i == 0:
                    V.tensor_copy(st[:, g, :], bank(4, 512)).then_inc(S["ssd_upd"], 1)
                else:
                    s8 = st[:, g, :].rearrange("p (a b) -> p a b", a=8)
                    v(tt(s8, s8, bc(dec.unsqueeze(2), 8, 64), ALU.mult))
                    tt(st[:, g, :], st[:, g, :], bank(4, 512), ALU.add).then_inc(S["ssd_upd"], 1)
            dve.wait_ge(S["state_in"], 16)
            ssd_before(0)
            for u in range(2 * TILES):
                if u + 1 < 2 * TILES:
                    ssd_before(u + 1)
                ssd_after(u)
            for n in range(2):
                if n:
                    dve.wait_ge(S["states_out"], 48)
                for c in range(2):
                    dve.wait_ge(S["st_T"], 2 + 2 * n + c + 1)
                    k = V.tensor_copy(s_stage[:, 4 * c:4 * c + 4, :], bank(6 + c, 4, P))
                    if c == 0:
                        v(k)
                    else:
                        k.then_inc(S["ssd_final"], 1)
            tt(cat[:, 0:8, :], cat[:, 0:8, :], Z[:, 0:8, :], ALU.mult).then_inc(S["yg_ready"], 1)
            for i in range(TILES):
                L, x0, c0 = LEN[i], AX[i], AT[i]
                st = GS[1 if i == 2 else 0]
                GB = bank(0, 8, P, n=2)
                cm = cum[0:L, i, SSD_HEADS:SCAL]
                dve.wait_ge(S["gdn_in"], i + 1)
                dve.wait_ge(S["gdn_exp"], 3 * i + 1)
                v(tt(Dm[0:L, :, 0:L], GB[0:L, :, 0:L], bc(cm.unsqueeze(2), 8, L), ALU.subtract))
                V.tensor_scalar(Dm[0:L, :, 0:L], Dm[0:L, :, 0:L], 0.0, None, ALU.min).then_inc(S["gdn_diff"], 1)
                tt(tail[0:L], GB[0:L, :, L - 1], cm, ALU.subtract).then_inc(S["gdn_diff"], 1)
                dve.wait_ge(S["gdn_exp"], 3 * i + 2)
                v(tt(Dm[0:L, :, 0:L], Dm[0:L, :, 0:L], bc(triu[0:L, 0:L].unsqueeze(1), 8, L), ALU.mult))
                pair = lambda ap: ap.rearrange("p (a b) c -> p a b c", b=2)
                tt(pair(DKK[0:L])[:, :, :, 0:L], pair(Dm[0:L])[:, :, :, 0:L],
                   bc(bank(2, 4, P)[0:L, :, 0:L].unsqueeze(2), 4, 2, L), ALU.mult).then_inc(S["gdn_mats"], 1)
                v(tt(pair(DQK[0:L])[:, :, :, 0:L], pair(Dm[0:L])[:, :, :, 0:L],
                     bc(bank(3, 4, P)[0:L, :, 0:L].unsqueeze(2), 4, 2, L), ALU.mult))
                if i == 0:
                    dve.wait_ge(S["beta_ready"], 1)
                v(V.scalar_tensor_tensor(nbe[0:L], beta[0:L, i, :], -1.0, ecum[0:L], ALU.mult, ALU.mult))
                lv = [n for n, b in enumerate(LEVELS) if b < L]
                for n in range(len(lv)):
                    k = gdn_level(i, n)
                    for f in range(2):
                        hh = slice(4 * f, 4 * f + 4)
                        dve.wait_ge(S["gdn_pt"], 2 * k + f + 1)
                        if n < len(lv) - 1:
                            TP = bank(6 + f, 4, P)[0:L, :, 0:L] if n else P8[0:L, hh, 0:L]
                            tt(T8[0:L, hh, 0:L], T8[0:L, hh, 0:L], TP, ALU.subtract)
                        tt(TT8[0:L, hh, 0:L], TT8[0:L, hh, 0:L], bank(f, 4, P)[0:L, :, 0:L], ALU.subtract
                           ).then_inc(S["gdn_tu"], 1)
                    if (i, n) == (0, NORM_LEVEL + 2):
                        dve.wait_ge(S["rs_done"], 3)
                        c4 = cat[:, 0:8, :].rearrange("p (g c) t -> p g c t", g=2)
                        v(tt(c4, c4, bc(rs0[:, 0:2, 0:TOK].unsqueeze(2), 2, 4, TOK), ALU.mult))
                    if (i, n) == (0, NORM_LEVEL + 3):
                        tt(cat[:, 0:8, :], cat[:, 0:8, :], bc(vec[:, V_SNORM:V_SNORM + 8].unsqueeze(2), 8, TOK), ALU.mult
                           ).then_inc(S["nrm_done"], 1)
                k = gdn_level(i, len(lv))
                dve.wait_ge(S["gdn_pt"], 2 * k)
                if i > 0:
                    dve.wait_ge(S["gdn_ks"], i)
                    v(tt(RHS[0:L], bank(4, 8, P, n=2)[0:L], bc(nbe[0:L].unsqueeze(2), 8, P), ALU.mult))
                    tt(RHS[0:L], RHS[0:L], VB[0:L], ALU.add).then_inc(S["gdn_rhs"], 1)
                else:
                    V.tensor_copy(RHS[0:L], VB[0:L]).then_inc(S["gdn_rhs"], 1)
                dve.wait_ge(S["gdn_u"], i + 1)
                V.tensor_copy(U8[0:L], bank(6, 8, P, n=2)[0:L]).then_inc(S["gdn_ue"], 1)
                dve.wait_ge(S["gdn_o"], i + 1)
                if i == 0:
                    V.tensor_copy(st, bank(4, 8, P, n=2)).then_inc(S["gdn_upd"], 1)
                else:
                    v(tt(st, st, bc(dec.unsqueeze(2), 8, P), ALU.mult))
                    tt(st, st, bank(4, 8, P, n=2), ALU.add).then_inc(S["gdn_upd"], 1)

            def head_norm(l, x, z, rs, w):
                V.engine_nop().then_inc(S["yg_ready"], 1)
                for r, (h0, h1) in enumerate(HEAD_ROUNDS):
                    xr = x[:, h0:h1, :]
                    dve.wait_ge(S["rs_done"], 4 + 3 * l + r)
                    tt(xr, xr, rs[:, 0:h1 - h0, 0:TOK], ALU.mult).then_inc(S["nrm_done"], 1)
                    dve.wait_ge(S["nrm_done"], 4 + 3 * l + r)
                    V.scalar_tensor_tensor(flat(xr), flat(xr), w, flat(z[:, h0:h1, :]), ALU.mult, ALU.mult
                                           ).then_inc(S["cat_ready"], 1)

            def flat(ap):
                return ap.rearrange("p a b -> p (a b)")

            dve.wait_ge(S["gdn_upd"], TILES)
            head_norm(0, cat[:, 8:16, :], Z[:, 8:16, :], rs0, vec[:, V_GNORM:V_GNORM + 1])

            def residual(groups, n):
                dve.wait_ge(S["out_ps"], groups)
                for i in range(2):
                    tt(h[:, i, :], h[:, i, :], bank(2 * i, D_MODEL, n=2), ALU.add).then_inc(S["h_ready"], 1)
                for j in range(4):
                    t_ = tt(h[0:DEC_SEQ, 2, 256 * j:256 * j + 256], h[0:DEC_SEQ, 2, 256 * j:256 * j + 256],
                            ps[32 * j:32 * j + 32, 4, 0:256], ALU.add)
                t_.then_inc(S["h_ready"], 1)

            residual(4, 0)

            def route(l):
                B = lambda ap, *d: bc(ap, *d)
                dve.wait_ge(S["lg_ps"], l + 1)
                for i in range(TILES):
                    v(V.tensor_copy(LG[0:LEN[i], i, :], ps[0:LEN[i], 0, i * 64:i * 64 + 36]))
                v(V.memset(gl8, -3.0e38))
                v(V.tensor_copy(gl8[:, :, 0:4], LG[:, :, 0:4]))
                for i in range(TILES):
                    v(V.max(gm8[:, i, :], gl8[:, i, :]))
                    v(V.max_index(gi8[:, i, :], gm8[:, i, :], gl8[:, i, :]))
                v(V.tensor_copy(gif, gi8[:, :, 0:1]))
                tt(rt_ge, LG[:, :, 0:4], B(gm8[:, :, 0:1], 3, 4), ALU.subtract).then_inc(S["rt_diff"], 1)
                v(tt(ohg, B(iota[:, 0:4].unsqueeze(1), 3, 4), B(gif, 3, 4), ALU.is_equal))
                s4 = selm.rearrange("p i (g j) -> p i g j", g=4)
                v(tt(s4, LG[:, :, 4:36].rearrange("p i (g j) -> p i g j", g=4), B(ohg.unsqueeze(3), 3, 4, 8), ALU.mult))
                v(V.tensor_reduce(esel, selm.rearrange("p i (g j) -> p i j g", g=4), AX_X, ALU.add))
                for i in range(TILES):
                    v(V.max(ev8[:, i, :], esel[:, i, :]))
                    v(V.max_index(ei8[:, i, :], ev8[:, i, :], esel[:, i, :]))
                v(V.tensor_copy(eif, ei8[:, :, 0:2]))
                tt(rt_e2, ev8[:, :, 1:2], ev8[:, :, 0:1], ALU.subtract).then_inc(S["rt_diff"], 1)
                v(V.tensor_scalar(sgm, gif, float(E_PER), None, ALU.mult))
                v(tt(eid, eif, B(sgm, 3, 2), ALU.add))
                v(tt(O2, B(iota[:, 0:32].unsqueeze(1).unsqueeze(1), 3, 2, 32), B(eid.unsqueeze(3), 3, 2, 32), ALU.is_equal))
                tt(A2, O2[:, :, 0, :], O2[:, :, 1, :], ALU.add).then_inc(S["rt_A"], 1)
                dve.wait_ge(S["rt_exp"], 2 * l + 2)
                v(V.tensor_reduce(sgm, rt_ge, AX_X, ALU.add))
                v(V.tensor_scalar(den, rt_e2, 1.0, None, ALU.add))
                v(tt(den, den, sgm, ALU.mult))
                v(V.reciprocal(gates[:, :, 0:1], den))
                v(tt(gates[:, :, 1:2], gates[:, :, 0:1], rt_e2, ALU.mult))
                dve.wait_ge(S["rt_R"], l + 1)
                for i in range(TILES):
                    v(V.tensor_copy(R2[0:LEN[i], i, :], ps[0:LEN[i], 1, i * 32:i * 32 + 32]))
                v(V.tensor_copy(cnt, ps[:, 1, 96:128]))
                v(V.tensor_scalar(nx, cnt, float(SLOTS), None, ALU.is_gt))
                for full in range(2 * SLOTS, TOK, SLOTS):
                    v(V.scalar_tensor_tensor(nx, cnt, float(full), nx, ALU.is_gt, ALU.add))
                v(V.tensor_tensor_scan(incl, ones[:, 0:32], nx, 0.0, ALU.mult, ALU.add))
                v(tt(exb, incl, nx, ALU.subtract))
                v(V.tensor_scalar(over, R2, float(SLOTS) - 0.5, None, ALU.is_gt))
                v(V.tensor_scalar(exb, exb, float(SLOTS), float(SLOTS * (EXPERTS - 1)), ALU.mult, ALU.add))
                v(V.tensor_scalar(cnt, iota[:, 0:32], float(SLOTS), None, ALU.mult))
                v(tt(exb, exb, cnt, ALU.subtract))
                v(tt(extb, over, B(exb.unsqueeze(1), 3, 32), ALU.mult))
                v(tt(R2, R2, extb, ALU.add))
                v(tt(R2, R2, B(cnt.unsqueeze(1), 3, 32), ALU.add))
                v(tt(OD, O2, B(R2.unsqueeze(2), 3, 2, 32), ALU.mult))
                v(V.tensor_reduce(pos.rearrange("p (a b) -> p a b", a=3), OD, AX_X, ALU.add))
                v(V.tensor_copy(posi[:, 0, :], pos))
                v(V.tensor_scalar(posi[:, 1, :], posi[:, 0, :], SLOTS - 1, None, ALU.bitwise_and))
                v(V.tensor_scalar(posi[:, 2, :], posi[:, 0, :], SHIFT, None, ALU.logical_shift_right))
                v(V.tensor_copy(p1f, posi[:, 1, :]))
                v(V.tensor_copy(b1f, posi[:, 2, :]))
                v(tt(OPm, B(con[:, C_SLOT:C_SLOT + P].unsqueeze(1), 6, P), B(p1f.unsqueeze(2), 6, P), ALU.is_equal))
                tc = lambda ap: ap.rearrange("p (i c) s -> p i c s", c=2)
                v(tt(OBg, B(iota[:, 0:COLS].unsqueeze(1), 6, COLS), B(b1f.unsqueeze(2), 6, COLS), ALU.is_equal))
                tt(tc(OBm), tc(OBg), B(con[:, C_VAL:C_VAL + TILES].unsqueeze(2).unsqueeze(3), TILES, 2, COLS), ALU.mult
                   ).then_inc(S["rt_OH"], 1)
                tt(tc(OBg), tc(OBg), B(gates[:, :, :].unsqueeze(3), TILES, 2, COLS), ALU.mult).then_inc(S["rt_OH"], 1)
                v(tt(cmp[0:1], B(incl[0:1].unsqueeze(1), EXTRA, 32), B(iota[0:1, 0:EXTRA].unsqueeze(2), EXTRA, 32), ALU.is_le))
                v(V.tensor_reduce(xe[0:1, 0:EXTRA], cmp[0:1], AX_X, ALU.add))
                v(V.tensor_scalar(xe[0:1, 0:EXTRA], xe[0:1, 0:EXTRA], float(EXPERTS - 1), float(l * EXPERTS),
                                  ALU.min, ALU.add))
                v(V.tensor_copy(xe[0:1, EXTRA:EXTRA + 1], incl[0:1, 31:32]))
                v(V.tensor_copy(extra_e[0:1, l, :], xe[0:1]))
                dve.wait_ge(S["rt_tab"], 2 * l + 1)
                v(V.tensor_scalar(none, ps[:, 2, 0:COLS], 0.5, NOWHERE, ALU.is_lt, ALU.mult))
                v(V.tensor_scalar(slot_token[:, :], ps[:, 2, 0:COLS], -1.0, None, ALU.add))
                v(tt(rows, slot_token[:, :], none, ALU.add))
                V.tensor_copy(gidx[:, :], rows).then_inc(S["route_done"], 1)
                dve.wait_ge(S["rt_tab"], 2 * l + 2)
                V.tensor_copy(slot_gate[:, :], ps[:, 3, 0:COLS]).then_inc(S["route_done"], 1)
                dve.wait_ge(S["route_done"], 2 * l + 2)

            def moe_dve(l):
                if l:
                    v(V.memset(R2, 0.0))
                route(l)
                nw = vec[:, V_NORM + KD * (2 * l + 1):V_NORM + KD * (2 * l + 2)]

                for r in range(TILES):
                    v(V.tensor_scalar(tokens[:, AT[r]:AT[r] + LEN[r]], iota[:, 0:LEN[r]], float(AT[r]), None, ALU.add))
                if l == 0:
                    V.memset(none, 0.0).then_inc(S["h_added"], AHEAD)

                def weigh(N, q, b):
                    r = slice(SLOTS * q, SLOTS * (q + 1))
                    V.tensor_scalar(weight[r], tokens[r], slot_token[r, bass.ds(b, 1)], slot_gate[r, bass.ds(b, 1)],
                                    ALU.is_equal, ALU.mult).then_inc(N["weight_ready"], 1)

                def xT_evac(N, n):
                    dve.wait_ge(N["xg_T"], n + 1)
                    tt(xT, bank(0, KD, SLOTS), bc(nw.unsqueeze(2), KD, SLOTS), ALU.mult).then_inc(N["xT_ready"], 1)

                def gated(N, n):
                    dve.wait_ge(N["up_ps"], n + 1)
                    dve.wait_ge(N["sg_ready"], n + 1)
                    tt(hid, sg, bank(3, D_EXP // HALVES), ALU.mult).then_inc(N["hid_ready"], 1)

                def add(N, n3, t, b=6):
                    dve.wait_ge(N["placed_ps"], n3 + (t + 1))
                    tt(h[0:LEN[t], t, :], h[0:LEN[t], t, :], bank(b, D_MODEL, n=2)[0:LEN[t]], ALU.add
                       ).then_inc(N["h_added"], 1)

                def one(q, b, n, first=False):
                    ends = q == 0 and not first
                    if ends:
                        dve.wait_ge(S["h_added"], n(1.5) - 3 + AHEAD)
                        add(S, n(1.5) - 3, 0)
                    need(dve, S["hT_ps"], n())
                    gated(S, n())
                    if ends:
                        add(S, n(1.5) - 3, 1)
                    xT_evac(S, n() + (l + 1))
                    if ends:
                        add(S, n(1.5) - 3, 2)
                    weigh(S, q, b)

                xT_evac(S, l * (EXPERTS + 1))
                for b in range(PEELED):
                    _, _, n = peeled(l, b)
                    one(b, b, n, first=(b == 0))
                with dve.Fori(0, ROUNDS) as i:
                    for j in range(ROUND):
                        _, b, n = looped(l, i, j)
                        one(j % 2, b, n)
                before = 3 * ((l + 1) * EXPERTS // 2 - 1)
                dve.wait_ge(S["h_added"], before + AHEAD)
                for t in range(TILES):
                    add(S, before, t, LAST_BANKS[t])
                X = extra_signals[l]
                count = dve.value_load(extra_e[0:1, l, EXTRA:EXTRA + 1], min_val=0, max_val=EXTRA)
                dve.wait_ge(S["h_added"], before + 3 + AHEAD)
                for x in range(EXTRA):
                    with dve.If(count > x):
                        weigh(X, 0, EXPERTS + x)
                        xT_evac(X, x)
                        gated(X, x)
                        for t in range(TILES):
                            add(X, 3 * x, t)
                        dve.wait_ge(X["h_added"], 3 * x + 3)
                V.memset(none, 0.0).then_inc(S["h_ready"], TILES)

            norm(1)
            moe_dve(0)

            norm(2)
            lg = vec[:, V_LB:V_LB + 16].rearrange("p (a b) -> p a b", a=2)
            v(tt(lbv[:, 0, :], lg[:, 0], lg[:, 1], ALU.max))
            tt(lbv[:, 1:3, :], lg, bc(lbv[:, 0:1, :], 2, HEADS), ALU.subtract).then_inc(S["decay_in"], 1)
            dve.wait_ge(S["decay_act"], 1)
            v(tt(lbv[:, 3, :], lbv[:, 1, :], lbv[:, 2, :], ALU.add))
            v(V.reciprocal(lbv[:, 3, :], lbv[:, 3, :]))
            v(tt(lbv[:, 1:3, :], lbv[:, 1:3, :], bc(lbv[:, 3:4, :], 2, HEADS), ALU.mult))
            v(tt(lbv[:, 4, :], lbv[:, 1, :], lbv[:, 2, :], ALU.add))
            v(tt(lbv[:, 4, :], lbv[:, 4, :], lbv[:, 1, :], ALU.subtract))
            v(V.tensor_scalar(lbv[:, 5, :], lbv[:, 4, :], -1.0, 1.0, ALU.mult, ALU.add))
            dve.wait_ge(S["proj_evac"], CONV_TILES + Z_TILES + HEADS)
            v(tt(hg, hg, bc(lbv[:, 5, :].unsqueeze(2), HEADS, TOK), ALU.mult))
            v(tt(hg, hg, bc(lbv[:, 4, :].unsqueeze(2), HEADS, TOK), ALU.add))
            V.tensor_scalar(hk, hg, -1.0, 1.0, ALU.mult, ALU.add).then_inc(S["decay_in"], 1)
            dve.wait_ge(S["decay_act"], 2)
            for hd in range(HEADS):
                v(V.tensor_tensor_scan(hg[:, hd, :], con[:, C_SCAN:C_SCAN + TOK], hg[:, hd, :], 0.0,
                                       ALU.mult, ALU.add))
            for i in range(TILES):
                L, c0 = LEN[i], AT[i]
                v(V.memset(hA[i], 0.0))
                if i == 0:
                    dve.wait_ge(S["proj_evac"], CONV_TILES + Z_TILES + 2 * HEADS)
                lv = [n for n, b in enumerate(LEVELS) if b < L]

                def halves(ap, b):
                    w_ = ap.rearrange("p a (n c) -> p a n c", c=2 * b)
                    return w_[:, :, :, 0:b], w_[:, :, :, b:2 * b]

                def to_middle(n):
                    b, k = LEVELS[n], gdn_level(i, n)
                    (glo, ghi), (lo, hi) = halves(hg[:, :, c0:c0 + L], b), halves(hD[k % 2][:, :, 0:L], b)
                    mid = bc(glo[:, :, :, b - 1:b], 8, L // (2 * b), b)
                    need(dve, S["hg_qk"], k - 1)
                    tt(lo, mid, glo, ALU.subtract)
                    tt(hi, ghi, mid, ALU.subtract).then_inc(S["hg_d"], 1)

                def scaled(n):
                    b, k = LEVELS[n], gdn_level(i, n)
                    dve.wait_ge(S["hg_e"], k + 1)
                    (klo, _), (_, qhi) = halves(hk[:, :, c0:c0 + L], b), halves(hq[:, :, c0:c0 + L], b)
                    (dlo, dhi), (rlo, rhi) = halves(hD[k % 2][:, :, 0:L], b), halves(hR[k % 2][:, :, 0:L], b)
                    tt(rlo, klo, dlo, ALU.mult)
                    tt(rhi, qhi, dhi, ALU.mult).then_inc(S["hg_qk"], 1)

                def keep(n):
                    m = gdn_level(i, n) + i
                    msk = ident if n == 0 else mask(n - 1)
                    dve.wait_ge(S["hg_att"], m + 1)
                    need(dve, S["hg_keep"], m)
                    V.copy_predicated(hA[i][0:L, :, 0:L], bc(msk[0:L, 0:L].bitcast(U32).unsqueeze(1), 8, L),
                                      bank(step_bank(m), 8, P, n=2)[0:L, :, 0:L]).then_inc(S["hg_keep"], 1)

                to_middle(0)
                for n in range(len(lv)):
                    if n + 1 < len(lv):
                        to_middle(n + 1)
                    if n == 0:
                        need(dve, S["hg_in"], i)
                        tt(hEq[:, :, 0:L], bc(hg[:, :, c0 + L - 1:c0 + L], 8, L), hg[:, :, c0:c0 + L], ALU.subtract
                           ).then_inc(S["hg_x"], 1)
                    scaled(n)
                    keep(n)
                keep(len(lv))
            for i in range(TILES):
                st = hS[1 if i == 2 else 0]
                if i == 2:
                    dve.wait_ge(S["state_loaded"], 32)
                dve.wait_ge(S["hg_y"], i + 1)
                if i == 0:
                    V.tensor_copy(st, bank(0, 8, P, n=2)).then_inc(S["hg_upd"], 1)
                else:
                    v(tt(st, st, bc(hDec[i].unsqueeze(2), 8, P), ALU.mult))
                    tt(st, st, bank(0, 8, P, n=2), ALU.add).then_inc(S["hg_upd"], 1)
            dve.wait_ge(S["hg_upd"], TILES)
            dve.wait_ge(S["hg_out"], TILES)
            head_norm(1, hcat, hz, rs1, vec[:, V_HNORM:V_HNORM + 1])
            residual(6, 2)
            norm(3)
            moe_dve(1)
            norm(4)

        @block.tensor
        def _(pe):
            MM = nc.tensor.matmul

            def norm(n):
                for i in range(TILES):
                    pe.wait_ge(S["xn_ready"], n * TILES + i + 1)
                    L = LEN[i]
                    for c in range(2):
                        k = 2 * i + c
                        if k >= 4:
                            pe.wait_ge(S["uT_ready"], 6 * n + k - 3)
                        for j in range(4):
                            t_ = nc.tensor.transpose(bank(4 + k % 4, 4, P)[:, j, 0:L],
                                                     xn[0:L, i, 4 * c + j::KD], ident[0:L, 0:L])
                        t_.then_inc(S["xnT_ps"], 1)

            def project(tiles, first, group, between):
                for t in range(tiles):
                    s = (t // 4) % 3
                    if t % 4 == 0:
                        pe.wait_ge(S[f"ring{s}"], 16 * (ring_use(group, t // 4)))
                    if t >= 4:
                        pe.wait_ge(S["proj_evac"], first + t - 3)
                    for k in range(KD):
                        m_ = MM(ps[:, t % 4, 0:TOK], ring[s][:, k, (t % 4) * P:(t % 4 + 1) * P], uT[:, k, :],
                                start=(k == 0), stop=(k == KD - 1))
                    m_.then_inc(S["proj_ps"], 1)
                    between(t)

            def small_steps(t):
                if t == AT_SMALL:
                    pe.wait_ge(S["small_loaded"], 48)
                    for i in range(TILES):
                        for k in range(KD):
                            m_ = MM(ps[0:LEN[i], 4 + i, 0:32], uT[:, k, AT[i]:AT[i] + LEN[i]], wsm[:, k, :],
                                    start=(k == 0), stop=(k == KD - 1))
                        m_.then_inc(S["small_ps"], 1)
                elif t == AT_DECAY:
                    pe.wait_ge(S["g_ready"], 1)
                    for i in range(TILES):
                        m_ = MM(ps[0:LEN[i], 7, i * 32:i * 32 + SCAL], triu[0:LEN[i], 0:LEN[i]],
                                G24[0:LEN[i], i, :], start=True, stop=True)
                    m_.then_inc(S["cum_ps"], 1)
                elif t == AT_QUERY:
                    pe.wait_ge(S["cum_ready"], 1)
                    channel_sums(1)
                elif t == AT_KEY:
                    pe.wait_ge(S["rs_done"], 1)
                    channel_sums(2)

            def channel_sums(n):
                pe.wait_ge(S["sq2_done"], n)
                for c in range(4):
                    m_ = MM(ps[:, 4 + c, 0:XW], ones, sq4[:, c, :], start=True, stop=True)
                m_.then_inc(S["nrm_ps"], 1)

            def decays(i, h0):
                L = LEN[i]
                for hd in range(8):
                    m_ = MM(bank(0, 8, P, n=2)[:, hd, 0:L], G24[0:L, i, h0 + hd:h0 + hd + 1].to_broadcast([L, P]),
                            triu[0:L, 0:L], start=True, stop=True)
                return m_

            pe.wait_ge(S["consts_loaded"], 32)
            norm(0)
            pe.wait_ge(S["uT_ready"], 6)
            project(CONV_TILES + Z_TILES, 0, 0, small_steps)
            pe.wait_ge(S["proj_evac"], CONV_TILES + Z_TILES)
            pe.wait_ge(S["nrm_done"], 2)
            def ssd_first(u):
                i, g = u // 2, u % 2
                L, x0 = LEN[i], AX[i]
                if u:
                    pe.wait_ge(S["ssd_exp"], 3 * u - 2)
                    pe.wait_ge(S["ssd_diff"], 2 * u)
                if u == 4:
                    pe.wait_ge(S["state_in"], 16)
                    for c in range(2):
                        for j in range(4):
                            t_ = nc.tensor.transpose(bank(6 + c, 4, P)[:, j, :], s_load[:, 4 * c + j, :], ident)
                        t_.then_inc(S["st_T"], 1)
                    pe.wait_ge(S["st_Tevac"], 1)
                decays(i, 8 * g)
                for c in range(4):
                    nc.tensor.transpose(bank(5, 4, P)[0:L, c, :], XC[:, 4 * g + c, x0:x0 + L], ident)
                nc.tensor.transpose(ps[0:L, 6, 0:P], XC[:, 8 + g, x0:x0 + L], ident)
                MM(ps[0:L, 2, 0:L], XC[:, 8 + g, x0:x0 + L], XC[:, 10 + g, x0:x0 + L], start=True, stop=True
                   ).then_inc(S["ssd_in"], 1)

            ssd_first(0)
            for u in range(2 * TILES):
                i, g = u // 2, u % 2
                L = LEN[i]
                st = HT[1 if i == 2 else 0]
                Xdt, Xtl, Btok, W8, Cs = [two[u % 2] for two in (Xdt2, Xtl2, Btok2, W82, Cs2)]
                if u + 1 < 2 * TILES:
                    ssd_first(u + 1)
                pe.wait_ge(S["ssd_w"], u + 1)
                if u:
                    pe.wait_ge(S["ssd_upd"], u)
                for hd in range(8):
                    lo = 64 * (hd % 2)
                    out = bank(3, 4, P)[lo:lo + 64, hd // 2, 0:L]
                    MM(out, Xdt[0:L, hd, :], W8[0:L, hd, 0:L], start=True, stop=(i == 0))
                    if i:
                        MM(out, st[:, g, 64 * hd:64 * hd + 64], Cs[:, hd, 0:L], start=False, stop=True)
                MM(bank(4, 512), Btok[0:L], Xtl[0:L].rearrange("p a b -> p (a b)"), start=True, stop=True
                   ).then_inc(S["ssd_y"], 1)
            pe.wait_ge(S["ssd_upd"], 2 * TILES)
            for n in range(2):
                for c in range(2):
                    if n:
                        pe.wait_ge(S["ssd_final"], n)
                    for j in range(4):
                        t_ = nc.tensor.transpose(bank(6 + c, 4, P)[:, j, :], HT[n][:, c, P * j:P * j + P], ident)
                    t_.then_inc(S["st_T"], 1)
            pe.wait_ge(S["ssd_final"], 2)
            for i in range(TILES):
                L, x0 = LEN[i], AX[i]
                st = GS[1 if i == 2 else 0]
                if i:
                    pe.wait_ge(S["gdn_upd"], i)
                    pe.wait_ge(S["gdn_out"], i)
                if i == 0:
                    decays(0, SSD_HEADS)
                for j in range(4):
                    kk = XC[:, 16 + j, x0:x0 + L]
                    MM(bank(2, 4, P)[0:L, j, 0:L], kk, kk, start=True, stop=True)
                    MM(bank(3, 4, P)[0:L, j, 0:L], kk, XC[:, 12 + j, x0:x0 + L], start=True, stop=True)
                    nc.tensor.transpose(bank(6, 4, P)[0:L, j, :], kk, ident)
                for hd in range(8):
                    t_ = nc.tensor.transpose(bank(4, 8, P, n=2)[0:L, hd, :], XC[:, 20 + hd, x0:x0 + L], ident)
                t_.then_inc(S["gdn_in"], 1)
                lv = [n for n, b in enumerate(LEVELS) if b < L]
                for n in range(len(lv)):
                    k = gdn_level(i, n)
                    if n == 0:
                        pe.wait_ge(S["gdn_unit"], i + 1)
                        pe.wait_ge(S["gdn_vb"], i + 1)
                    pe.wait_ge(S["gdn_bm"], k + 1)
                    for f in range(2):
                        if k:
                            pe.wait_ge(S["gdn_tu"], 2 * k - 1 + f)
                        for j in range(4):
                            hd = 4 * f + j
                            m_ = MM(bank(4 + f, 4, P)[0:L, j, 0:L], Bm[k % 2][0:L, hd, 0:L], T8[0:L, hd, 0:L],
                                    start=True, stop=True)
                        m_.then_inc(S["gdn_pe"], 1)
                    for f in range(2):
                        pe.wait_ge(S["gdn_p"], 2 * k + f + 1)
                        if 0 < n < len(lv) - 1:
                            for j in range(4):
                                hd = 4 * f + j
                                MM(bank(6 + f, 4, P)[0:L, j, 0:L], TT8[0:L, hd, 0:L], P8[0:L, hd, 0:L],
                                   start=True, stop=True)
                        for j in range(4):
                            hd = 4 * f + j
                            m_ = MM(bank(f, 4, P)[0:L, j, 0:L], P8[0:L, hd, 0:L], TT8[0:L, hd, 0:L],
                                    start=True, stop=True)
                        m_.then_inc(S["gdn_pt"], 1)
                    if (i, n) == (0, NORM_LEVEL):
                        pe.wait_ge(S["sq2_done"], 3)
                        for g in range(2):
                            for c in range(4):
                                m_ = MM(ps[:, 2 + g, 0:TOK], ones, uT[:, 4 * g + c, :], start=(c == 0), stop=(c == 3))
                        m_.then_inc(S["nrm_ps"], 1)
                k = gdn_level(i, len(lv))
                if i > 0:
                    if i == 2:
                        pe.wait_ge(S["state_loaded"], 16)
                    for hd in range(8):
                        m_ = MM(bank(4, 8, P, n=2)[0:L, hd, :], XC[:, 16 + hd // 2, x0:x0 + L], st[:, hd, :],
                                start=True, stop=True)
                    m_.then_inc(S["gdn_ks"], 1)
                pe.wait_ge(S["gdn_tu"], 2 * k)
                if i + 1 < TILES:
                    decays(i + 1, SSD_HEADS)
                pe.wait_ge(S["gdn_rhs"], i + 1)
                for hd in range(8):
                    m_ = MM(bank(6, 8, P, n=2)[0:L, hd, :], TT8[0:L, hd, 0:L], RHS[0:L, hd, :], start=True, stop=True)
                m_.then_inc(S["gdn_u"], 1)
                pe.wait_ge(S["gdn_ue"], i + 1)
                pe.wait_ge(S["gdn_side"], i + 1)
                pe.wait_ge(S["rs_done"], 3)
                for hd in range(8):
                    out = bank(2, 8, P, n=2)[:, hd, 0:L]
                    MM(out, U8[0:L, hd, :], DQK[0:L, hd, 0:L], start=True, stop=(i == 0))
                    if i:
                        MM(out, st[:, hd, :], qs[:, hd, 0:L], start=False, stop=True)
                for hd in range(8):
                    m_ = MM(bank(4, 8, P, n=2)[:, hd, :], Kt[0:L, hd, :], U8[0:L, hd, :], start=True, stop=True)
                m_.then_inc(S["gdn_o"], 1)

            def round_sums(l, r):
                pe.wait_ge(S["sq2_done"], 4 + 3 * l + r)
                if r:
                    pe.wait_ge(S["rs_done"], 3 + 3 * l + r)
                h0, h1 = HEAD_ROUNDS[r]
                for hd in range(h0, h1):
                    m_ = MM(ps[:, 5 + hd - h0, 0:TOK], ones, uT[:, hd, :], start=True, stop=True)
                m_.then_inc(S["nrm_ps"], 1)

            def out_steps_0(g, c):
                if (g, c) == (0, 2):
                    round_sums(0, 1)
                elif (g, c) == (1, 1):
                    round_sums(0, 2)
                elif (g, c) == (2, 0):
                    pe.wait_ge(S["cat_ready"], 2)
                elif (g, c) == (3, 0):
                    pe.wait_ge(S["cat_ready"], 3)

            def out_steps_1(g, c):
                for r, (h0, h1) in enumerate(HEAD_ROUNDS):
                    if 4 * g + c == h0:
                        if r + 1 < len(HEAD_ROUNDS):
                            round_sums(1, r + 1)
                        pe.wait_ge(S["cat_ready"], 4 + r)

            round_sums(0, 0)

            def project_out(src, groups, first, between):
                for g in range(groups):
                    pe.wait_ge(S[f"out_loaded{g % 3}"], 16 * out_use(first, g))
                    w = ring[g % 3].rearrange("p a b -> p (a b)").rearrange("p (c d) -> p c d", c=4)
                    for c in range(4):
                        k = 4 * g + c
                        between(g, c)
                        for i in range(2):
                            for n in range(2):
                                MM(ps[:, 2 * i + n, :], src[:, k, AT[i]:AT[i] + P],
                                   w[:, c, 512 * n:512 * n + 512], start=(k == 0), stop=(k == 4 * groups - 1))
                    for c in range(4):
                        k = 4 * g + c
                        for j in range(4):
                            m_ = MM(ps[32 * j:32 * j + 32, 4, 0:256], src[:, k, AT[2]:AT[2] + DEC_SEQ],
                                    w[:, c, 256 * j:256 * j + 256], start=(k == 0), stop=(k == 4 * groups - 1))
                    m_.then_inc(S["out_ps"], 1)

            pe.wait_ge(S["nrm_done"], 3)
            project_out(cat, 4, 0, out_steps_0)

            def moe_pe(l):
                for i in range(TILES):
                    pe.wait_ge(S["uT_ready"], 6 * (2 * l + 1) + 2 * (i + 1))
                    for k in range(KD):
                        m_ = MM(ps[0:LEN[i], 0, i * 64:i * 64 + 36], uT[:, k, AT[i]:AT[i] + LEN[i]], wrt[:, l, k, :],
                                start=(k == 0), stop=(k == KD - 1))
                m_.then_inc(S["lg_ps"], 1)
                pe.wait_ge(S["rt_A"], l + 1)
                for i in range(TILES):
                    L = LEN[i]
                    for j in range(i):
                        MM(ps[0:L, 1, i * 32:i * 32 + 32], ones[:, 0:L], A2[:, j, :], start=(j == 0), stop=False)
                    MM(ps[0:L, 1, i * 32:i * 32 + 32], striu[0:L, 0:L], A2[0:L, i, :], start=(i == 0), stop=True)
                for i in range(TILES):
                    m_ = MM(ps[:, 1, 96:128], ones[0:LEN[i], :], A2[0:LEN[i], i, :], start=(i == 0), stop=(i == 2))
                m_.then_inc(S["rt_R"], 1)
                for table, O in enumerate((OBm, OBg)):
                    pe.wait_ge(S["rt_OH"], 2 * l + table + 1)
                    for k in range(6):
                        L = LEN[k // 2]
                        m_ = MM(ps[:, 2 + table, 0:COLS], OPm[0:L, k, :], O[0:L, k, :],
                                start=(k == 0), stop=(k == 5))
                    m_.then_inc(S["rt_tab"], 1)

                def turn(N, q):
                    for k in range(KD):
                        t_ = nc.tensor.transpose(bank(0, KD, SLOTS)[:, k, :], xg[q][0:SLOTS, k::KD],
                                                 ident[0:SLOTS, 0:SLOTS])
                    t_.then_inc(N["xg_T"], 1)

                def up(N, s, w, out, done):
                    n_ = D_EXP // HALVES
                    for k in range(KD):
                        for g in range(HALVES):
                            m_ = MM(ps[SLOTS * g:SLOTS * (g + 1), out, 0:n_], xT[:, k, :],
                                    w[s][:, k, n_ * g:n_ * (g + 1)], start=(k == 0), stop=(k == KD - 1))
                    m_.then_inc(done, 1)

                def turn_hidden(N):
                    for m in range(KE // HALVES):
                        t_ = nc.tensor.transpose(bank(4, KE // HALVES, P)[:, m, :], hid[:, m * P:(m + 1) * P], ident)
                    t_.then_inc(N["hT_ps"], 1)

                def down(N, s):
                    n_ = D_MODEL // HALVES
                    for k in range(KE):
                        src, m = k // (KE // HALVES), k % (KE // HALVES)
                        for g in range(HALVES):
                            m_ = MM(ps[SLOTS * g:SLOTS * (g + 1), 5, 0:n_], hidT[:, m, SLOTS * src:SLOTS * (src + 1)],
                                    wdb[s][:, k, n_ * g:n_ * (g + 1)], start=(k == 0), stop=(k == KE - 1))
                    m_.then_inc(N["y_ps"], 1)

                def place(N, n3, t, slots, b=6):
                    if b == 6:
                        need(pe, N["h_added"], n3 + (t + AHEAD if N is S else t))
                    L, n_ = LEN[t], D_MODEL // 2
                    for g in range(2):
                        m_ = MM(ps[0:L, b + g, 0:n_], weight[0:slots, AT[t]:AT[t] + L],
                                yb[0:slots, n_ * g:n_ * (g + 1)], start=True, stop=True)
                    m_.then_inc(N["placed_ps"], 1)

                def one(s, q, n, loaded, gathered, first=False):
                    ends = q == 0 and not first
                    pe.wait_ge(S[f"wg{s}"], loaded)
                    pe.wait_ge(S["xT_ready"], n() + (l + 1))
                    need(pe, S["sg_ready"], n())
                    up(S, s, wgb, 2, S["gate_ps"])
                    if ends:
                        pe.wait_ge(S["y_ready"], n())
                        pe.wait_ge(S["weight_ready"], n())
                        place(S, n(1.5) - 3, 0, P)
                    pe.wait_ge(S[f"wu{s}"], loaded)
                    need(pe, S["hid_ready"], n())
                    pe.wait_ge(S[f"xgathered{1 - q}"], gathered)
                    up(S, s, wub, 3, S["up_ps"])
                    if ends:
                        place(S, n(1.5) - 3, 1, P)
                    turn(S, 1 - q)
                    pe.wait_ge(S["hid_ready"], n() + 1)
                    need(pe, S["hidT_ready"], n())
                    turn_hidden(S)
                    if ends:
                        place(S, n(1.5) - 3, 2, P)
                    pe.wait_ge(S["hidT_ready"], n() + 1)
                    pe.wait_ge(S[f"wd{s}"], loaded)
                    need(pe, S["y_ready"], n())
                    down(S, s)

                even = 16 * l * (PAIRS + 1)
                odd = 16 * l * PAIRS
                pe.wait_ge(S["xgathered0"], even + 16)
                turn(S, 0)
                pe.wait_ge(S["route_done"], 2 * l + 2)
                for b in range(PEELED):
                    s, _, n = peeled(l, b)
                    one(s, b, n, 16 * (loads_before(l, s) + 1), even + 32 if b else odd + 16, first=(b == 0))
                with pe.Fori(0, ROUNDS) as i:
                    for j in range(ROUND):
                        s, _, n = looped(l, i, j)
                        one(s, j % 2, n, i * 32 + 16 * (loads_before(l, s) + (PEELED + j) // BUFFERS + 1),
                            i * (8 * ROUND) + 16 * ((PEELED + j + 1) // 2 + 1) + (even if j % 2 else odd))
                before = 3 * ((l + 1) * EXPERTS // 2 - 1)
                pe.wait_ge(S["y_ready"], (l + 1) * EXPERTS)
                pe.wait_ge(S["weight_ready"], (l + 1) * EXPERTS)
                for t in range(TILES):
                    place(S, before, t, P, LAST_BANKS[t])
                X = extra_signals[l]
                count = pe.value_load(extra_e[0:1, l, EXTRA:EXTRA + 1], min_val=0, max_val=EXTRA)
                for x in range(EXTRA):
                    with pe.If(count > x):
                        if x == 0:
                            pe.wait_ge(S["h_added"], before + 3 + AHEAD)
                            pe.wait_ge(S["xT_ready"], (l + 1) * (EXPERTS + 1))
                        pe.wait_ge(X["xgathered"], 16 * (x + 1))
                        turn(X, 0)
                        pe.wait_ge(X["wg"], 16 * (x + 1))
                        pe.wait_ge(X["xT_ready"], x + 1)
                        up(X, 0, wgb, 2, X["gate_ps"])
                        pe.wait_ge(X["wu"], 16 * (x + 1))
                        up(X, 0, wub, 3, X["up_ps"])
                        pe.wait_ge(X["hid_ready"], x + 1)
                        turn_hidden(X)
                        pe.wait_ge(X["hidT_ready"], x + 1)
                        pe.wait_ge(X["wd"], 16 * (x + 1))
                        down(X, 0)
                        pe.wait_ge(X["y_ready"], x + 1)
                        pe.wait_ge(X["weight_ready"], x + 1)
                        for t in range(TILES):
                            place(X, 3 * x, t, SLOTS)

            norm(1)
            moe_pe(0)
            norm(2)
            pe.wait_ge(S["uT_ready"], 18)

            def hg_step(i, n):
                L, c0 = LEN[i], AT[i]
                m = gdn_level(i, n) + i
                if n == 0 and i == 0:
                    pe.wait_ge(S["decay_in"], 2)
                    pe.wait_ge(S["proj_evac"], CONV_TILES + Z_TILES + 2 * HEADS)
                if m >= 2:
                    pe.wait_ge(S["hg_keep"], m - 1)
                if n:
                    pe.wait_ge(S["hg_qk"], gdn_level(i, n))
                for hd in range(8):
                    R = hR[(gdn_level(i, n) - 1) % 2][:, hd, 0:L]
                    a_, b_ = (R, R) if n else (hk[:, hd, c0:c0 + L], hq[:, hd, c0:c0 + L])
                    m_ = MM(bank(step_bank(m), 8, P, n=2)[0:L, hd, 0:L], a_, b_, start=True, stop=True)
                m_.then_inc(S["hg_att"], 1)

            def hg_turn(i):
                L, c0 = LEN[i], AT[i]
                pe.wait_ge(S["hg_in"], i + 1)
                for hd in range(8):
                    nc.tensor.transpose(bank(4, 8, P, n=2)[0:L, hd, :], hK[i][:, hd, 0:L], ident)
                    t_ = nc.tensor.transpose(bank(6, 8, P, n=2)[0:L, hd, :], hv[:, hd, c0:c0 + L], ident)
                t_.then_inc(S["hg_tr"], 1)

            def steps(t):
                for (i, n), at_tile in zip(HG_STEPS, STEP_AT):
                    if at_tile == t:
                        hg_step(i, n)

            project(4 * HEADS, CONV_TILES + Z_TILES, 1, steps)
            pe.wait_ge(S["proj_evac"], CONV_TILES + Z_TILES + 4 * HEADS)
            pe.wait_ge(S["hg_keep"], len(HG_STEPS))
            hg_turn(0)
            for i in range(TILES):
                L = LEN[i]
                st = hS[1 if i == 2 else 0]
                GB = bank(0, 8, P, n=2)
                kt, vt = tok_rows[i % 2]
                pe.wait_ge(S["hg_acc"], i + 1)
                if i + 1 < TILES:
                    hg_turn(i + 1)
                if i:
                    pe.wait_ge(S["hg_upd"], i)
                    pe.wait_ge(S["hg_out"], i)
                if i == 2:
                    pe.wait_ge(S["state_loaded"], 32)
                for hd in range(8):
                    out = bank(2, 8, P, n=2)[:, hd, 0:L]
                    MM(out, vt[0:L, hd, :], hA[i][0:L, hd, 0:L], start=True, stop=(i == 0))
                    if i:
                        MM(out, st[:, hd, :], hQ[i][:, hd, 0:L], start=False, stop=True)
                for hd in range(8):
                    m_ = MM(GB[:, hd, :], kt[0:L, hd, :], vt[0:L, hd, :], start=True, stop=True)
                m_.then_inc(S["hg_y"], 1)
            round_sums(1, 0)
            project_out(hcat, 2, 4, out_steps_1)
            norm(3)
            moe_pe(1)


def step_bank(m):
    return 4 + 2 * (m % 2)


def gdn_level(i, n):
    return sum(sum(b < LEN[j] for b in LEVELS) for j in range(i)) + n


def ring_use(projection, group):
    slot = group % 3
    before = len(range(slot, AB_GROUPS, 3)) if projection else 0
    return before + group // 3 + 1


def out_use(first, group):
    slot = group % 3
    before = len(range(slot, 4, 3)) if first else 0
    return before + group // 3 + 1


def constants():
    import numpy as np
    c = np.zeros((P, C_END), np.float32)
    i, j = np.arange(P)[:, None], np.arange(P)[None, :]
    c[:, C_ID:C_ID + P] = i == j
    c[:, C_ONES:C_ONES + P] = 1
    c[:, C_TRIU:C_TRIU + P] = i <= j
    c[:, C_STRIU:C_STRIU + P] = i < j
    for n, b in enumerate(LEVELS):
        c[:, C_MASK + n * P:C_MASK + (n + 1) * P] = (i // (2 * b) == j // (2 * b)) & (i % (2 * b) < b) & (j % (2 * b) >= b)
    c[:, C_IOTA:C_IOTA + P] = j
    for t in range(TILES):
        c[:, C_VAL + t] = AT[t] + np.arange(P) + 1
    c[:, C_SCAN:C_SCAN + TOK] = 1
    for t in range(TILES):
        c[:, C_SCAN + AT[t]] = 0
    c[:, C_EPS] = EPS
    c[:, C_EPSQ] = EPS * P
    c[:, C_SLOT:C_SLOT + P] = j % SLOTS
    return c


def lay_out(x):
    import numpy as np
    f = {n: np.asarray(a) for n, a in x.items()}
    w = f["w_in_ab"][0]
    zs, xbc, dt, qkv, zg, b, a = np.split(w, np.cumsum([1024, 1536, 16, 2048, 1024, 8])[:].tolist(), axis=1)
    main = np.concatenate([xbc, qkv, zs, zg], axis=1)
    tile = lambda m: np.ascontiguousarray(
        m.reshape(P, KD, -1, GROUP).transpose(2, 0, 1, 3)).reshape(-1, P, KD * GROUP)
    part = np.split(f["w_in_c"][0], 4, axis=1)
    chan = lambda m: m.reshape(-1, P).T
    conv_w = np.concatenate([f["ssd_conv_w"][0], f["gdn_conv_w"][0]], axis=1).reshape(CONV_W, CONV_TILES, P)
    conv_b = np.concatenate([f["ssd_conv_b"][0], np.zeros(QKV_TILES * P, np.float32)])
    vec = np.concatenate(
        [f[n][l].reshape(P, KD) for l in range(2) for n in ("norm_mix", "norm_ffn")]
        + [conv_w.transpose(2, 1, 0).reshape(P, -1), chan(conv_b), chan(np.repeat(f["ssd_d"][0], 64)),
           chan(f["ssd_norm"][0]), f["gdn_norm"][0][:, None], f["hgrn_norm"][0][:, None],
           f["hgrn_lb_logits"].reshape(2, HEADS, P).transpose(2, 0, 1).reshape(P, -1)], axis=1)
    st = np.concatenate([f["state_ssd_conv"][0, 0], f["state_gdn_conv"][0, 0]], axis=1)
    return {
        "con": constants(), "vec": np.ascontiguousarray(vec),
        "row": np.concatenate([f["ssd_dt_bias"][0], f["gdn_dt_bias"][0], f["ssd_a_log"][0], f["gdn_a_log"][0]])[None],
        "final": np.ascontiguousarray(f["norm_final"][None]),
        "wsm": np.ascontiguousarray(np.concatenate([dt, a, b], axis=1).reshape(P, KD, 32)),
        "wrt": np.ascontiguousarray(np.concatenate([f["moe_w_group"], f["moe_w_router"]], axis=2)
                                    .reshape(2, P, KD, 36).transpose(1, 0, 2, 3)),
        "wA": tile(main), "wC": tile(np.concatenate([part[1], part[0], part[2], part[3]], axis=1)),
        "w_out_ab": f["w_out_ab"][0], "w_out_c": f["w_out_c"][0],
        "wg": f["moe_w_gate"], "wu": f["moe_w_up"], "wd": f["moe_w_down"],
        "xp": f["x_prompt"][0], "xs": f["x_sample"][0],
        "conv_st": np.ascontiguousarray(st.reshape(TAPS, CONV_TILES, P).transpose(2, 1, 0)),
        "st_ssd": f["state_ssd"].reshape(SSD_HEADS * 64, 128), "st_gdn": f["state_gdn"][0, 0],
        "st_hgrn": f["state_hgrn"][0, 0],
    }


OUTS = {"y_p": (SEQ, D_MODEL), "y_s": (DEC_SEQ, D_MODEL), "conv": (2, P, CONV_TILES, TAPS),
        "ssd_p": (SSD_HEADS * 64, P), "ssd_s": (SSD_HEADS * 64, P), "gdn_p": (8, P, P), "gdn_s": (8, P, P),
        "hgrn_p": (8, P, P), "hgrn_s": (8, P, P)}


def kernel(**inputs):
    import concourse.bacc as _bacc
    from concourse import mybir as _mybir
    from concourse.bass_utils import run_bass_kernel_spmd as _run

    arrays = lay_out(inputs)
    nc = _bacc.Bacc("TRN2", target_bir_lowering=False, num_devices=1)
    ins = {n: nc.dram_tensor(f"in_{n}", a.shape, _mybir.dt.from_np(a.dtype), kind="ExternalInput").ap()
           for n, a in arrays.items()}
    outs = {n: nc.dram_tensor(f"out_{n}", s, _mybir.dt.float32, kind="ExternalOutput").ap() for n, s in OUTS.items()}
    build(nc, ins, outs)
    r = _run(nc, [{f"in_{n}": a for n, a in arrays.items()}], core_ids=[0]).results[0]
    out = {n: r[f"out_{n}"] for n in OUTS}
    conv = out["conv"].transpose(0, 3, 2, 1).reshape(2, 1, 1, TAPS, CONV_TILES * P)
    cut = XBC_TILES * P
    ssd = lambda a: a.reshape(1, 1, SSD_HEADS, 64, P)
    hd = lambda a: a.reshape(1, 1, 8, P, P)
    return (out["y_p"][None], out["y_s"][None],
            ssd(out["ssd_p"]), conv[0, ..., :cut], hd(out["gdn_p"]), conv[0, ..., cut:], hd(out["hgrn_p"]),
            ssd(out["ssd_s"]), conv[1, ..., :cut], hd(out["gdn_s"]), conv[1, ..., cut:], hd(out["hgrn_s"]))
```
